# Optimizing a Trainium2 kernel written in Bass

```python
import math
import jax, jax.numpy as jnp
from jax import lax
import numpy as np

D_MODEL = 1024
BATCH = 1
SEQ = 256
DEPTH = 2

A_WIDTH = D_MODEL // 2
A_HEAD_DIM = 128
A_HEADS = A_WIDTH // A_HEAD_DIM
A_CHUNK = 64
B_WIDTH = D_MODEL - A_WIDTH
B_HEAD_DIM = 64
B_HEADS = B_WIDTH // B_HEAD_DIM
B_CONFIGS = ((128, 1), (512, 4), (2048, 16))
EVEN_IN = 5 * A_WIDTH + 3 * B_WIDTH
C_HEADS = 8
C_HEAD_DIM = D_MODEL // C_HEADS // 2
C_Q_BLOCK = 128
ODD_IN = 3 * D_MODEL
D_FF = 2816
N_EXPERTS = 8
TOP_K = 2
ROPE_THETA = 10000.0
LN_EPS = 1e-5
RMS_EPS = 1e-5
MASK_VALUE = -1e30
MIN_FORGET = 1e-30
DEEPNORM_ALPHA = (2 * DEPTH) ** 0.25
DEEPNORM_BETA = (8 * DEPTH) ** -0.25
N_EVEN = (DEPTH + 1) // 2
N_ODD = DEPTH // 2
F32 = jnp.float32

kernel_name = 'hybrid_hgrn2_dilated_diffattn_moe_encoder'

def layer_norm(x, g, b):
    xf = x.astype(F32)
    mu = jnp.mean(xf, axis=-1, keepdims=True)
    var = jnp.mean(jnp.square(xf - mu), axis=-1, keepdims=True)
    return ((xf - mu) * lax.rsqrt(var + LN_EPS)).astype(x.dtype) * g + b

def rms_norm(x, w):
    xf = x.astype(F32)
    return (xf * lax.rsqrt(jnp.mean(xf * xf, axis=-1, keepdims=True) + RMS_EPS)).astype(x.dtype) * w

def rope_tables(seq, dim):
    inv = ROPE_THETA ** (-jnp.arange(0, dim, 2, dtype=F32) / dim)
    ang = jnp.arange(seq, dtype=F32)[:, None] * inv[None, :]
    return jnp.cos(ang), jnp.sin(ang)

def apply_rope(x, cos, sin):
    x1, x2 = jnp.split(x, 2, axis=-1)
    c = cos.astype(x.dtype)
    s = sin.astype(x.dtype)
    return jnp.concatenate([x1 * c - x2 * s, x2 * c + x1 * s], axis=-1)

def heads(t, n, hd):
    bsz, s, _ = t.shape
    return t.reshape(bsz, s, n, hd).transpose(0, 2, 1, 3)

def merge_heads(t):
    bsz, h, s, hd = t.shape
    return t.transpose(0, 2, 1, 3).reshape(bsz, s, h * hd)

def hgrn2_direction(q, k, v, log_f):
    bsz, h, s, dk = q.shape
    dv = v.shape[-1]
    n = s // A_CHUNK

    def chunks(t):
        return t.reshape(bsz, h, n, A_CHUNK, t.shape[-1]).transpose(2, 0, 1, 3, 4)

    seen = jnp.tril(jnp.ones((A_CHUNK, A_CHUNK), dtype=bool))[:, :, None]

    def step(state, inp):
        qc, kc, vc, gc = inp
        b = jnp.cumsum(gc, axis=2)
        pair = b[:, :, :, None, :] - b[:, :, None, :, :]
        decay = jnp.where(seen, jnp.exp(jnp.where(seen, pair, 0.0)), 0.0)
        scores = jnp.einsum('bhtsk,bhsk->bhts', decay * qc[:, :, :, None, :], kc)
        o = jnp.einsum('bhts,bhsv->bhtv', scores, vc) + jnp.einsum('bhtk,bhkv->bhtv', qc * jnp.exp(b), state)
        b_last = b[:, :, -1, :]
        new_state = jnp.exp(b_last)[..., None] * state + jnp.einsum(
            'bhsk,bhsv->bhkv', kc * jnp.exp(b_last[:, :, None, :] - b), vc)
        return new_state, o

    init = jnp.zeros((bsz, h, dk, dv), F32)
    _, outs = lax.scan(step, init, (chunks(q), chunks(k), chunks(v), chunks(log_f)))
    return outs.transpose(1, 2, 0, 3, 4).reshape(bsz, h, s, dv)

def dilated_band(q, k, v, dil, radius):
    bsz, h, s, hd = q.shape
    L = s // dil
    nb = -(-L // radius)
    lp = nb * radius

    def residues(t):
        return t.reshape(bsz, h, L, dil, hd).transpose(0, 1, 3, 2, 4)

    qr = jnp.pad(residues(q), ((0, 0), (0, 0), (0, 0), (0, lp - L), (0, 0)))
    qr = qr.reshape(bsz, h, dil, nb, radius, hd)

    def key_blocks(t):
        tp = jnp.pad(residues(t), ((0, 0), (0, 0), (0, 0), (radius, lp - L + radius), (0, 0)))
        tp = tp.reshape(bsz, h, dil, nb + 2, radius, hd)
        return jnp.concatenate([tp[:, :, :, 0:nb], tp[:, :, :, 1:nb + 1], tp[:, :, :, 2:nb + 2]], axis=4)

    kb = key_blocks(k)
    vb = key_blocks(v)
    scores = jnp.einsum('bhrnqd,bhrnkd->bhrnqk', qr, kb).astype(F32) * (hd ** -0.5)
    qi = jnp.arange(radius)[:, None]
    kj = jnp.arange(3 * radius)[None, :]
    key_l = jnp.arange(nb)[:, None, None] * radius + kj[None] - radius
    valid = (jnp.abs(kj - radius - qi) <= radius)[None] & (key_l >= 0) & (key_l < L)
    scores = jnp.where(valid, scores, MASK_VALUE)
    lse = jax.nn.logsumexp(scores, axis=-1)
    probs = jnp.where(valid, jnp.exp(scores - lse[..., None]), 0.0).astype(v.dtype)
    out = jnp.einsum('bhrnqk,bhrnkd->bhrnqd', probs, vb)
    out = out.reshape(bsz, h, dil, lp, hd)[:, :, :, :L].transpose(0, 1, 3, 2, 4).reshape(bsz, h, s, hd)
    lse = lse.reshape(bsz, h, dil, lp)[..., :L].transpose(0, 1, 3, 2).reshape(bsz, h, s)
    return out, lse

def dilated_attention(q, k, v):
    outs, lses = [], []
    for window, dil in B_CONFIGS:
        o, l = dilated_band(q, k, v, dil, window // (2 * dil))
        outs.append(o)
        lses.append(l)
    w = jax.nn.softmax(jnp.stack(lses, axis=0), axis=0)
    out = jnp.einsum('cbhs,cbhsd->bhsd', w, jnp.stack(outs, axis=0).astype(F32))
    return out.astype(q.dtype)

def even_mixer(x, w_in, lb, norm_w, w_out, cos, sin):
    proj = x @ w_in
    splits = np.cumsum([A_WIDTH] * 5 + [B_WIDTH] * 2).tolist()
    qa, fz_fw, fz_bw, va, ga, qb, kb, vb = jnp.split(proj, splits, axis=-1)
    lbh = lb.astype(F32).reshape(A_HEADS, 1, A_HEAD_DIM)

    def gates(z):
        zf = heads(z, A_HEADS, A_HEAD_DIM).astype(F32)
        f = lbh + (1.0 - lbh) * jax.nn.sigmoid(zf)
        log_f = jnp.log(jnp.maximum(f, MIN_FORGET))
        return log_f, (1.0 - lbh) * jax.nn.sigmoid(-zf)

    qa_h = heads(qa, A_HEADS, A_HEAD_DIM).astype(F32)
    va_h = heads(va, A_HEADS, A_HEAD_DIM).astype(F32)
    logf_fw, k_fw = gates(fz_fw)
    logf_bw, k_bw = gates(fz_bw)
    flip = lambda t: jnp.flip(t, axis=2)
    o_fw = hgrn2_direction(qa_h, k_fw, va_h, logf_fw)
    o_bw = flip(hgrn2_direction(flip(qa_h), flip(k_bw), flip(va_h), flip(logf_bw)))
    oa = rms_norm((o_fw + o_bw).astype(x.dtype), norm_w) * jax.nn.silu(heads(ga, A_HEADS, A_HEAD_DIM))
    qb_h = apply_rope(heads(qb, B_HEADS, B_HEAD_DIM), cos, sin)
    kb_h = apply_rope(heads(kb, B_HEADS, B_HEAD_DIM), cos, sin)
    vb_h = heads(vb, B_HEADS, B_HEAD_DIM)
    ob = dilated_attention(qb_h, kb_h, vb_h)
    return jnp.concatenate([merge_heads(oa), merge_heads(ob)], axis=-1) @ w_out

def diff_attention(q, k, v, lam, lambda_init, subln_w):
    bsz, h2, s, hd = q.shape
    h = h2 // 2
    nb = s // C_Q_BLOCK
    qblocks = q.reshape(bsz, h2, nb, C_Q_BLOCK, hd).transpose(2, 0, 1, 3, 4)

    def one_block(qblk):
        scores = jnp.einsum('bhqd,bhkd->bhqk', qblk, k).astype(F32) * (hd ** -0.5)
        p = jax.nn.softmax(scores, axis=-1).reshape(bsz, h, 2, C_Q_BLOCK, s)
        a = (p[:, :, 0] - lam * p[:, :, 1]).astype(v.dtype)
        return jnp.einsum('bhqk,bhkd->bhqd', a, v)

    out = lax.map(one_block, qblocks)
    out = out.transpose(1, 2, 0, 3, 4).reshape(bsz, h, s, v.shape[-1])
    return rms_norm(out, subln_w) * (1.0 - lambda_init)

def odd_mixer(x, w_in, lam_params, subln_w, w_out, cos, sin, lambda_init):
    q, k, v = jnp.split(x @ w_in, 3, axis=-1)
    q = apply_rope(heads(q, 2 * C_HEADS, C_HEAD_DIM), cos, sin)
    k = apply_rope(heads(k, 2 * C_HEADS, C_HEAD_DIM), cos, sin)
    v = heads(v, C_HEADS, 2 * C_HEAD_DIM)
    lp = lam_params.astype(F32)
    lam = jnp.exp(jnp.sum(lp[0] * lp[1])) - jnp.exp(jnp.sum(lp[2] * lp[3])) + lambda_init
    o = diff_attention(q, k, v, lam, lambda_init, subln_w)
    return merge_heads(o) @ w_out

def swiglu(x, w1, w3, w2):
    return (jax.nn.silu(x @ w1) * (x @ w3)) @ w2

def moe_swiglu(x, router, w1, w3, w2):
    bsz, s, d = x.shape
    xt = x.reshape(bsz * s, d)
    logits = (xt @ router).astype(F32)
    top_v, top_i = lax.top_k(logits, TOP_K)
    gates = jax.nn.softmax(top_v, axis=-1)
    dense_gate = jnp.sum(jax.nn.one_hot(top_i, N_EXPERTS, dtype=F32) * gates[..., None], axis=1)
    y = jnp.zeros_like(xt)
    for e in range(N_EXPERTS):
        h = jax.nn.silu(xt @ w1[e]) * (xt @ w3[e])
        y = y + dense_gate[:, e:e + 1].astype(x.dtype) * (h @ w2[e])
    return y.reshape(bsz, s, d)

def setup_inputs(seed: int = 0) -> dict:
    key = jax.random.key(seed)
    keys = iter(jax.random.split(key, 32))
    D = D_MODEL
    beta = DEEPNORM_BETA

    def normal(shape, scale):
        return jax.random.normal(next(keys), shape, F32) * scale

    def gain(shape):
        return 1.0 + normal(shape, 0.02)

    even_cols = jnp.concatenate([jnp.ones((3 * A_WIDTH,), F32), jnp.full((A_WIDTH,), beta, F32),
                                 jnp.ones((A_WIDTH + 2 * B_WIDTH,), F32), jnp.full((B_WIDTH,), beta, F32)])
    odd_cols = jnp.concatenate([jnp.ones((2 * D,), F32), jnp.full((D,), beta, F32)])
    return {
        'x': normal((BATCH, SEQ, D), 1.0),
        'ev_w_in': normal((N_EVEN, D, EVEN_IN), D ** -0.5) * even_cols,
        'ev_lb_logits': normal((N_EVEN, A_WIDTH), 0.5),
        'ev_hgrn_norm': gain((N_EVEN, A_HEAD_DIM)),
        'ev_w_out': normal((N_EVEN, D, D), beta * D ** -0.5),
        'ev_ln1_g': gain((N_EVEN, D)),
        'ev_ln1_b': normal((N_EVEN, D), 0.02),
        'ev_w1': normal((N_EVEN, D, D_FF), beta * D ** -0.5),
        'ev_w3': normal((N_EVEN, D, D_FF), beta * D ** -0.5),
        'ev_w2': normal((N_EVEN, D_FF, D), beta * D_FF ** -0.5),
        'ev_ln2_g': gain((N_EVEN, D)),
        'ev_ln2_b': normal((N_EVEN, D), 0.02),
        'od_w_in': normal((N_ODD, D, ODD_IN), D ** -0.5) * odd_cols,
        'od_lambda': normal((N_ODD, 4, C_HEAD_DIM), 0.1),
        'od_subln': gain((N_ODD, 2 * C_HEAD_DIM)),
        'od_w_out': normal((N_ODD, D, D), beta * D ** -0.5),
        'od_ln1_g': gain((N_ODD, D)),
        'od_ln1_b': normal((N_ODD, D), 0.02),
        'od_router': normal((N_ODD, D, N_EXPERTS), D ** -0.5),
        'od_w1': normal((N_ODD, N_EXPERTS, D, D_FF), beta * D ** -0.5),
        'od_w3': normal((N_ODD, N_EXPERTS, D, D_FF), beta * D ** -0.5),
        'od_w2': normal((N_ODD, N_EXPERTS, D_FF, D), beta * D_FF ** -0.5),
        'od_ln2_g': gain((N_ODD, D)),
        'od_ln2_b': normal((N_ODD, D), 0.02),
    }

def reference(x, ev_w_in, ev_lb_logits, ev_hgrn_norm, ev_w_out, ev_ln1_g, ev_ln1_b, ev_w1, ev_w3, ev_w2,
              ev_ln2_g, ev_ln2_b, od_w_in, od_lambda, od_subln, od_w_out, od_ln1_g, od_ln1_b, od_router,
              od_w1, od_w3, od_w2, od_ln2_g, od_ln2_b):
    s = x.shape[1]
    cos_b, sin_b = rope_tables(s, B_HEAD_DIM)
    cos_c, sin_c = rope_tables(s, C_HEAD_DIM)
    lb_soft = jax.nn.softmax(ev_lb_logits.astype(F32), axis=0)
    lower_bounds = jnp.cumsum(lb_soft, axis=0) - lb_soft[0]
    for layer in range(DEPTH):
        j = layer // 2
        if layer % 2 == 0:
            h = even_mixer(x, ev_w_in[j], lower_bounds[j], ev_hgrn_norm[j], ev_w_out[j], cos_b, sin_b)
            x = layer_norm(DEEPNORM_ALPHA * x + h, ev_ln1_g[j], ev_ln1_b[j])
            h = swiglu(x, ev_w1[j], ev_w3[j], ev_w2[j])
            x = layer_norm(DEEPNORM_ALPHA * x + h, ev_ln2_g[j], ev_ln2_b[j])
        else:
            lambda_init = 0.8 - 0.6 * math.exp(-0.3 * layer)
            h = odd_mixer(x, od_w_in[j], od_lambda[j], od_subln[j], od_w_out[j], cos_c, sin_c, lambda_init)
            x = layer_norm(DEEPNORM_ALPHA * x + h, od_ln1_g[j], od_ln1_b[j])
            h = moe_swiglu(x, od_router[j], od_w1[j], od_w3[j], od_w2[j])
            x = layer_norm(DEEPNORM_ALPHA * x + h, od_ln2_g[j], od_ln2_b[j])
    return x


_drawn_inputs = setup_inputs


def setup_inputs(seed=0):
    import zlib

    import numpy as np

    out = dict(_drawn_inputs(seed))
    spreads = {}
    factors = {'ev_hgrn_norm': 8.0,
     'ev_ln2_g': 2.701,
     'od_lambda': 8.0,
     'od_subln': 37.427,
     'od_ln1_g': 7.564,
     'od_ln1_b': 16.445,
     'od_ln2_g': 22.649,
     'od_ln2_b': 23.264,
     'ev_ln2_b': 2.831}
    for name, (base, spread) in spreads.items():
        noise = np.random.default_rng([zlib.crc32(name.encode()), seed]).standard_normal(out[name].shape)
        drawn = base * np.exp(spread * noise) if base else spread * noise
        out[name] = __import__('jax').numpy.asarray(drawn.astype(out[name].dtype))
    for name, factor in factors.items():
        out[name] = (out[name] * factor).astype(out[name].dtype)
    return out
```

```python
import math
from contextlib import ExitStack

import numpy as np
import concourse.bass as bass
from concourse import mybir

ALU = mybir.AluOpType
ACT = mybir.ActivationFunctionType
AX_X = mybir.AxisListType.X
F32 = mybir.dt.float32
F32R = mybir.dt.float32r
U8 = mybir.dt.uint8
I32 = mybir.dt.int32

P = 128
S, D = 256, 1024
NT = S // P
KD = D // P
AH, AD = 4, 128
BH, BD = 8, 64
CH, CD = 8, 64
FF = 2816
KF = FF // P
NE = 8
EVEN_IN, ODD_IN = 4096, 3072
QA, ZF, ZB, VA, GA, QB, KB, VB = (512 * i for i in range(8))
DEPTH = 2
ALPHA = (2 * DEPTH) ** 0.25
LAMBDA_INIT = 0.8 - 0.6 * math.exp(-0.3 * 1)
EPS = 1e-5
MIN_FORGET = 1e-30
LEVELS = (128, 64, 32, 16, 8, 4, 2, 1)
NL = len(LEVELS)

NB = 512
NU = 352
UB = FF // NU
TILE = 1536
GT = 4
RAW = 2 * GT
G_SQ = [(2, NB)] * GT
G_UP = [(4, NU)] * GT
G_DN = [[(3, NB)] * 4, [(3, NB), (3, NB), (2, NB), (2, NB)]]
DN_K0 = [[0, 3, 6, 9], [12, 15, 18, 20]]


def level_matrices():
    u, t = np.arange(P)[:, None], np.arange(P)[None, :]
    out = np.zeros((P, 2, NL + 1, P), np.float32)
    out[:, 0, 0], out[:, 1, 0] = u > t, u >= t
    out[:, 0, 1], out[:, 1, 1] = u <= t, u < t
    for i, m in enumerate(LEVELS[1:]):
        mid = t // (2 * m) * 2 * m + m
        right = t >= mid
        out[:, 0, 2 + i] = np.where(right, (u >= mid) & (u <= t), (u > t) & (u < mid))
        out[:, 1, 2 + i] = np.where(right, (u >= mid) & (u < t), (u >= t) & (u < mid))
    return out.reshape(P, -1)


def level_masks():
    s, t = np.arange(P)[:, None], np.arange(P)[None, :]
    ms = [(s // (2 * m) == t // (2 * m)) & (s // m != t // m) for m in LEVELS[2:]] + [s == t]
    return np.stack(ms, 1).astype(np.float32).reshape(P, -1)


def constants():
    pos = np.arange(S)
    diff = pos[:, None] - pos[None, :]
    times = (np.abs(diff) <= 64).astype(np.int32) + (diff % 4 == 0) + (diff % 16 == 0)
    bias = np.where(times > 0, np.log(np.maximum(times, 1).astype(np.float32)), -1e30).astype(np.float32)
    inv = np.float32(10000.0) ** (-np.arange(0, BD, 2, dtype=np.float32) / np.float32(BD))
    ang = pos.astype(np.float32)[:, None] * inv.astype(np.float32)[None, :]
    rope = np.concatenate([np.cos(ang), np.sin(ang)], 1).astype(np.float32)
    a = np.arange(P)
    e = np.arange(NE)
    small = np.zeros((P, 3, P), np.float32)
    small[:, 0] = np.eye(P)
    small[:, 1] = a[:, None] < a[None, :]
    small[:, 2] = a[None, :]
    before = np.broadcast_to((e[None, :] < e[:, None]).astype(np.float32).reshape(1, -1), (P, NE * NE))
    return {
        "levels": np.concatenate([level_matrices(), level_masks()], 1),
        "band": np.ascontiguousarray(bias.reshape(NT, P, S).transpose(1, 0, 2)).reshape(P, -1),
        "rope": np.ascontiguousarray(rope.reshape(NT, P, BD).transpose(1, 0, 2)).reshape(P, -1),
        "small": small.reshape(P, -1),
        "before": np.ascontiguousarray(before),
    }


def trunk(nc, a, c, out):
    with ExitStack() as ctx:
        sem = lambda name: ctx.enter_context(nc.semaphore(name))

        base = (nc.sbuf_base + 63) // 64 * 64
        top = nc.sbuf_usable_end
        cur = [base]

        def at(name, shape, dt=F32, offset=None):
            size = int(np.prod(shape[1:])) * (1 if dt == U8 else 4)
            here = cur[0] if offset is None else offset
            if offset is None:
                cur[0] = here + (size + 31) // 32 * 32
            assert here + size <= top, (name, here + size, top)
            return nc.alloc_sbuf_tensor_at(name, shape, dt, offset=here), here + (size + 31) // 32 * 32

        def own(name, shape, dt=F32):
            return at(name, shape, dt)[0]

        raw = [own(f"raw{i}", [P, TILE]) for i in range(RAW)]
        whi = [own(f"whi{i}", [P, TILE], F32R) for i in range(GT)]
        wlo = [own(f"wlo{i}", [P, TILE], F32R) for i in range(GT)]
        x = own("x", [P, NT, D])
        xT_hi = own("xT_hi", [P, KD, S], F32R)
        xT_lo = own("xT_lo", [P, KD, S], F32R)
        small = own("small", [P, 3, P])
        ident, earlier, slots = small[:, 0, :], small[:, 1, :], small[:, 2, :]
        rope = own("rope", [P, NT, 2, BD // 2])
        stat = own("stat", [P, NT, 2, 6])
        mv = own("mv", [P, NT, 2])
        ln_rs = own("ln_rs", [P, NT])
        neg_half = own("neg_half", [P, 8])
        vec = own("vec", [P, 96])
        phase = cur[0]

        gains, after_gains = at("gains", [P, 2, D], F32, phase)
        lev, after_lev = at("lev", [P, 2, NL + 1, P], F32R, phase)
        o = max(after_gains, after_lev)
        masks, o = at("masks", [P, NL - 1, P], U8, o)
        band, o = at("band", [P, NT, S], F32, o)
        lbs, o = at("lbs", [P, 2, 512], F32, o)
        proj, o = at("proj", [P, NT, EVEN_IN], F32, o)
        levraw = nc.alloc_sbuf_tensor_at("levraw", [P, (2 * (NL + 1) + NL - 1) * P], F32, offset=o - NT * EVEN_IN * 4)
        sA, oA = at("sA", [P, NT, 1024], F32, o)
        expE = [at(f"expE{i}", [P, 2, 2, S], F32, o + i * 4096)[0] for i in range(2)]
        sB, oB = at("sB", [P, NT, 1024], F32, oA)
        qk2 = [at(f"qk2_{i}", [P, 2, 2, S], F32, oA + i * 4096)[0] for i in range(2)]
        hT, oC = at("hgT", [P, 3, AH, S], F32, oB)
        ATo, oD = at("ATo", [P, AH, 2, P], F32, oC)
        ATd = proj[:, :, ZB:ZB + 512].rearrange("p t (h c) -> p t h c", h=AH)
        qkT, q1 = at("qkT", [P, 8, S], F32, oB)
        zP = [at(f"zP{i}", [P, NT, S], F32, q1 + 2048 * i)[0] for i in range(2)]
        pT = [at(f"pT{i}", [P, NT, S], F32, q1 + 4096 + 2048 * i)[0] for i in range(2)]
        ropeT, oE = at("ropeT", [P, 2, 512], F32, max(oD, q1 + 8192))
        hnorm, oF = at("hnorm", [P, AD], F32, oE)
        sga = at("sga", [P, NT, 512], F32, oC)[0]
        h_nat, f1 = at("h_nat", [P, NT, FF], F32, after_gains)
        hT_hi, f2 = at("hT_hi", [P, KF, S], F32R, f1)
        hT_lo, f3 = at("hT_lo", [P, KF, S], F32R, f2)
        silu, f4 = at("silu", [P, NT, NU], F32, f3)
        proj2, d1 = at("proj2", [P, NT, ODD_IN], F32, after_gains)
        qkT2, d2 = at("qkT2", [P, 16, S], F32, d1)
        eP = [at(f"eP{i}", [P, 2, NT, S], F32, d2 + 4096 * i)[0] for i in range(2)]
        aP = [at(f"aP{i}", [P, NT, S], F32, d2 + 8192 + 2048 * i)[0] for i in range(2)]
        aT = [at(f"aT{i}", [P, NT, S], F32, d2 + 12288 + 2048 * i)[0] for i in range(2)]
        rtD, d3 = at("rtD", [P, 2, 1024], F32, d2 + 16384)
        rtP, d4 = at("rtP", [P, 2, 1024], F32, d3)
        sub, d5 = at("sub", [P, 2 * CD], F32, d4)
        lamv, d6 = at("lamv", [P, 4, CD], F32, d5)
        sq2 = proj2[:, :, D:D + 512].rearrange("p t (h c) -> p t h c", h=4)
        on2 = proj2[:, :, D + 512:2 * D].rearrange("p t (h c) -> p t h c", h=4)

        xn, m2 = at("xn", [P, NT, D], F32, after_gains)
        xe_hi, m3 = at("xe_hi", [P, KD, P], F32R, m2)
        xe_lo, m4 = at("xe_lo", [P, KD, P], F32R, m3)
        h_e, m5 = at("h_e", [P, FF], F32, m4)
        hTe_hi, m6 = at("hTe_hi", [P, KF, P], F32R, m5)
        hTe_lo, m7 = at("hTe_lo", [P, KF, P], F32R, m6)
        silu_e, m8 = at("silu_e", [P, 2, NU], F32, m7)
        pick, m9 = at("pick", [P, NT, P], F32, m8)
        put_next, m10 = at("put_next", [P, S], F32R, m9)
        put, m11 = at("put", [P, S], F32R, m10)
        y_hi, m12 = at("y_hi", [P, D], F32R, m11)
        y_lo, m13 = at("y_lo", [P, D], F32R, m12)
        xT_f, m14 = at("xT_f", [P, KD, S], F32, m5)
        router, m15 = at("router", [P, KD, NE], F32, m13)
        route, m16 = at("route", [P, 12, NT, NE], F32, m15)
        cmp, m17 = at("cmp", [P, 2, NT, NE, NE], F32, m16)
        before, m18 = at("before", [P, NE, NE], F32, m17)
        ones, m19 = at("ones", [P, P], F32, m18)
        seat, m20 = at("seat", [P, NT, 2 * NE], F32, m19)
        gate_col, m21 = at("gate_col", [P, NT], F32, m20)
        slot_gate, m22 = at("slot_gate", [P, 2], F32, m21)
        more, m23 = at("more", [P, 1], I32, m22)

        psum = ctx.enter_context(nc.psum_tensor("psum", [P, 8, 512], F32))

        raw_full = [sem(f"raw_full{i}") for i in range(RAW)]
        hi_done, lo_done, tile_used = sem("hi_done"), sem("lo_done"), sem("tile_used")
        const_in, x_in, band_in, lb_in = sem("const_in"), sem("x_in"), sem("band_in"), sem("lb_in")
        lev_in, vec_in, gain_in, lam_in, rope_in = (sem(n) for n in ("lev_in", "vec_in", "gain_in", "lam_in", "rope_in"))
        act_link, dve_link, pool_link = sem("act_link"), sem("dve_link"), sem("pool_link")
        t_ps, t_hi, t_lo = sem("t_ps"), sem("t_hi"), sem("t_lo")
        in_act, in_dve = sem("in_act"), sem("in_dve")
        ln_mv, ln_rstd = sem("ln_mv"), sem("ln_rstd")
        ln_done, mix_done = sem("ln_done"), sem("mix_done")
        up_silu, up_h = sem("up_silu"), sem("up_h")
        ht_ps, ht_hi, ht_lo = sem("ht_ps"), sem("ht_hi"), sem("ht_lo")
        g_sig, g_k, g_f, g_ln, g_hi, g_lo, g_lev = (sem(n) for n in ("g_sig", "g_k", "g_f", "g_ln", "g_hi", "g_lo", "g_lev"))
        gate_c = sem("gate_c")
        lb_e, lb_d = sem("lb_e"), sem("lb_d")
        rope_done = sem("rope_done")
        bt_ps, bt_act, bt_dve = sem("bt_ps"), sem("bt_act"), sem("bt_dve")
        b_s, b_z, b_nm, b_p, b_tp, b_te, b_av, b_out = (sem(n) for n in ("b_s", "b_z", "b_nm", "b_p", "b_tp", "b_te", "b_av", "b_out"))
        ht2_ps, ht2_act, ht2_dve = sem("ht2_ps"), sem("ht2_act"), sem("ht2_dve")
        e_ps, e_exp, e_qk, s_ps, s_ev, o_ps = (sem(n) for n in ("e_ps", "e_exp", "e_qk", "s_ps", "s_ev", "o_ps"))
        r_sq, r_ms, r_rs, r_out = (sem(n) for n in ("r_sq", "r_ms", "r_rs", "r_out"))
        rope2_dve, rope2_pool = sem("rope2_dve"), sem("rope2_pool")
        lam_x, lam_d = sem("lam_x"), sem("lam_d")
        c_s, c_mx, c_e, c_a, c_tp, c_te, c_av = (sem(n) for n in ("c_s", "c_mx", "c_e", "c_a", "c_tp", "c_te", "c_av"))
        rt_in, bf_in, rx_act, rx_dve, m_lg, m_sel, m_ex, m_d, m_pos, more_set, xn_set = (
            sem(n) for n in ("rt_in", "bf_in", "rx_act", "rx_dve", "m_lg", "m_sel", "m_ex", "m_d", "m_pos", "more_set", "xn_set"))
        m_pick, m_ga, m_ga_hi, m_ga_lo, m_put_r, m_gt, m_cur = (
            sem(n) for n in ("m_pick", "m_ga", "m_ga_hi", "m_ga_lo", "m_put_r", "m_gt", "m_cur"))
        m_silu, m_h, m_tp, m_thi, m_tlo, m_yhi, m_ylo, m_sc, m_acc = (
            sem(n) for n in ("m_silu", "m_h", "m_tp", "m_thi", "m_tlo", "m_yhi", "m_ylo", "m_sc", "m_acc"))
        ones_set, sub_in, lm_in, lam_s = sem("ones_set"), sem("sub_in"), sem("lm_in"), sem("lam_s")
        out_ready, out_sent = sem("out_ready"), sem("out_sent")

        def rawv(par, j, kc, n):
            return raw[GT * par + j][:, 0:kc * n].rearrange("p (k n) -> p k n", n=n)

        def load_group(sp, q, par, shapes, srcs, first=False):
            for j, ((kc, n), src) in enumerate(zip(shapes, srcs)):
                if not first:
                    sp.wait_ge(lo_done, 2 * GT * q + GT * (par - 2) + j + 1)
                sp.dma_start(rawv(par, j, kc, n), src).then_inc(raw_full[GT * par + j], 16)

        def split_hi(act, q, par, shapes, first=False):
            for j, (kc, n) in enumerate(shapes):
                act.wait_ge(raw_full[GT * par + j], 16 * (q + 1))
                if not first:
                    act.wait_ge(tile_used, 2 * GT * q + GT * (par - 1) + j + 1)
                nc.scalar.copy(whi[j][:, 0:kc * n], raw[GT * par + j][:, 0:kc * n]).then_inc(hi_done, 1)

        def split_lo(dve, q, par, shapes):
            for j, (kc, n) in enumerate(shapes):
                dve.wait_ge(hi_done, 2 * GT * q + GT * par + j + 1)
                nc.vector.tensor_tensor(wlo[j][:, 0:kc * n], raw[GT * par + j][:, 0:kc * n],
                                        whi[j][:, 0:kc * n].bitcast(F32), ALU.subtract).then_inc(lo_done, 1)

        def group_used(q, par):
            return 2 * GT * q + GT * (par + 1)

        def tile_products(pe, q, par, j, kc, n, k0, lhs, outs, first_k, last_k):
            pe.wait_ge(lo_done, 2 * GT * q + GT * par + j + 1)
            hi, lo = lhs
            for kk in range(kc):
                k = k0 + kk
                w_h = whi[j][:, kk * n:(kk + 1) * n]
                w_l = wlo[j][:, kk * n:(kk + 1) * n]
                for ps, t0 in outs:
                    nc.tensor.matmul(ps, hi[:, k, t0:t0 + P], w_h, start=(k == first_k), stop=False)
                    nc.tensor.matmul(ps, hi[:, k, t0:t0 + P], w_l, start=False, stop=False)
                    last = nc.tensor.matmul(ps, lo[:, k, t0:t0 + P], w_h, start=False, stop=(k == last_k))
            last.then_inc(tile_used, 1)

        Q_IN, Q_OUT, Q_UP, Q_DN, Q_IN2, Q_OUT2, Q_MOE = 0, 4, 5, 9, 11, 14, 15
        w_in = a["ev_w_in"][0].rearrange("(k p) n -> p k n", p=P)
        w_out = a["ev_w_out"][0].rearrange("(k p) n -> p k n", p=P)
        w_1 = a["ev_w1"][0].rearrange("(k p) n -> p k n", p=P)
        w_3 = a["ev_w3"][0].rearrange("(k p) n -> p k n", p=P)
        w_2 = a["ev_w2"][0].rearrange("(k p) n -> p k n", p=P)
        w_in2 = a["od_w_in"][0].rearrange("(k p) n -> p k n", p=P)
        w_out2 = a["od_w_out"][0].rearrange("(k p) n -> p k n", p=P)

        def sq_src(w, b):
            return [w[:, 2 * j:2 * j + 2, bass.ds(b * NB, NB)] for j in range(GT)]

        def up_src(w1, w3, b):
            return [w[:, 4 * j:4 * j + 4, bass.ds(b * NU, NU)] for w in (w1, w3) for j in range(2)]

        def dn_src(w2, half, part):
            return [w2[:, k0:k0 + kc, half * NB:(half + 1) * NB] for k0, (kc, _) in zip(DN_K0[part], G_DN[part])]

        m_w1 = a["od_w1"][0].rearrange("e (k p) n -> p e k n", p=P)
        m_w3 = a["od_w3"][0].rearrange("e (k p) n -> p e k n", p=P)
        m_w2 = a["od_w2"][0].rearrange("e (k p) n -> p e k n", p=P)

        def up_src_e(e, b):
            return [w[:, bass.ds(e, 1), 4 * j:4 * j + 4, bass.ds(b * NU, NU)].rearrange("p e k n -> p (e k) n")
                    for w in (m_w1, m_w3) for j in range(2)]

        def dn_src_e(e, half, part):
            return [m_w2[:, bass.ds(e, 1), k0:k0 + kc, half * NB:(half + 1) * NB].rearrange("p e k n -> p (e k) n")
                    for k0, (kc, _) in zip(DN_K0[part], G_DN[part])]

        TURNS = [(0, 4, 6, 3), (4, 4, 7, 4), (8, 4, 6, 5), (12, 4, 7, 6), (16, 3, 6, 7), (19, 3, 3, None)]
        TURN_AFTER = {after: g for g, (_, _, _, after) in enumerate(TURNS) if after is not None}
        GATHER_AFTER = 2

        def q_moe(n):
            return Q_MOE + 6 * n

        def up_group(n, b):
            return q_moe(n) + b // 2, b % 2

        def up_shapes(b):
            return G_UP if b < UB else G_DN[0]

        block = ctx.enter_context(nc.Block())

        @block.sync
        def _(sp):
            sp.dma_start(x[:], a["x"][0].rearrange("(t p) d -> p t d", p=P)).then_inc(x_in, 16)
            sp.dma_start(small[:].rearrange("p a b -> p (a b)"), c["small"]).then_inc(const_in, 16)
            for par in range(2):
                load_group(sp, 0, par, G_SQ, sq_src(w_in, par), first=True)
            with sp.Fori(1, 4) as q:
                for par in range(2):
                    load_group(sp, Q_IN + q, par, G_SQ, sq_src(w_in, 2 * q + par))
            for par in range(2):
                load_group(sp, Q_OUT, par, G_SQ, sq_src(w_out, par))
            with sp.Fori(0, 4) as q:
                for par in range(2):
                    load_group(sp, Q_UP + q, par, G_UP, up_src(w_1, w_3, 2 * q + par))
            for half in range(2):
                for part in range(2):
                    load_group(sp, Q_DN + half, part, G_DN[part], dn_src(w_2, half, part))
            with sp.Fori(0, 3) as q:
                for par in range(2):
                    load_group(sp, Q_IN2 + q, par, G_SQ, sq_src(w_in2, 2 * q + par))
            for par in range(2):
                load_group(sp, Q_OUT2, par, G_SQ, sq_src(w_out2, par))

            def load_expert(n, e):
                with sp.Fori(0, 4) as q:
                    for par in range(2):
                        load_group(sp, q_moe(n) + q, par, G_UP, up_src_e(e, 2 * q + par))
                for half in range(2):
                    for part in range(2):
                        load_group(sp, q_moe(n) + 4 + half, part, G_DN[part], dn_src_e(e, half, part))

            with sp.Fori(0, NE) as n:
                load_expert(n, n)
            sp.wait_ge(more_set, 1)
            flag = sp.value_load(more[0:1, 0:1], min_val=0, max_val=1)
            with sp.If(flag):
                with sp.Fori(0, NE) as e:
                    load_expert(e + NE, e)
            sp.wait_ge(out_ready, 1)
            sp.dma_start(out[0].rearrange("(t p) d -> p t d", p=P), x[:]).then_inc(out_sent, 16)
            sp.wait_ge(out_sent, 16)

        @block.gpsimd
        def _(pool):
            n_link = [0]

            def link(ins):
                n_link[0] += 1
                ins.then_inc(pool_link, 1)
                pool.wait_ge(pool_link, n_link[0])

            def load_gains(i, g, b):
                if i:
                    pool.wait_ge(ln_done, i)
                pool.dma_start(gains[:, 0, :], a[g].partition_broadcast(P)).then_inc(gain_in, 16)
                pool.dma_start(gains[:, 1, :], a[b].partition_broadcast(P)).then_inc(gain_in, 16)

            def rsqrt(dst, src, scale):
                link(nc.gpsimd.tensor_scalar(dst, src, scale, EPS, ALU.mult, ALU.add))
                return nc.gpsimd.tensor_tensor(dst, dst, neg_half[:, 0:dst.shape[1]], ALU.pow)

            def ln_rsqrt(i):
                for t in range(NT):
                    pool.wait_ge(ln_mv, NT * i + t + 1)
                    rsqrt(ln_rs[:, t:t + 1], mv[:, t, 1:2], 1.0).then_inc(ln_rstd, 1)

            def rotate(src, t, tmp, done):
                n = src.shape[1] // 32
                both = src.rearrange("p (n c) -> p n c", c=32)
                half = src.rearrange("p (n h c) -> p n h c", h=2, c=32)
                A = tmp[:, 0, 0:n * 32].rearrange("p (n c) -> p n c", c=32)
                B = tmp[:, 1, 0:n * 32].rearrange("p (n c) -> p n c", c=32)
                Ah = tmp[:, 0, 0:n * 32].rearrange("p (n h c) -> p n h c", h=2, c=32)
                Bh = tmp[:, 1, 0:n * 32].rearrange("p (n h c) -> p n h c", h=2, c=32)
                cos = rope[:, t, 0:1, :].broadcast_to([P, n, 32])
                sin = rope[:, t, 1:2, :].broadcast_to([P, n, 32])
                nc.gpsimd.tensor_tensor(A, both, cos, ALU.mult)
                link(nc.gpsimd.tensor_tensor(B, both, sin, ALU.mult))
                nc.gpsimd.tensor_tensor(half[:, :, 0, :], Ah[:, :, 0, :], Bh[:, :, 1, :], ALU.subtract).then_inc(done, 1)
                nc.gpsimd.tensor_tensor(half[:, :, 1, :], Ah[:, :, 1, :], Bh[:, :, 0, :], ALU.add).then_inc(done, 1)

            pool.dma_start(rope[:].rearrange("p t h c -> p (t h c)"), c["rope"]).then_inc(rope_in, 16)
            pool.dma_start(lbs[:, 0, :], a["ev_lb_logits"][0].partition_broadcast(P)).then_inc(lb_in, 16)
            pool.dma_start(levraw[:], c["levels"]).then_inc(lev_in, 16)
            pool.dma_start(band[:].rearrange("p t s -> p (t s)"), c["band"]).then_inc(band_in, 16)
            pool.dma_start(hnorm[:], a["ev_hgrn_norm"][0].partition_broadcast(P)).then_inc(vec_in, 16)
            nc.gpsimd.memset(neg_half[:], -0.5)
            pool.wait_ge(rope_in, 16)
            pool.wait_ge(g_sig, 3)
            pool.wait_ge(vec_in, 16)
            for t in range(NT):
                link(nc.gpsimd.tensor_tensor(proj[:, t, GA:GA + 512], proj[:, t, GA:GA + 512],
                                             sga[:, t, :], ALU.mult))
                v = proj[:, t, GA:GA + 512].rearrange("p (h c) -> p h c", h=AH)
                nc.gpsimd.tensor_tensor(v, v, hnorm[:, None, :].broadcast_to([P, AH, AD]), ALU.mult).then_inc(gate_c, 1)
            for u, (t, col) in enumerate((t, col) for t in range(NT) for col in (QB, KB)):
                if u:
                    pool.wait_ge(rope_done, 2 * u)
                rotate(proj[:, t, col:col + 512], t, ropeT, rope_done)
            pool.wait_ge(r_ms, 1)
            rsqrt(vec[:, 40:48], vec[:, 32:40], 1.0 / AD).then_inc(r_rs, 1)
            load_gains(0, "ev_ln1_g", "ev_ln1_b")
            ln_rsqrt(0)
            load_gains(1, "ev_ln2_g", "ev_ln2_b")
            ln_rsqrt(1)

            pool.wait_ge(ln_done, 2)
            pool.dma_start(sub[:], a["od_subln"][0].partition_broadcast(P)).then_inc(sub_in, 16)
            pool.dma_start(lamv[:].rearrange("p a b -> p (a b)"),
                           a["od_lambda"][0].rearrange("a b -> (a b)").partition_broadcast(P)).then_inc(lm_in, 16)
            load_gains(2, "od_ln1_g", "od_ln1_b")
            pool.wait_ge(in_act, 14)
            pool.wait_ge(in_dve, 14)
            rotate(proj2[:, 1, D:2 * D], 1, rtP, rope2_pool)
            for r in (1, 2):
                pool.wait_ge(r_ms, r + 1)
                rsqrt(vec[:, 40:48], vec[:, 32:40], 1.0 / AD).then_inc(r_rs, 1)
            ln_rsqrt(2)
            pool.wait_ge(ln_done, 3)
            pool.dma_start(router[:], a["od_router"][0].rearrange("(k p) e -> p k e", p=P)).then_inc(rt_in, 16)
            pool.dma_start(before[:].rearrange("p a b -> p (a b)"), c["before"]).then_inc(bf_in, 16)
            nc.gpsimd.memset(ones[:], 1.0).then_inc(ones_set, 1)
            load_gains(3, "od_ln2_g", "od_ln2_b")
            ln_rsqrt(3)


        @block.scalar
        def _(act):
            def transposed_hi(i):
                for b in range(4):
                    act.wait_ge(t_ps, 4 * i + b + 1)
                    nc.scalar.copy(xT_hi[:, 2 * b:2 * b + 2, :].rearrange("p k s -> p (k s)"),
                                   psum[:, 4 + b, :]).then_inc(t_hi, 1)

            def square_out(r, sq, ready, value):
                act.wait_ge(ready, value)
                nc.scalar.activation(sq, psum[:, 6:8, :].rearrange("p t (h c) -> p t h c", h=4),
                                     ACT.Square).then_inc(r_sq, 1)

            transposed_hi(0)
            split_hi(act, Q_IN, 0, G_SQ, first=True)
            act.wait_ge(lb_d, 1)
            nc.scalar.activation(lbs[:, 0, :], lbs[:, 0, :], ACT.Exp).then_inc(lb_e, 1)
            act.wait_ge(g_lev, 2)

            def in_block(q, par, dst, col, after):
                after()
                act.wait_ge(tile_used, group_used(q, par))
                nc.scalar.copy(dst[:, 0, bass.ds(col, NB)], psum[:, 2 * par, :]).then_inc(in_act, 1)

            with act.Fori(0, 3) as q:
                in_block(Q_IN + q, 0, proj, q * 2 * NB, lambda: split_hi(act, Q_IN + q, 1, G_SQ))
                in_block(Q_IN + q, 1, proj, q * 2 * NB + NB, lambda: split_hi(act, Q_IN + q + 1, 0, G_SQ))
            in_block(Q_IN + 3, 0, proj, 6 * NB, lambda: split_hi(act, Q_IN + 3, 1, G_SQ))
            in_block(Q_IN + 3, 1, proj, 7 * NB, lambda: split_hi(act, Q_OUT, 0, G_SQ))

            act.wait_ge(in_dve, 8)
            act.wait_ge(in_act, 8)
            nc.scalar.activation(sB[:], proj[:, :, ZF:ZF + 1024], ACT.Sigmoid, scale=-1.0).then_inc(g_sig, 1)
            nc.scalar.activation(sA[:], proj[:, :, ZF:ZF + 1024], ACT.Sigmoid).then_inc(g_sig, 1)
            nc.scalar.activation(sga[:], proj[:, :, GA:GA + 512], ACT.Sigmoid).then_inc(g_sig, 1)
            for b in range(0, 6, 2):
                act.wait_ge(ht2_ps, b + 1)
                nc.scalar.copy(hT[:, b // 2, 0:2, :].rearrange("p h s -> p (h s)"), psum[:, b, :]).then_inc(ht2_act, 1)
            act.wait_ge(g_f, 1)
            nc.scalar.activation(sA[:], sA[:], ACT.Ln).then_inc(g_ln, 1)
            act.wait_ge(g_ln, 1)
            nc.scalar.copy(xT_hi[:].rearrange("p k s -> p (k s)"), sA[:].rearrange("p t c -> p (t c)")).then_inc(g_hi, 1)
            for n in range(2 * NL):
                act.wait_ge(e_ps, n + 1)
                if n == 0:
                    act.wait_ge(g_lo, 1)
                if n >= 2:
                    act.wait_ge(e_qk, n - 1)
                nc.scalar.activation(expE[n % 2][:].rearrange("p h d s -> p h (d s)"),
                                     psum[:, 2 * (n % 2):2 * (n % 2) + 2, :], ACT.Exp).then_inc(e_exp, 1)
            square_out(0, expE[0][:].rearrange("p a b (h c) -> p (a b) h c", h=2).rearrange(
                "p a h c -> p (a h c)").rearrange("p (t h c) -> p t h c", t=2, h=4), o_ps, 1)

            for b in (0, 2):
                act.wait_ge(bt_ps, b + 1)
                nc.scalar.copy(qkT[:, 2 * b:2 * b + 2, :].rearrange("p k s -> p (k s)"), psum[:, b, :]).then_inc(bt_act, 1)

            def move_probs(h):
                act.wait_ge(b_tp, h + 1)
                if h >= 2:
                    act.wait_ge(b_av, h - 1)
                nc.scalar.copy(pT[h % 2][:].rearrange("p s t -> p (s t)"), psum[:, 4 + h % 2, :]).then_inc(b_te, 1)

            for h in range(BH):
                act.wait_ge(b_nm, h + 1)
                for t in range(NT):
                    nc.scalar.activation(zP[h % 2][:, t, :], zP[h % 2][:, t, :], ACT.Exp,
                                         bias=vec[:, 16 + 2 * h + t:17 + 2 * h + t],
                                         accum_out=vec[:, 48 + 2 * h + t:49 + 2 * h + t]).then_inc(b_p, 1)
                if h:
                    move_probs(h - 1)
            move_probs(BH - 1)
            transposed_hi(1)
            split_hi(act, Q_OUT, 1, G_SQ)
            split_hi(act, Q_UP, 0, G_UP)

            transposed_hi(2)

            def up_blocks(q, first=False, last=False):
                for par in range(2):
                    if par == 0:
                        split_hi(act, Q_UP + q, 1, G_UP)
                    elif last:
                        split_hi(act, Q_DN, 0, G_DN[0])
                    else:
                        split_hi(act, Q_UP + q + 1, 0, G_UP)
                    act.wait_ge(tile_used, group_used(Q_UP + q, par))
                    if not (first and par == 0):
                        act.wait_ge(up_h, 2 * q + par)
                    nc.scalar.activation(silu[:], psum[:, 4 * par:4 * par + 2, 0:NU], ACT.Silu).then_inc(up_silu, 1)

            def hidden_hi(g):
                act.wait_ge(ht_ps, g + 1)
                nc.scalar.copy(hT_hi[:, 2 * g:2 * g + 2, :].rearrange("p k s -> p (k s)"), psum[:, g % 4, :]).then_inc(ht_hi, 1)

            up_blocks(0, first=True)
            with act.Fori(1, 3) as q:
                up_blocks(q)
            up_blocks(3, last=True)
            for g in range(6):
                hidden_hi(g)
            split_hi(act, Q_DN, 1, G_DN[1])
            for g in range(6, 11):
                hidden_hi(g)
            split_hi(act, Q_DN + 1, 0, G_DN[0])
            split_hi(act, Q_DN + 1, 1, G_DN[1])
            split_hi(act, Q_IN2, 0, G_SQ)

            transposed_hi(3)
            with act.Fori(0, 2) as q:
                in_block(Q_IN2 + q, 0, proj2, q * 2 * NB, lambda: split_hi(act, Q_IN2 + q, 1, G_SQ))
                in_block(Q_IN2 + q, 1, proj2, q * 2 * NB + NB, lambda: split_hi(act, Q_IN2 + q + 1, 0, G_SQ))
            in_block(Q_IN2 + 2, 0, proj2, 4 * NB, lambda: split_hi(act, Q_IN2 + 2, 1, G_SQ))
            in_block(Q_IN2 + 2, 1, proj2, 5 * NB, lambda: split_hi(act, Q_OUT2, 0, G_SQ))

            act.wait_ge(lam_s, 1)
            nc.scalar.activation(vec[:, 90:92], vec[:, 88:90], ACT.Exp).then_inc(lam_x, 1)
            for b in range(0, 8, 2):
                act.wait_ge(bt_ps, 4 + b + 1)
                nc.scalar.copy(qkT2[:, 2 * b:2 * b + 2, :].rearrange("p k s -> p (k s)"), psum[:, b, :]).then_inc(bt_act, 1)

            def map_exps(h):
                p = h % 2
                act.wait_ge(c_mx, h + 1)
                if h >= 2:
                    act.wait_ge(c_a, h - 1)
                for u in range(4):
                    nc.scalar.activation(eP[p][:, u // 2, u % 2, :], psum[:, 2 * p + u // 2, (u % 2) * S:(u % 2 + 1) * S],
                                         ACT.Exp, bias=vec[:, 16 + 4 * p + u:17 + 4 * p + u], scale=CD ** -0.5,
                                         accum_out=vec[:, 48 + 4 * p + u:49 + 4 * p + u]).then_inc(c_e, 1)

            def move_maps(h):
                act.wait_ge(c_tp, h + 1)
                if h >= 2:
                    act.wait_ge(c_av, h - 1)
                nc.scalar.copy(aT[h % 2][:].rearrange("p s t -> p (s t)"), psum[:, 4 + h % 2, :]).then_inc(c_te, 1)

            for h in range(CH + 1):
                if h < CH:
                    map_exps(h)
                if h:
                    move_maps(h - 1)
                if h == 5:
                    square_out(1, sq2, c_av, 4)
            square_out(2, sq2, c_av, 8)
            transposed_hi(4)
            split_hi(act, Q_OUT2, 1, G_SQ)
            split_hi(act, q_moe(0), 0, G_UP)

            for b in range(0, 4, 2):
                act.wait_ge(t_ps, 20 + b + 1)
                nc.scalar.copy(xT_f[:, 2 * b:2 * b + 2, :].rearrange("p k s -> p (k s)"), psum[:, 4 + b, :]).then_inc(rx_act, 1)
            nc.scalar.copy(xn[:], x[:]).then_inc(xn_set, 1)
            act.wait_ge(m_d, 1)
            nc.scalar.activation(route[:, 4], route[:, 3], ACT.Exp).then_inc(m_ex, 1)

            def gather_hi(n):
                for b in range(2):
                    act.wait_ge(m_ga, 2 * n + b + 1)
                    nc.scalar.copy(xe_hi[:, 4 * b:4 * b + 4, :].rearrange("p k s -> p (k s)"), psum[:, 4 + b, :]).then_inc(m_ga_hi, 1)

            def keep_map(n, first=False):
                act.wait_ge(m_gt, n + 1)
                if not first:
                    act.wait_ge(m_cur, n)
                nc.scalar.copy(put_next[:], psum[:, 6, 2 * P:4 * P]).then_inc(m_put_r, 1)
                nc.scalar.copy(slot_gate[:, 0:1], psum[:, 6, 0:1]).then_inc(m_put_r, 1)

            def turn_hi(n, g):
                k0, kc, bank, _ = TURNS[g]
                act.wait_ge(m_tp, 6 * n + g + 1)
                nc.scalar.copy(hTe_hi[:, k0:k0 + kc, :].rearrange("p k s -> p (k s)"), psum[:, bank, 0:kc * P]).then_inc(m_thi, 1)

            def block_e(n, b):
                split_hi(act, *up_group(n, b + 1), up_shapes(b + 1))
                act.wait_ge(tile_used, group_used(*up_group(n, b)))
                act.wait_ge(m_h, 8 * n + b + 1)
                nc.scalar.activation(silu_e[:, b % 2, :], psum[:, 2 * (b % 2), 0:NU], ACT.Silu).then_inc(m_silu, 1)

            def expert(n, last):
                q0 = q_moe(n)
                for b in range(1, UB):
                    block_e(n, b)
                    if b == GATHER_AFTER and not last:
                        keep_map(n + 1)
                    if b in TURN_AFTER:
                        turn_hi(n, TURN_AFTER[b])
                if not last:
                    gather_hi(n + 1)
                turn_hi(n, 5)
                split_hi(act, q0 + 4, 1, G_DN[1])
                split_hi(act, q0 + 5, 0, G_DN[0])
                for half in range(2):
                    if half:
                        split_hi(act, q0 + 5, 1, G_DN[1])
                        if not last:
                            split_hi(act, q0 + 6, 0, G_UP)
                    act.wait_ge(tile_used, group_used(q0 + 4 + half, 1))
                    act.wait_ge(m_cur, n + 1)
                    nc.scalar.activation(y_hi[:, half * NB:(half + 1) * NB], psum[:, 2 * half, :], ACT.Copy,
                                         scale=slot_gate[:, 1:2]).then_inc(m_yhi, 1)
                if not last:
                    block_e(n + 1, 0)

            gather_hi(0)
            keep_map(0, first=True)
            block_e(0, 0)
            with act.Fori(0, NE - 1) as n:
                expert(n, False)
            expert(NE - 1, True)
            act.wait_ge(more_set, 1)
            flag = act.value_load(more[0:1, 0:1], min_val=0, max_val=1)
            with act.If(flag):
                with act.Fori(NE, 2 * NE) as n:
                    split_hi(act, q_moe(n), 0, G_UP)
                    gather_hi(n)
                    keep_map(n)
                    block_e(n, 0)
                    expert(n, True)

        @block.vector
        def _(dve):
            n_link = [0]

            def link(ins):
                n_link[0] += 1
                ins.then_inc(dve_link, 1)
                dve.wait_ge(dve_link, n_link[0])

            def transposed_lo(i):
                for b in range(4):
                    dve.wait_ge(t_hi, 4 * i + b + 1)
                    dst = slice(2 * b, 2 * b + 2)
                    nc.vector.tensor_tensor(xT_lo[:, dst, :].rearrange("p k s -> p (k s)"), psum[:, 4 + b, :],
                                            xT_hi[:, dst, :].rearrange("p k s -> p (k s)").bitcast(F32),
                                            ALU.subtract).then_inc(t_lo, 1)

            def residual(bank, half):
                for t in range(NT):
                    v = x[:, t, half * NB:(half + 1) * NB]
                    link(nc.vector.scalar_tensor_tensor(v, v, ALPHA, psum[:, bank + t, :], ALU.mult, ALU.add))
                    link(nc.vector.bn_stats(stat[:, t, half, :], v))

            def layer_norm(i):
                for t in range(NT):
                    nc.vector.bn_aggr(mv[:, t, :], stat[:, t, :, :].rearrange("p a b -> p (a b)")).then_inc(ln_mv, 1)
                dve.wait_ge(gain_in, 32 * (i + 1))
                for t in range(NT):
                    v = x[:, t, :]
                    dve.wait_ge(ln_rstd, NT * i + t + 1)
                    link(nc.vector.tensor_scalar(v, v, mv[:, t, 0:1], ln_rs[:, t:t + 1], ALU.subtract, ALU.mult))
                    link(nc.vector.tensor_tensor(v, v, gains[:, 0, :], ALU.mult))
                    ins = nc.vector.tensor_tensor(v, v, gains[:, 1, :], ALU.add)
                    if t < NT - 1:
                        link(ins)
                ins.then_inc(ln_done, 1)

            def rms_out(r, sq, on, gain, dst):
                dve.wait_ge(r_sq, r + 1)
                nc.vector.tensor_reduce(vec[:, 32:40].rearrange("p (t h) -> p t h", h=4), sq, AX_X, ALU.add).then_inc(r_ms, 1)
                dve.wait_ge(r_rs, r + 1)
                o_v = psum[:, 6:8, :].rearrange("p t (h c) -> p t h c", h=4)
                rs = vec[:, 40:48].rearrange("p (t h) -> p t h", h=4)[:, :, :, None].broadcast_to([P, NT, 4, 128])
                link(nc.vector.tensor_tensor(on, o_v, rs, ALU.mult))
                return nc.vector.tensor_tensor(dst.rearrange("p t (h c) -> p t h c", h=4), on, gain, ALU.mult)

            dve.wait_ge(lev_in, 16)
            nc.vector.tensor_copy(lev[:].rearrange("p a b c -> p (a b c)"), levraw[:, 0:2 * (NL + 1) * P]).then_inc(g_lev, 1)
            nc.vector.tensor_copy(masks[:].rearrange("p l t -> p (l t)"), levraw[:, 2 * (NL + 1) * P:]).then_inc(g_lev, 1)
            transposed_lo(0)
            split_lo(dve, Q_IN, 0, G_SQ)
            dve.wait_ge(lb_in, 16)
            nc.vector.tensor_tensor(lbs[:, 0, :], lbs[:, 0, :], lbs[:, 0, :], ALU.subtract).then_inc(lb_d, 1)
            dve.wait_ge(lb_e, 1)
            link(nc.vector.reciprocal(lbs[:, 1, :], lbs[:, 0, :]))
            link(nc.vector.tensor_tensor(lbs[:, 1, :], lbs[:, 1, :], lbs[:, 0, :], ALU.mult))
            link(nc.vector.tensor_tensor(lbs[:, 0, :], lbs[:, 1, :], lbs[:, 1, :], ALU.subtract))
            link(nc.vector.tensor_scalar(lbs[:, 1, :], lbs[:, 0, :], -1.0, 1.0, ALU.mult, ALU.add))

            def in_block(q, par, dst, col):
                dve.wait_ge(tile_used, group_used(q, par))
                nc.vector.tensor_copy(dst[:, 1, bass.ds(col, NB)], psum[:, 2 * par + 1, :]).then_inc(in_dve, 1)

            with dve.Fori(0, 3) as q:
                split_lo(dve, Q_IN + q, 1, G_SQ)
                in_block(Q_IN + q, 0, proj, q * 2 * NB)
                split_lo(dve, Q_IN + q + 1, 0, G_SQ)
                in_block(Q_IN + q, 1, proj, q * 2 * NB + NB)
            split_lo(dve, Q_IN + 3, 1, G_SQ)
            in_block(Q_IN + 3, 0, proj, 6 * NB)
            split_lo(dve, Q_OUT, 0, G_SQ)
            in_block(Q_IN + 3, 1, proj, 7 * NB)

            sBv = sB[:].rearrange("p t (d c) -> p (t d) c", d=2)
            sAv = sA[:].rearrange("p t (d c) -> p (t d) c", d=2)
            lb = lbs[:, 0:1, :].broadcast_to([P, 4, 512])
            one_lb = lbs[:, 1:2, :].broadcast_to([P, 4, 512])
            dve.wait_ge(g_sig, 1)
            nc.vector.tensor_tensor(sBv, sBv, one_lb, ALU.mult).then_inc(g_k, 1)
            dve.wait_ge(g_sig, 2)
            link(nc.vector.tensor_tensor(sAv, sAv, one_lb, ALU.mult))
            link(nc.vector.tensor_tensor(sAv, sAv, lb, ALU.add))
            nc.vector.tensor_scalar(sAv, sAv, MIN_FORGET, None, ALU.max).then_inc(g_f, 1)
            for b in range(1, 6, 2):
                dve.wait_ge(ht2_ps, b + 1)
                nc.vector.tensor_copy(hT[:, b // 2, 2:4, :].rearrange("p h s -> p (h s)"), psum[:, b, :]).then_inc(ht2_dve, 1)
            dve.wait_ge(g_hi, 1)
            nc.vector.tensor_tensor(xT_lo[:].rearrange("p k s -> p (k s)"), sA[:].rearrange("p t c -> p (t c)"),
                                    xT_hi[:].rearrange("p k s -> p (k s)").bitcast(F32), ALU.subtract).then_inc(g_lo, 1)

            def scale_pair(n):
                m, pair = LEVELS[n // 2], n % 2
                dve.wait_ge(e_exp, n + 1)
                if n >= 2:
                    dve.wait_ge(s_ps, n - 1)
                if n == 0:
                    dve.wait_ge(ht2_act, 3)
                    dve.wait_ge(ht2_dve, 3)
                cut = lambda v: v.rearrange("p h (b f m) -> p h b f m", f=2, m=m)
                q_, kf, kb = (cut(hT[:, i, 2 * pair:2 * pair + 2, :]) for i in range(3))
                Ef, Eb = (cut(expE[n % 2][:, :, d, :]) for d in range(2))
                Qn, Kn = (cut(qk2[n % 2][:, i, :, :]) for i in range(2))
                for out_, in_, e, f in ((Qn, q_, Ef, 1), (Qn, q_, Eb, 0), (Kn, kf, Ef, 0), (Kn, kb, Eb, 1)):
                    ins = nc.vector.tensor_tensor(out_[:, :, :, f, :], in_[:, :, :, f, :], e[:, :, :, f, :], ALU.mult)
                ins.then_inc(e_qk, 1)

            def keep_scores(n):
                li, pair = n // 2, n % 2
                dve.wait_ge(s_ps, n + 1)
                src = psum[:, 4 + n % 2, :].rearrange("p (h i c) -> p h i c", h=2, i=2)
                dst = (ATo[:, 2 * pair:2 * pair + 2, :, :] if li == 0 else
                       ATd[:, :, 2 * pair:2 * pair + 2, :].rearrange("p t h c -> p h t c"))
                if li < 2:
                    ins = nc.vector.tensor_copy(dst, src)
                else:
                    dve.wait_ge(s_ev, n - 1)
                    for h in range(2):
                        ins = nc.vector.copy_predicated(dst[:, h, :, :], masks[:, li - 2:li - 1, :].broadcast_to([P, 2, P]), src[:, h, :, :])
                ins.then_inc(s_ev, 1)

            dve.wait_ge(vec_in, 16)
            dve.wait_ge(gate_c, 2)
            for n in range(2 * NL):
                scale_pair(n)
                if n:
                    keep_scores(n - 1)
            for n in range(2 * NL - 1, 2 * NL + 2):
                keep_scores(n)
            sq0 = expE[0][:].rearrange("p a b c -> p (a b c)").rearrange("p (t h c) -> p t h c", t=2, h=4)
            on0 = qk2[0][:].rearrange("p a b c -> p (a b c)").rearrange("p (t h c) -> p t h c", t=2, h=4)
            rms_out(0, sq0, on0, proj[:, :, GA:GA + 512].rearrange("p t (h c) -> p t h c", h=4),
                    proj[:, :, 0:512]).then_inc(mix_done, 1)

            for b in (1, 3):
                dve.wait_ge(bt_ps, b + 1)
                nc.vector.tensor_copy(qkT[:, 2 * b:2 * b + 2, :].rearrange("p k s -> p (k s)"), psum[:, b, :]).then_inc(bt_dve, 1)
            dve.wait_ge(band_in, 16)
            for h in range(BH):
                dve.wait_ge(b_s, h + 1)
                if h >= 2:
                    dve.wait_ge(b_tp, h - 1)
                link(nc.vector.scalar_tensor_tensor(zP[h % 2][:].rearrange("p t s -> p (t s)"), psum[:, h % 4, :],
                                                    BD ** -0.5, band[:].rearrange("p t s -> p (t s)"), ALU.mult, ALU.add))
                link(nc.vector.tensor_reduce(vec[:, 2 * h:2 * h + 2], zP[h % 2][:], AX_X, ALU.max))
                nc.vector.tensor_scalar(vec[:, 16 + 2 * h:18 + 2 * h], vec[:, 2 * h:2 * h + 2], -1.0, None,
                                        ALU.mult).then_inc(b_nm, 1)
            dve.wait_ge(b_p, 2 * BH)
            link(nc.vector.reciprocal(vec[:, 64:80], vec[:, 48:64]))
            dve.wait_ge(b_av, BH)
            rinv = vec[:, 64:80].rearrange("p (h t) -> p t h", t=NT)
            for t in range(NT):
                ins = nc.vector.tensor_tensor(proj[:, t, 512:1024].rearrange("p (h c) -> p h c", h=BH),
                                              psum[:, 6 + t, :].rearrange("p (h c) -> p h c", h=BH),
                                              rinv[:, t, :, None].broadcast_to([P, BH, BD]), ALU.mult)
                ins.then_inc(mix_done, 1)
            transposed_lo(1)

            def out_projection(q, nxt):
                split_lo(dve, q, 1, G_SQ)
                dve.wait_ge(tile_used, group_used(q, 0))
                residual(0, 0)
                nxt()
                dve.wait_ge(tile_used, group_used(q, 1))
                residual(2, 1)

            out_projection(Q_OUT, lambda: split_lo(dve, Q_UP, 0, G_UP))
            layer_norm(0)
            transposed_lo(2)

            def up_blocks(q, last=False):
                for par in range(2):
                    if par == 0:
                        split_lo(dve, Q_UP + q, 1, G_UP)
                    elif last:
                        split_lo(dve, Q_DN, 0, G_DN[0])
                    else:
                        split_lo(dve, Q_UP + q + 1, 0, G_UP)
                    b = 2 * q + par
                    dve.wait_ge(up_silu, b + 1)
                    nc.vector.tensor_tensor(h_nat[:, :, bass.ds(b * NU, NU)], silu[:],
                                            psum[:, 4 * par + 2:4 * par + 4, 0:NU], ALU.mult).then_inc(up_h, 1)

            def hidden_lo(g):
                dve.wait_ge(ht_hi, g + 1)
                dst = slice(2 * g, 2 * g + 2)
                nc.vector.tensor_tensor(hT_lo[:, dst, :].rearrange("p k s -> p (k s)"), psum[:, g % 4, :],
                                        hT_hi[:, dst, :].rearrange("p k s -> p (k s)").bitcast(F32),
                                        ALU.subtract).then_inc(ht_lo, 1)

            with dve.Fori(0, 3) as q:
                up_blocks(q)
            up_blocks(3, last=True)
            for g in range(6):
                hidden_lo(g)
            split_lo(dve, Q_DN, 1, G_DN[1])
            for g in range(6, 11):
                hidden_lo(g)
            split_lo(dve, Q_DN + 1, 0, G_DN[0])
            dve.wait_ge(tile_used, group_used(Q_DN, 1))
            residual(4, 0)
            split_lo(dve, Q_DN + 1, 1, G_DN[1])
            split_lo(dve, Q_IN2, 0, G_SQ)
            dve.wait_ge(tile_used, group_used(Q_DN + 1, 1))
            residual(6, 1)
            layer_norm(1)
            transposed_lo(3)
            with dve.Fori(0, 2) as q:
                split_lo(dve, Q_IN2 + q, 1, G_SQ)
                in_block(Q_IN2 + q, 0, proj2, q * 2 * NB)
                split_lo(dve, Q_IN2 + q + 1, 0, G_SQ)
                in_block(Q_IN2 + q, 1, proj2, q * 2 * NB + NB)
            dve.wait_ge(lm_in, 16)
            lam4 = lamv[:].rearrange("p (a b) c -> p a b c", b=2)
            link(nc.vector.tensor_tensor(lam4[:, :, 0, :], lam4[:, :, 0, :], lam4[:, :, 1, :], ALU.mult))
            nc.vector.tensor_reduce(vec[:, 88:90], lam4[:, :, 0, :], AX_X, ALU.add).then_inc(lam_s, 1)
            dve.wait_ge(sub_in, 16)
            link(nc.vector.tensor_scalar(sub[:], sub[:], 1.0 - LAMBDA_INIT, None, ALU.mult))
            split_lo(dve, Q_IN2 + 2, 1, G_SQ)
            in_block(Q_IN2 + 2, 0, proj2, 4 * NB)
            split_lo(dve, Q_OUT2, 0, G_SQ)
            in_block(Q_IN2 + 2, 1, proj2, 5 * NB)
            dve.wait_ge(lam_x, 1)
            link(nc.vector.tensor_tensor(vec[:, 92:93], vec[:, 91:92], vec[:, 90:91], ALU.subtract))
            link(nc.vector.tensor_scalar(vec[:, 92:93], vec[:, 92:93], -LAMBDA_INIT, None, ALU.add))

            def rotate(src, t, tmp, done):
                n = src.shape[1] // 32
                both = src.rearrange("p (n c) -> p n c", c=32)
                half = src.rearrange("p (n h c) -> p n h c", h=2, c=32)
                A, B = (tmp[:, i, 0:n * 32].rearrange("p (n c) -> p n c", c=32) for i in range(2))
                Ah, Bh = (tmp[:, i, 0:n * 32].rearrange("p (n h c) -> p n h c", h=2, c=32) for i in range(2))
                nc.vector.tensor_tensor(A, both, rope[:, t, 0:1, :].broadcast_to([P, n, 32]), ALU.mult)
                link(nc.vector.tensor_tensor(B, both, rope[:, t, 1:2, :].broadcast_to([P, n, 32]), ALU.mult))
                nc.vector.tensor_tensor(half[:, :, 0, :], Ah[:, :, 0, :], Bh[:, :, 1, :], ALU.subtract).then_inc(done, 1)
                nc.vector.tensor_tensor(half[:, :, 1, :], Ah[:, :, 1, :], Bh[:, :, 0, :], ALU.add).then_inc(done, 1)

            dve.wait_ge(in_act, 14)
            dve.wait_ge(in_dve, 14)
            dve.wait_ge(rope_in, 16)
            for u, (t, col) in enumerate(((0, 0), (0, D), (1, 0))):
                if u:
                    dve.wait_ge(rope2_dve, 2 * u)
                rotate(proj2[:, t, col:col + D], t, rtD, rope2_dve)
            for b in range(1, 8, 2):
                dve.wait_ge(bt_ps, 4 + b + 1)
                nc.vector.tensor_copy(qkT2[:, 2 * b:2 * b + 2, :].rearrange("p k s -> p (k s)"), psum[:, b, :]).then_inc(bt_dve, 1)

            def map_max(h):
                p = h % 2
                dve.wait_ge(c_s, h + 1)
                link(nc.vector.tensor_reduce(vec[:, 4 * p:4 * p + 4],
                                             psum[:, 2 * p:2 * p + 2, :].rearrange("p m (t s) -> p (m t) s", t=2), AX_X, ALU.max))
                nc.vector.tensor_scalar(vec[:, 16 + 4 * p:20 + 4 * p], vec[:, 4 * p:4 * p + 4], -(CD ** -0.5), None,
                                        ALU.mult).then_inc(c_mx, 1)

            def combine(h):
                p = h % 2
                dve.wait_ge(c_e, 4 * h + 4)
                if h >= 2:
                    dve.wait_ge(c_tp, h - 1)
                link(nc.vector.reciprocal(vec[:, 64 + 4 * p:68 + 4 * p], vec[:, 48 + 4 * p:52 + 4 * p]))
                link(nc.vector.tensor_scalar(vec[:, 80 + 2 * p:82 + 2 * p], vec[:, 66 + 4 * p:68 + 4 * p], vec[:, 92:93], None, ALU.mult))
                for t in range(NT):
                    link(nc.vector.tensor_scalar(eP[p][:, 1, t, :], eP[p][:, 1, t, :], vec[:, 80 + 2 * p + t:81 + 2 * p + t], None, ALU.mult))
                    ins = nc.vector.scalar_tensor_tensor(aP[p][:, t, :], eP[p][:, 0, t, :], vec[:, 64 + 4 * p + t:65 + 4 * p + t],
                                                         eP[p][:, 1, t, :], ALU.mult, ALU.add)
                ins.then_inc(c_a, 1)

            def maps_out(r):
                g = r - 1
                rms_out(r, sq2, on2, sub[:, None, None, :].broadcast_to([P, NT, 4, 128]),
                        proj2[:, :, g * 512:(g + 1) * 512]).then_inc(mix_done, 1)

            for h in range(CH + 1):
                if h < CH:
                    map_max(h)
                if h:
                    combine(h - 1)
                if h == 5:
                    maps_out(1)
            maps_out(2)
            transposed_lo(4)
            out_projection(Q_OUT2, lambda: split_lo(dve, q_moe(0), 0, G_UP))
            layer_norm(2)
            dve.wait_ge(ln_done, 3)

            LG, GTR, TOP, DIF, EXS, SEL, GATE, POS = range(8)
            for b in range(1, 4, 2):
                dve.wait_ge(t_ps, 20 + b + 1)
                nc.vector.tensor_copy(xT_f[:, 2 * b:2 * b + 2, :].rearrange("p k s -> p (k s)"), psum[:, 4 + b, :]).then_inc(rx_dve, 1)
            dve.wait_ge(m_lg, 1)
            link(nc.vector.tensor_copy(route[:, LG], psum[:, 0, 0:NT * NE].rearrange("p (t e) -> p t e", e=NE)))
            dve.wait_ge(bf_in, 16)
            for t in range(NT):
                other = route[:, LG, t, None, :].broadcast_to([P, NE, NE])
                mine = route[:, LG, t, :, None].broadcast_to([P, NE, NE])
                nc.vector.tensor_tensor(cmp[:, 0, t], other, mine, ALU.is_gt)
                link(nc.vector.tensor_tensor(cmp[:, 1, t], other, mine, ALU.is_equal))
                link(nc.vector.tensor_tensor(cmp[:, 1, t], cmp[:, 1, t], before[:], ALU.mult))
                link(nc.vector.tensor_tensor(cmp[:, 0, t], cmp[:, 0, t], cmp[:, 1, t], ALU.add))
            flat = lambda i: route[:, i].rearrange("p t e -> p (t e)")
            link(nc.vector.tensor_reduce(flat(GTR), cmp[:, 0].rearrange("p t a b -> p (t a) b"), AX_X, ALU.add))
            nc.vector.tensor_scalar(flat(SEL), flat(GTR), 2.0, None, ALU.is_lt).then_inc(m_sel, 1)
            link(nc.vector.tensor_reduce(route[:, TOP, :, 0], route[:, LG], AX_X, ALU.max))
            nc.vector.tensor_tensor(route[:, DIF], route[:, LG], route[:, TOP, :, 0:1].broadcast_to([P, NT, NE]),
                                    ALU.subtract).then_inc(m_d, 1)
            dve.wait_ge(m_ex, 1)
            dve.wait_ge(m_sel, 1)
            link(nc.vector.tensor_tensor(route[:, EXS], route[:, EXS], route[:, SEL], ALU.mult))
            link(nc.vector.tensor_reduce(route[:, TOP, :, 1], route[:, EXS], AX_X, ALU.add))
            link(nc.vector.reciprocal(route[:, TOP, :, 2], route[:, TOP, :, 1]))
            link(nc.vector.tensor_tensor(route[:, GATE], route[:, EXS], route[:, TOP, :, 2:3].broadcast_to([P, NT, NE]), ALU.mult))
            dve.wait_ge(m_pos, 1)
            link(nc.vector.tensor_scalar(flat(POS), psum[:, 1, 0:NT * NE], 1.0, None, ALU.add))
            link(nc.vector.tensor_tensor(flat(POS), flat(POS), flat(SEL), ALU.mult))
            for r in range(2):
                link(nc.vector.tensor_scalar(seat[:, :, r * NE:(r + 1) * NE], route[:, POS], -1.0 - r * P, None, ALU.add))
            link(nc.vector.tensor_reduce(route[:, TOP, 0, 3:4], psum[:, 2, 0:NE], AX_X, ALU.max))
            nc.vector.tensor_scalar(more[:], route[:, TOP, 0, 3:4], float(P), None, ALU.is_gt).then_inc(more_set, 1)

            def pick_tokens(n, e):
                for t in range(NT):
                    nc.vector.tensor_scalar(pick[:, t, :], slots, seat[:, t, bass.ds(n, 1)], None, ALU.is_equal)
                nc.vector.tensor_copy(gate_col[:], route[:, GATE, :, bass.ds(e, 1)].rearrange("p t e -> p (t e)")).then_inc(m_pick, 1)

            def gather_lo(n):
                for b in range(2):
                    dve.wait_ge(m_ga_hi, 2 * n + b + 1)
                    dst = slice(4 * b, 4 * b + 4)
                    nc.vector.tensor_tensor(xe_lo[:, dst, :].rearrange("p k s -> p (k s)"), psum[:, 4 + b, :],
                                            xe_hi[:, dst, :].rearrange("p k s -> p (k s)").bitcast(F32),
                                            ALU.subtract).then_inc(m_ga_lo, 1)

            def make_current(n):
                dve.wait_ge(m_put_r, 2 * n + 2)
                nc.vector.tensor_copy(put[:], put_next[:].bitcast(F32))
                nc.vector.tensor_copy(slot_gate[:, 1:2], slot_gate[:, 0:1]).then_inc(m_cur, 1)

            def turn_lo(n, g):
                k0, kc, bank, _ = TURNS[g]
                dve.wait_ge(m_thi, 6 * n + g + 1)
                nc.vector.tensor_tensor(hTe_lo[:, k0:k0 + kc, :].rearrange("p k s -> p (k s)"), psum[:, bank, 0:kc * P],
                                        hTe_hi[:, k0:k0 + kc, :].rearrange("p k s -> p (k s)").bitcast(F32),
                                        ALU.subtract).then_inc(m_tlo, 1)

            def block_e(n, b):
                split_lo(dve, *up_group(n, b + 1), up_shapes(b + 1))
                dve.wait_ge(m_silu, 8 * n + b + 1)
                nc.vector.tensor_tensor(h_e[:, b * NU:(b + 1) * NU], silu_e[:, b % 2, :], psum[:, 2 * (b % 2) + 1, 0:NU],
                                        ALU.mult).then_inc(m_h, 1)

            def add_half(n, half):
                cols = slice(half * NB, (half + 1) * NB)
                dve.wait_ge(m_sc, 2 * n + half + 1)
                nc.vector.tensor_tensor(x[:, :, cols], x[:, :, cols], psum[:, 4 + 2 * half:6 + 2 * half, :],
                                        ALU.add).then_inc(m_acc, 1)

            def expert(n, e, last):
                q0 = q_moe(n)
                if not last:
                    dve.wait_ge(m_gt, n + 1)
                    pick_tokens(n + 1, e + 1)
                for b in range(1, UB):
                    block_e(n, b)
                    if b in TURN_AFTER:
                        turn_lo(n, TURN_AFTER[b])
                if not last:
                    gather_lo(n + 1)
                turn_lo(n, 5)
                split_lo(dve, q0 + 4, 1, G_DN[1])
                split_lo(dve, q0 + 5, 0, G_DN[0])
                for half in range(2):
                    if half:
                        split_lo(dve, q0 + 5, 1, G_DN[1])
                        add_half(n, 0)
                        if not last:
                            split_lo(dve, q0 + 6, 0, G_UP)
                    cols = slice(half * NB, (half + 1) * NB)
                    dve.wait_ge(m_yhi, 2 * n + half + 1)
                    nc.vector.scalar_tensor_tensor(y_lo[:, cols], psum[:, 2 * half, :], slot_gate[:, 1:2],
                                                   y_hi[:, cols].bitcast(F32), ALU.mult, ALU.subtract).then_inc(m_ylo, 1)
                if not last:
                    block_e(n + 1, 0)
                add_half(n, 1)
                if not last:
                    make_current(n + 1)

            pick_tokens(0, 0)
            gather_lo(0)
            make_current(0)
            nc.vector.memset(mv[:, 0, :], 0.0).then_inc(m_h, 1)
            nc.vector.memset(mv[:, 1, :], 0.0).then_inc(m_h, 1)
            nc.vector.memset(stat[:], 0.0).then_inc(m_acc, 1)
            dve.wait_ge(xn_set, 1)
            link(nc.vector.tensor_scalar(x[:], x[:], ALPHA, None, ALU.mult))
            block_e(0, 0)
            with dve.Fori(0, NE - 1) as n:
                expert(n, n, False)
            expert(NE - 1, NE - 1, True)
            dve.wait_ge(m_acc, 2 * NE + 1)
            flag = dve.value_load(more[0:1, 0:1], min_val=0, max_val=1)
            with dve.If(flag):
                with dve.Fori(0, NE) as e:
                    split_lo(dve, q_moe(e + NE), 0, G_UP)
                    dve.wait_ge(m_gt, e + NE)
                    pick_tokens(e + NE, e)
                    gather_lo(e + NE)
                    make_current(e + NE)
                    block_e(e + NE, 0)
                    expert(e + NE, e, True)
                dve.wait_ge(m_acc, 4 * NE + 1)
            for t in range(NT):
                for half in range(2):
                    link(nc.vector.bn_stats(stat[:, t, half, :], x[:, t, half * NB:(half + 1) * NB]))
            layer_norm(3)
            dve.wait_ge(ln_done, 4)
            nc.vector.memset(mv[:, 0, :], 0.0).then_inc(out_ready, 1)

        @block.tensor
        def _(pe):
            def transpose_chunks(src):
                for b in range(4):
                    for kk in range(2):
                        for t in range(NT):
                            ins = nc.tensor.transpose(psum[:, 4 + b, kk * S + t * P:kk * S + t * P + P],
                                                      src(2 * b + kk, t), ident)
                    ins.then_inc(t_ps, 1)

            def x_chunk(k, t):
                return x[:, t, k * P:(k + 1) * P]

            def square_block(q, par, bank):
                for j in range(GT):
                    tile_products(pe, q, par, j, 2, NB, 2 * j, (xT_hi, xT_lo),
                                  [(psum[:, bank + t, :], t * P) for t in range(NT)], 0, KD - 1)

            pe.wait_ge(x_in, 16)
            pe.wait_ge(const_in, 16)
            transpose_chunks(x_chunk)
            pe.wait_ge(t_lo, 4)
            for par in range(2):
                square_block(Q_IN, par, 2 * par)
            with pe.Fori(1, 4) as q:
                for par in range(2):
                    pe.wait_ge(in_act, 2 * q + par - 1)
                    pe.wait_ge(in_dve, 2 * q + par - 1)
                    square_block(Q_IN + q, par, 2 * par)

            pe.wait_ge(in_act, 8)
            pe.wait_ge(in_dve, 8)
            for i in range(3):
                if i == 1:
                    pe.wait_ge(g_k, 1)
                for hp in range(2):
                    for hh in range(2):
                        for t in range(NT):
                            h = 2 * hp + hh
                            src = proj[:, t, h * AD:(h + 1) * AD] if i == 0 else sB[:, t, (i - 1) * 512 + h * AD:(i - 1) * 512 + (h + 1) * AD]
                            ins = nc.tensor.transpose(psum[:, 2 * i + hp, hh * S + t * P:hh * S + t * P + P], src, ident)
                    ins.then_inc(ht2_ps, 1)

            lf_hi = xT_hi[:].rearrange("p k s -> p (k s)").rearrange("p (t d c) -> p t d c", t=2, d=2)
            lf_lo = xT_lo[:].rearrange("p k s -> p (k s)").rearrange("p (t d c) -> p t d c", t=2, d=2)

            def exponents(n):
                li, pair = n // 2, n % 2
                if n == 0:
                    pe.wait_ge(g_lo, 1)
                    pe.wait_ge(g_lev, 1)
                    pe.wait_ge(ht2_act, 3)
                    pe.wait_ge(ht2_dve, 3)
                if n >= 2:
                    pe.wait_ge(e_exp, n - 1)
                for hh in range(2):
                    h = 2 * pair + hh
                    for d in range(2):
                        for t in range(NT):
                            dst = psum[:, 2 * (n % 2) + hh, d * S + t * P:d * S + t * P + P]
                            m = lev[:, d, t if li == 0 else li + 1, :]
                            nc.tensor.matmul(dst, lf_hi[:, t, d, h * AD:(h + 1) * AD], m, start=True, stop=False)
                            ins = nc.tensor.matmul(dst, lf_lo[:, t, d, h * AD:(h + 1) * AD], m, start=False, stop=True)
                ins.then_inc(e_ps, 1)

            def scores(n):
                li, pair = n // 2, n % 2
                if n >= 2:
                    pe.wait_ge(s_ev, n - 1)
                if n < 2 * NL:
                    pe.wait_ge(e_qk, n + 1)
                for hh in range(2):
                    h = 2 * pair + hh
                    for i in range(2):
                        dst = psum[:, 4 + n % 2, hh * S + i * P:hh * S + i * P + P]
                        ts, tt = (i, 1 - i) if li == 0 else (i, i)
                        if n < 2 * NL:
                            q_, k_ = (qk2[n % 2][:, w, hh, :] for w in range(2))
                            ins = nc.tensor.matmul(dst, k_[:, ts * P:(ts + 1) * P], q_[:, tt * P:(tt + 1) * P], start=True, stop=True)
                        else:
                            q_ = hT[:, 0, h, tt * P:(tt + 1) * P]
                            nc.tensor.matmul(dst, hT[:, 1, h, ts * P:(ts + 1) * P], q_, start=True, stop=False)
                            ins = nc.tensor.matmul(dst, hT[:, 2, h, ts * P:(ts + 1) * P], q_, start=False, stop=True)
                ins.then_inc(s_ps, 1)

            exponents(0)
            for n in range(2 * NL + 2):
                if n + 1 < 2 * NL:
                    exponents(n + 1)
                scores(n)
            pe.wait_ge(s_ev, 2 * NL + 2)
            for t in range(NT):
                for h in range(AH):
                    dst = psum[:, 6 + t, h * AD:(h + 1) * AD]
                    v = [proj[:, tt, VA + h * AD:VA + (h + 1) * AD] for tt in range(NT)]
                    nc.tensor.matmul(dst, ATd[:, t, h, :], v[t], start=True, stop=False)
                    ins = nc.tensor.matmul(dst, ATo[:, h, 1 - t, :], v[1 - t], start=False, stop=True)
            ins.then_inc(o_ps, 1)

            pe.wait_ge(rope_done, 8)
            pe.wait_ge(e_exp, 2 * NL)
            for b in range(4):
                for kk in range(2):
                    for t in range(NT):
                        col = QB + (2 * b + kk) * P
                        ins = nc.tensor.transpose(psum[:, b, kk * S + t * P:kk * S + t * P + P], proj[:, t, col:col + P], ident)
                ins.then_inc(bt_ps, 1)

            def b_scores(h):
                if h == 0:
                    pe.wait_ge(bt_act, 2)
                    pe.wait_ge(bt_dve, 2)
                if h >= 4:
                    pe.wait_ge(b_nm, h - 3)
                rows = slice(BD * (h % 2), BD * (h % 2) + BD)
                for t in range(NT):
                    ins = nc.tensor.matmul(psum[:, h % 4, t * S:(t + 1) * S], qkT[rows, h // 2, t * P:(t + 1) * P],
                                           qkT[rows, 4 + h // 2, :], start=True, stop=True)
                ins.then_inc(b_s, 1)

            def turn(src, h, done):
                for sc in range(NT):
                    for t in range(NT):
                        ins = nc.tensor.transpose(psum[:, 4 + h % 2, sc * S + t * P:sc * S + t * P + P],
                                                  src[:, t, sc * P:(sc + 1) * P], ident)
                ins.then_inc(done, 1)

            def b_turn(h):
                pe.wait_ge(b_p, 2 * h + 2)
                if h >= 2:
                    pe.wait_ge(b_te, h - 1)
                turn(zP[h % 2], h, b_tp)

            def b_values(h):
                pe.wait_ge(b_te, h + 1)
                if h == 0:
                    pe.wait_ge(mix_done, 1)
                for t in range(NT):
                    for sc in range(NT):
                        ins = nc.tensor.matmul(psum[:, 6 + t, h * BD:(h + 1) * BD], pT[h % 2][:, sc, t * P:(t + 1) * P],
                                               proj[:, sc, VB + h * BD:VB + (h + 1) * BD], start=(sc == 0), stop=(sc == NT - 1))
                ins.then_inc(b_av, 1)

            for h in range(BH + 2):
                if h < BH:
                    b_scores(h)
                if 1 <= h <= BH:
                    b_turn(h - 1)
                if h >= 2:
                    b_values(h - 2)
            pe.wait_ge(mix_done, 3)
            transpose_chunks(lambda k, t: proj[:, t, k * P:(k + 1) * P])
            pe.wait_ge(t_lo, 8)
            for par in range(2):
                square_block(Q_OUT, par, 2 * par)

            pe.wait_ge(ln_done, 1)
            transpose_chunks(x_chunk)
            pe.wait_ge(t_lo, 12)

            def up_block(q, par, wait):
                if wait:
                    pe.wait_ge(up_h, 2 * q + par - 1)
                for j in range(GT):
                    tile_products(pe, Q_UP + q, par, j, 4, NU, 4 * (j % 2), (xT_hi, xT_lo),
                                  [(psum[:, 4 * par + 2 * (j // 2) + t, 0:NU], t * P) for t in range(NT)], 0, KD - 1)

            for par in range(2):
                up_block(0, par, False)
            with pe.Fori(1, 4) as q:
                for par in range(2):
                    up_block(q, par, True)
            pe.wait_ge(up_h, 8)

            n_turned = [0]

            def turn_hidden(upto):
                while n_turned[0] < min(upto, KF // 2):
                    g = n_turned[0]
                    n_turned[0] += 1
                    if g >= 4:
                        pe.wait_ge(ht_lo, g - 3)
                    for kk in range(2):
                        for t in range(NT):
                            k = 2 * g + kk
                            ins = nc.tensor.transpose(psum[:, g % 4, kk * S + t * P:kk * S + t * P + P],
                                                      h_nat[:, t, k * P:(k + 1) * P], ident)
                    ins.then_inc(ht_ps, 1)

            for half in range(2):
                for part in range(2):
                    for j, (kc, n) in enumerate(G_DN[part]):
                        k0 = DN_K0[part][j]
                        if half == 0:
                            need = (k0 + kc + 1) // 2
                            turn_hidden(need + 3)
                            pe.wait_ge(ht_lo, need)
                        tile_products(pe, Q_DN + half, part, j, kc, n, k0, (hT_hi, hT_lo),
                                      [(psum[:, 4 + 2 * half + t, :], t * P) for t in range(NT)], 0, KF - 1)

            pe.wait_ge(ln_done, 2)
            transpose_chunks(x_chunk)
            pe.wait_ge(t_lo, 16)
            for par in range(2):
                square_block(Q_IN2, par, 2 * par)
            with pe.Fori(1, 3) as q:
                for par in range(2):
                    pe.wait_ge(in_act, 8 + 2 * q + par - 1)
                    pe.wait_ge(in_dve, 8 + 2 * q + par - 1)
                    square_block(Q_IN2 + q, par, 2 * par)

            pe.wait_ge(rope2_dve, 6)
            pe.wait_ge(rope2_pool, 2)
            for b in range(8):
                for kk in range(2):
                    for t in range(NT):
                        col = (2 * b + kk) * P
                        ins = nc.tensor.transpose(psum[:, b, kk * S + t * P:kk * S + t * P + P], proj2[:, t, col:col + P], ident)
                ins.then_inc(bt_ps, 1)
            pe.wait_ge(bt_act, 6)
            pe.wait_ge(bt_dve, 6)

            def map_scores(h):
                if h >= 2:
                    pe.wait_ge(c_e, 4 * (h - 1))
                for t in range(NT):
                    for m in range(2):
                        rows = slice(CD * m, CD * m + CD)
                        ins = nc.tensor.matmul(psum[:, 2 * (h % 2) + m, t * S:(t + 1) * S], qkT2[rows, h, t * P:(t + 1) * P],
                                               qkT2[rows, 8 + h, :], start=True, stop=True)
                ins.then_inc(c_s, 1)

            def map_turn(h):
                pe.wait_ge(c_a, h + 1)
                if h >= 2:
                    pe.wait_ge(c_te, h - 1)
                turn(aP[h % 2], h, c_tp)

            def map_values(h):
                pe.wait_ge(c_te, h + 1)
                if h == 4:
                    pe.wait_ge(mix_done, 4)
                for t in range(NT):
                    for sc in range(NT):
                        ins = nc.tensor.matmul(psum[:, 6 + t, (h % 4) * 128:(h % 4 + 1) * 128], aT[h % 2][:, sc, t * P:(t + 1) * P],
                                               proj2[:, sc, 2 * D + h * 128:2 * D + (h + 1) * 128], start=(sc == 0), stop=(sc == NT - 1))
                ins.then_inc(c_av, 1)

            for h in range(CH + 2):
                if h < CH:
                    map_scores(h)
                if 1 <= h <= CH:
                    map_turn(h - 1)
                if h >= 2:
                    map_values(h - 2)
            pe.wait_ge(mix_done, 5)
            transpose_chunks(lambda k, t: proj2[:, t, k * P:(k + 1) * P])
            pe.wait_ge(t_lo, 20)
            for par in range(2):
                square_block(Q_OUT2, par, 2 * par)

            pe.wait_ge(ln_done, 3)
            transpose_chunks(x_chunk)
            pe.wait_ge(rx_act, 2)
            pe.wait_ge(rx_dve, 2)
            pe.wait_ge(rt_in, 16)
            for t in range(NT):
                for k in range(KD):
                    ins = nc.tensor.matmul(psum[:, 0, t * NE:(t + 1) * NE], xT_f[:, k, t * P:(t + 1) * P], router[:, k, :],
                                           start=(k == 0), stop=(k == KD - 1))
            ins.then_inc(m_lg, 1)
            SEL = 5
            pe.wait_ge(m_sel, 1)
            pe.wait_ge(ones_set, 1)
            nc.tensor.matmul(psum[:, 1, 0:NE], earlier, route[:, SEL, 0, :], start=True, stop=True)
            nc.tensor.matmul(psum[:, 1, NE:2 * NE], ones[:], route[:, SEL, 0, :], start=True, stop=False)
            nc.tensor.matmul(psum[:, 1, NE:2 * NE], earlier, route[:, SEL, 1, :], start=False, stop=True)
            for t in range(NT):
                ins = nc.tensor.matmul(psum[:, 2, 0:NE], ones[:], route[:, SEL, t, :], start=(t == 0), stop=(t == NT - 1))
            ins.then_inc(m_pos, 1)

            def gather(n):
                pe.wait_ge(m_pick, n + 1)
                for k in range(KD):
                    for t in range(NT):
                        ins = nc.tensor.matmul(psum[:, 4 + k // 4, (k % 4) * P:(k % 4 + 1) * P],
                                               xn[:, t, k * P:(k + 1) * P], pick[:, t, :], start=(t == 0), stop=(t == NT - 1))
                    if k % 4 == 3:
                        ins.then_inc(m_ga, 1)
                for t in range(NT):
                    ins = nc.tensor.transpose(psum[:, 6, 2 * P + t * P:3 * P + t * P], pick[:, t, :], ident)
                for t in range(NT):
                    ins = nc.tensor.matmul(psum[:, 6, 0:1], pick[:, t, :], gate_col[:, t:t + 1],
                                           start=(t == 0), stop=(t == NT - 1))
                ins.then_inc(m_gt, 1)

            def turn_hidden_e(n, g):
                k0, kc, bank, _ = TURNS[g]
                for k in range(kc):
                    ins = nc.tensor.transpose(psum[:, bank, k * P:(k + 1) * P], h_e[:, (k0 + k) * P:(k0 + k + 1) * P], ident)
                ins.then_inc(m_tp, 1)

            def scatter(n, half):
                pe.wait_ge(m_ylo, 2 * n + half + 1)
                pe.wait_ge(m_cur, n + 1)
                for t in range(NT):
                    dst = psum[:, 4 + 2 * half + t, :]
                    cols = slice(half * NB, (half + 1) * NB)
                    nc.tensor.matmul(dst, put[:, t * P:(t + 1) * P], y_hi[:, cols], start=True, stop=False)
                    ins = nc.tensor.matmul(dst, put[:, t * P:(t + 1) * P], y_lo[:, cols], start=False, stop=True)
                ins.then_inc(m_sc, 1)

            def block_e(n, b):
                pe.wait_ge(m_h, 8 * n + b + 1)
                for j in range(GT):
                    tile_products(pe, *up_group(n, b), j, 4, NU, 4 * (j % 2), (xe_hi, xe_lo),
                                  [(psum[:, 2 * (b % 2) + j // 2, 0:NU], 0)], 0, KD - 1)

            def first_block(n):
                pe.wait_ge(m_ga_hi, 2 * n + 2)
                pe.wait_ge(m_ga_lo, 2 * n + 2)
                block_e(n, 0)

            def expert(n, last):
                q0 = q_moe(n)
                for b in range(1, UB):
                    block_e(n, b)
                    if b == GATHER_AFTER:
                        pe.wait_ge(m_acc, 2 * n + 1)
                        if not last:
                            gather(n + 1)
                    if b in TURN_AFTER:
                        g = TURN_AFTER[b]
                        pe.wait_ge(m_h, 8 * n + b + 2)
                        if g == 0 and not last:
                            pe.wait_ge(m_put_r, 2 * n + 4)
                        if g >= 2:
                            pe.wait_ge(m_tlo, 6 * n + g - 1)
                        turn_hidden_e(n, g)
                for half in range(2):
                    for part in range(2):
                        if half and part:
                            if not last:
                                pe.wait_ge(m_ga_lo, 2 * n + 4)
                            scatter(n, 0)
                        for j, (kc, w) in enumerate(G_DN[part]):
                            k0 = DN_K0[part][j]
                            if not half:
                                done = [g for g, (c0, _, _, _) in enumerate(TURNS) if c0 < k0 + kc]
                                pe.wait_ge(m_tlo, 6 * n + len(done))
                            tile_products(pe, q0 + 4 + half, part, j, kc, w, k0, (hTe_hi, hTe_lo),
                                          [(psum[:, 2 * half, :], 0)], 0, KF - 1)
                            if not half and not part and j == 0:
                                pe.wait_ge(m_h, 8 * n + 10)
                                turn_hidden_e(n, 5)
                if not last:
                    first_block(n + 1)
                scatter(n, 1)

            pe.wait_ge(xn_set, 1)
            pe.wait_ge(more_set, 1)
            gather(0)
            first_block(0)
            with pe.Fori(0, NE - 1) as n:
                expert(n, False)
            expert(NE - 1, True)
            flag = pe.value_load(more[0:1, 0:1], min_val=0, max_val=1)
            with pe.If(flag):
                with pe.Fori(NE, 2 * NE) as n:
                    pe.wait_ge(m_acc, 2 * n + 1)
                    gather(n)
                    first_block(n)
                    expert(n, True)


_INPUTS = ["x", "ev_w_in", "ev_lb_logits", "ev_hgrn_norm", "ev_w_out", "ev_ln1_g", "ev_ln1_b", "ev_w1", "ev_w3", "ev_w2",
           "ev_ln2_g", "ev_ln2_b", "od_w_in", "od_lambda", "od_subln", "od_w_out", "od_ln1_g", "od_ln1_b", "od_router",
           "od_w1", "od_w3", "od_w2", "od_ln2_g", "od_ln2_b"]


def kernel(**inputs):
    import concourse.bacc as bacc
    from concourse.bass_utils import run_bass_kernel_spmd as run

    nc = bacc.Bacc("TRN2", target_bir_lowering=False, num_devices=1)
    arrays, ins, consts = {}, {}, {}
    for name in _INPUTS:
        v = np.ascontiguousarray(inputs[name])
        arrays[f"in_{name}"] = v
        ins[name] = nc.dram_tensor(f"in_{name}", v.shape, mybir.dt.from_np(v.dtype), kind="ExternalInput").ap()
    for name, v in constants().items():
        arrays[f"const_{name}"] = v
        consts[name] = nc.dram_tensor(f"const_{name}", v.shape, mybir.dt.from_np(v.dtype), kind="ExternalInput").ap()
    out = nc.dram_tensor("out", (1, S, D), F32, kind="ExternalOutput").ap()
    trunk(nc, ins, consts, out)
    return run(nc, [arrays], core_ids=[0]).results[0]["out"]
```

```python
import math
from contextlib import ExitStack

import numpy as np
import concourse.bass as bass
from concourse import mybir

ALU = mybir.AluOpType
ACT = mybir.ActivationFunctionType
AX_X = mybir.AxisListType.X
F32 = mybir.dt.float32
F32R = mybir.dt.float32r
U8 = mybir.dt.uint8
I32 = mybir.dt.int32

P = 128
S, D = 256, 1024
NT = S // P
KD = D // P
AH, AD = 4, 128
BH, BD = 8, 64
CH, CD = 8, 64
FF = 2816
KF = FF // P
NE = 8
EVEN_IN, ODD_IN = 4096, 3072
QA, ZF, ZB, VA, GA, QB, KB, VB = (512 * i for i in range(8))
DEPTH = 2
ALPHA = (2 * DEPTH) ** 0.25
LAMBDA_INIT = 0.8 - 0.6 * math.exp(-0.3 * 1)
EPS = 1e-5
MIN_FORGET = 1e-30
LEVELS = (128, 64, 32, 16, 8, 4, 2, 1)
NL = len(LEVELS)

NB = 512
NU = 352
UB = FF // NU
TILE = 1536
GT = 4
RAW = 2 * GT
G_SQ = [(2, NB)] * GT
G_UP = [(4, NU)] * GT
G_DN = [[(3, NB)] * 4, [(3, NB), (3, NB), (2, NB), (2, NB)]]
DN_K0 = [[0, 3, 6, 9], [12, 15, 18, 20]]


def level_matrices():
    u, t = np.arange(P)[:, None], np.arange(P)[None, :]
    out = np.zeros((P, 2, NL + 1, P), np.float32)
    out[:, 0, 0], out[:, 1, 0] = u > t, u >= t
    out[:, 0, 1], out[:, 1, 1] = u <= t, u < t
    for i, m in enumerate(LEVELS[1:]):
        mid = t // (2 * m) * 2 * m + m
        right = t >= mid
        out[:, 0, 2 + i] = np.where(right, (u >= mid) & (u <= t), (u > t) & (u < mid))
        out[:, 1, 2 + i] = np.where(right, (u >= mid) & (u < t), (u >= t) & (u < mid))
    return out.reshape(P, -1)


def level_masks():
    s, t = np.arange(P)[:, None], np.arange(P)[None, :]
    ms = [(s // (2 * m) == t // (2 * m)) & (s // m != t // m) for m in LEVELS[2:]] + [s == t]
    return np.stack(ms, 1).astype(np.float32).reshape(P, -1)


def constants():
    pos = np.arange(S)
    diff = pos[:, None] - pos[None, :]
    times = (np.abs(diff) <= 64).astype(np.int32) + (diff % 4 == 0) + (diff % 16 == 0)
    bias = np.where(times > 0, np.log(np.maximum(times, 1).astype(np.float32)), -1e30).astype(np.float32)
    inv = np.float32(10000.0) ** (-np.arange(0, BD, 2, dtype=np.float32) / np.float32(BD))
    ang = pos.astype(np.float32)[:, None] * inv.astype(np.float32)[None, :]
    rope = np.concatenate([np.cos(ang), np.sin(ang)], 1).astype(np.float32)
    a = np.arange(P)
    e = np.arange(NE)
    small = np.zeros((P, 3, P), np.float32)
    small[:, 0] = np.eye(P)
    small[:, 1] = a[:, None] < a[None, :]
    small[:, 2] = a[None, :]
    before = np.broadcast_to((e[None, :] < e[:, None]).astype(np.float32).reshape(1, -1), (P, NE * NE))
    return {
        "levels": np.concatenate([level_matrices(), level_masks()], 1),
        "band": np.ascontiguousarray(bias.reshape(NT, P, S).transpose(1, 0, 2)).reshape(P, -1),
        "rope": np.ascontiguousarray(rope.reshape(NT, P, BD).transpose(1, 0, 2)).reshape(P, -1),
        "small": small.reshape(P, -1),
        "before": np.ascontiguousarray(before),
    }


def trunk(nc, a, c, out):
    with ExitStack() as ctx:
        sem = lambda name: ctx.enter_context(nc.semaphore(name))

        base = (nc.sbuf_base + 63) // 64 * 64
        top = nc.sbuf_usable_end
        cur = [base]

        def at(name, shape, dt=F32, offset=None):
            size = int(np.prod(shape[1:])) * (1 if dt == U8 else 4)
            here = cur[0] if offset is None else offset
            if offset is None:
                cur[0] = here + (size + 31) // 32 * 32
            assert here + size <= top, (name, here + size, top)
            return nc.alloc_sbuf_tensor_at(name, shape, dt, offset=here), here + (size + 31) // 32 * 32

        def own(name, shape, dt=F32):
            return at(name, shape, dt)[0]

        raw = [own(f"raw{i}", [P, TILE]) for i in range(RAW)]
        whi = [own(f"whi{i}", [P, TILE], F32R) for i in range(GT)]
        wlo = [own(f"wlo{i}", [P, TILE], F32R) for i in range(GT)]
        x = own("x", [P, NT, D])
        xT_hi = own("xT_hi", [P, KD, S], F32R)
        xT_lo = own("xT_lo", [P, KD, S], F32R)
        small = own("small", [P, 3, P])
        ident, earlier, slots = small[:, 0, :], small[:, 1, :], small[:, 2, :]
        rope = own("rope", [P, NT, 2, BD // 2])
        stat = own("stat", [P, NT, 2, 6])
        mv = own("mv", [P, NT, 2])
        ln_rs = own("ln_rs", [P, NT])
        neg_half = own("neg_half", [P, 8])
        vec = own("vec", [P, 96])
        phase = cur[0]

        gains, after_gains = at("gains", [P, 2, D], F32, phase)
        lev, after_lev = at("lev", [P, 2, NL + 1, P], F32R, phase)
        o = max(after_gains, after_lev)
        masks, o = at("masks", [P, NL - 1, P], U8, o)
        band, o = at("band", [P, NT, S], F32, o)
        lbs, o = at("lbs", [P, 2, 512], F32, o)
        proj, o = at("proj", [P, NT, EVEN_IN], F32, o)
        levraw = nc.alloc_sbuf_tensor_at("levraw", [P, (2 * (NL + 1) + NL - 1) * P], F32, offset=o)
        sA, oA = at("sA", [P, NT, 1024], F32, o)
        expE = [at(f"expE{i}", [P, 2, 2, S], F32, o + i * 4096)[0] for i in range(2)]
        sB, oB = at("sB", [P, NT, 1024], F32, oA)
        qk2 = [at(f"qk2_{i}", [P, 2, 2, S], F32, oA + i * 4096)[0] for i in range(2)]
        hT, oC = at("hgT", [P, 3, AH, S], F32, oB)
        ATo, oD = at("ATo", [P, AH, 2, P], F32, oC)
        ATd = proj[:, :, ZB:ZB + 512].rearrange("p t (h c) -> p t h c", h=AH)
        qkT, q1 = at("qkT", [P, 8, S], F32, oB)
        zP = [at(f"zP{i}", [P, NT, S], F32, q1 + 2048 * i)[0] for i in range(2)]
        pT = [at(f"pT{i}", [P, NT, S], F32, q1 + 4096 + 2048 * i)[0] for i in range(2)]
        ropeT, oE = at("ropeT", [P, 2, 512], F32, max(oD, q1 + 8192))
        hnorm, oF = at("hnorm", [P, AD], F32, oE)
        sga = at("sga", [P, NT, 512], F32, oC)[0]
        h_nat, f1 = at("h_nat", [P, NT, FF], F32, after_gains)
        hT_hi, f2 = at("hT_hi", [P, KF, S], F32R, f1)
        hT_lo, f3 = at("hT_lo", [P, KF, S], F32R, f2)
        silu, f4 = at("silu", [P, NT, NU], F32, f3)
        proj2, d1 = at("proj2", [P, NT, ODD_IN], F32, after_gains)
        qkT2, d2 = at("qkT2", [P, 16, S], F32, d1)
        eP = [at(f"eP{i}", [P, 2, NT, S], F32, d2 + 4096 * i)[0] for i in range(2)]
        aP = [at(f"aP{i}", [P, NT, S], F32, d2 + 8192 + 2048 * i)[0] for i in range(2)]
        aT = [at(f"aT{i}", [P, NT, S], F32, d2 + 12288 + 2048 * i)[0] for i in range(2)]
        rtP, d4 = at("rtP", [P, 2, 1024], F32, d2 + 16384)
        sub, d5 = at("sub", [P, 2 * CD], F32, d4)
        lamv, d6 = at("lamv", [P, 4, CD], F32, d5)
        sq2 = proj2[:, :, D:D + 512].rearrange("p t (h c) -> p t h c", h=4)
        on2 = proj2[:, :, D + 512:2 * D].rearrange("p t (h c) -> p t h c", h=4)

        four_heads = lambda v: v[:].rearrange("p a b c -> p (a b c)").rearrange("p (t h c) -> p t h c", t=NT, h=4)
        sq0, on0 = four_heads(expE[0]), four_heads(qk2[0])

        xn, m2 = at("xn", [P, NT, D], F32, after_gains)
        xe_hi, m3 = at("xe_hi", [P, KD, P], F32R, m2)
        xe_lo, m4 = at("xe_lo", [P, KD, P], F32R, m3)
        h_e, m5 = at("h_e", [P, FF], F32, m4)
        hTe_hi, m6 = at("hTe_hi", [P, KF, P], F32R, m5)
        hTe_lo, m7 = at("hTe_lo", [P, KF, P], F32R, m6)
        silu_e, m8 = at("silu_e", [P, 2, NU], F32, m7)
        pick, m9 = at("pick", [P, NT, P], F32, m8)
        put_next, m10 = at("put_next", [P, S], F32R, m9)
        put, m11 = at("put", [P, S], F32R, m10)
        y_hi, m12 = at("y_hi", [P, D], F32R, m11)
        y_lo, m13 = at("y_lo", [P, D], F32R, m12)
        xT_f, m14 = at("xT_f", [P, KD, S], F32, m5)
        router, m15 = at("router", [P, KD, NE], F32, m13)
        route, m16 = at("route", [P, 12, NT, NE], F32, m15)
        cmp, m17 = at("cmp", [P, 2, NT, NE, NE], F32, m16)
        before, m18 = at("before", [P, NE, NE], F32, m17)
        ones, m19 = at("ones", [P, P], F32, m18)
        seat, m20 = at("seat", [P, NT, 2 * NE], F32, m19)
        gate_col, m21 = at("gate_col", [P, NT], F32, m20)
        slot_gate, m22 = at("slot_gate", [P, 2], F32, m21)
        more, m23 = at("more", [P, 1], I32, m22)

        psum = ctx.enter_context(nc.psum_tensor("psum", [P, 8, 512], F32))

        raw_full = [sem(f"raw_full{i}") for i in range(RAW)]
        hi_done, lo_done, tile_used = sem("hi_done"), sem("lo_done"), sem("tile_used")
        const_in, x_in, band_in, lb_in = sem("const_in"), sem("x_in"), sem("band_in"), sem("lb_in")
        lev_in, vec_in, gain_in, lam_in, rope_in = (sem(n) for n in ("lev_in", "vec_in", "gain_in", "lam_in", "rope_in"))
        act_link, dve_link, pool_link = sem("act_link"), sem("dve_link"), sem("pool_link")
        t_ps, t_hi, t_lo = sem("t_ps"), sem("t_hi"), sem("t_lo")
        in_act, in_dve = sem("in_act"), sem("in_dve")
        ln_mv, ln_rstd = sem("ln_mv"), sem("ln_rstd")
        ln_done, mix_done = sem("ln_done"), sem("mix_done")
        up_silu, up_h = sem("up_silu"), sem("up_h")
        ht_ps, ht_hi, ht_lo = sem("ht_ps"), sem("ht_hi"), sem("ht_lo")
        g_sig, g_k, g_f, g_ln, g_hi, g_lo, g_lev = (sem(n) for n in ("g_sig", "g_k", "g_f", "g_ln", "g_hi", "g_lo", "g_lev"))
        gate_c = sem("gate_c")
        lb_e, lb_d = sem("lb_e"), sem("lb_d")
        rope_done = sem("rope_done")
        bt_ps, bt_act, bt_dve = sem("bt_ps"), sem("bt_act"), sem("bt_dve")
        b_s, b_z, b_nm, b_p, b_tp, b_te, b_av, b_out = (sem(n) for n in ("b_s", "b_z", "b_nm", "b_p", "b_tp", "b_te", "b_av", "b_out"))
        ht2_ps, ht2_act, ht2_dve = sem("ht2_ps"), sem("ht2_act"), sem("ht2_dve")
        e_ps, e_exp, e_qk, s_ps, s_ev, o_ps = (sem(n) for n in ("e_ps", "e_exp", "e_qk", "s_ps", "s_ev", "o_ps"))
        r_sq, r_ms, r_rs, r_out = (sem(n) for n in ("r_sq", "r_ms", "r_rs", "r_out"))
        rope2_pool = sem("rope2_pool")
        lam_x, lam_d = sem("lam_x"), sem("lam_d")
        c_s, c_mx, c_e, c_a, c_tp, c_te, c_av = (sem(n) for n in ("c_s", "c_mx", "c_e", "c_a", "c_tp", "c_te", "c_av"))
        rt_in, bf_in, rx_act, rx_dve, m_lg, m_sel, m_ex, m_d, m_pos, more_set, xn_set = (
            sem(n) for n in ("rt_in", "bf_in", "rx_act", "rx_dve", "m_lg", "m_sel", "m_ex", "m_d", "m_pos", "more_set", "xn_set"))
        m_pick, m_ga, m_ga_hi, m_ga_lo, m_put_r, m_gt, m_cur = (
            sem(n) for n in ("m_pick", "m_ga", "m_ga_hi", "m_ga_lo", "m_put_r", "m_gt", "m_cur"))
        m_silu, m_h, m_tp, m_thi, m_tlo, m_yhi, m_ylo, m_sc, m_acc = (
            sem(n) for n in ("m_silu", "m_h", "m_tp", "m_thi", "m_tlo", "m_yhi", "m_ylo", "m_sc", "m_acc"))
        on_kept, heads_out = sem("on_kept"), sem("heads_out")
        ones_set, sub_in, lm_in, lam_s = sem("ones_set"), sem("sub_in"), sem("lm_in"), sem("lam_s")
        rows_done, out_sent = sem("rows_done"), sem("out_sent")

        def by_bank(xT, b):
            return xT[:, 4 * (b % 2):4 * (b % 2) + 4, (b // 2) * P:(b // 2 + 1) * P]

        def rawv(par, j, kc, n):
            return raw[GT * par + j][:, 0:kc * n].rearrange("p (k n) -> p k n", n=n)

        def load_group(sp, q, par, shapes, srcs, first=False):
            for j, ((kc, n), src) in enumerate(zip(shapes, srcs)):
                if not first:
                    sp.wait_ge(lo_done, 2 * GT * q + GT * (par - 2) + j + 1)
                sp.dma_start(rawv(par, j, kc, n), src).then_inc(raw_full[GT * par + j], 16)

        def split_hi(act, q, par, shapes, first=False):
            for j, (kc, n) in enumerate(shapes):
                act.wait_ge(raw_full[GT * par + j], 16 * (q + 1))
                if not first:
                    act.wait_ge(tile_used, 2 * GT * q + GT * (par - 1) + j + 1)
                nc.scalar.copy(whi[j][:, 0:kc * n], raw[GT * par + j][:, 0:kc * n]).then_inc(hi_done, 1)

        def split_lo(dve, q, par, shapes, js=range(GT)):
            for j in js:
                kc, n = shapes[j]
                dve.wait_ge(hi_done, 2 * GT * q + GT * par + j + 1)
                nc.vector.tensor_tensor(wlo[j][:, 0:kc * n], raw[GT * par + j][:, 0:kc * n],
                                        whi[j][:, 0:kc * n].bitcast(F32), ALU.subtract).then_inc(lo_done, 1)

        def group_used(q, par):
            return 2 * GT * q + GT * (par + 1)

        def tile_products(pe, q, par, j, kc, n, k0, lhs, outs, first_k, last_k):
            pe.wait_ge(lo_done, 2 * GT * q + GT * par + j + 1)
            hi, lo = lhs
            for kk in range(kc):
                k = k0 + kk
                w_h = whi[j][:, kk * n:(kk + 1) * n]
                w_l = wlo[j][:, kk * n:(kk + 1) * n]
                for ps, t0 in outs:
                    nc.tensor.matmul(ps, hi[:, k, t0:t0 + P], w_h, start=(k == first_k), stop=False)
                    nc.tensor.matmul(ps, hi[:, k, t0:t0 + P], w_l, start=False, stop=False)
                    last = nc.tensor.matmul(ps, lo[:, k, t0:t0 + P], w_h, start=False, stop=(k == last_k))
            last.then_inc(tile_used, 1)

        Q_IN, Q_OUT, Q_UP, Q_DN, Q_IN2, Q_OUT2, Q_MOE = 0, 4, 5, 9, 11, 14, 15
        w_in = a["ev_w_in"][0].rearrange("(k p) n -> p k n", p=P)
        w_out = a["ev_w_out"][0].rearrange("(k p) n -> p k n", p=P)
        w_1 = a["ev_w1"][0].rearrange("(k p) n -> p k n", p=P)
        w_3 = a["ev_w3"][0].rearrange("(k p) n -> p k n", p=P)
        w_2 = a["ev_w2"][0].rearrange("(k p) n -> p k n", p=P)
        w_in2 = a["od_w_in"][0].rearrange("(k p) n -> p k n", p=P)
        w_out2 = a["od_w_out"][0].rearrange("(k p) n -> p k n", p=P)

        def sq_src(w, b):
            return [w[:, 2 * j:2 * j + 2, bass.ds(b * NB, NB)] for j in range(GT)]

        def up_src(w1, w3, b):
            return [w[:, 4 * j:4 * j + 4, bass.ds(b * NU, NU)] for w in (w1, w3) for j in range(2)]

        def dn_src(w2, half, part):
            return [w2[:, k0:k0 + kc, half * NB:(half + 1) * NB] for k0, (kc, _) in zip(DN_K0[part], G_DN[part])]

        m_w1 = a["od_w1"][0].rearrange("e (k p) n -> p e k n", p=P)
        m_w3 = a["od_w3"][0].rearrange("e (k p) n -> p e k n", p=P)
        m_w2 = a["od_w2"][0].rearrange("e (k p) n -> p e k n", p=P)

        def up_src_e(e, b):
            return [w[:, bass.ds(e, 1), 4 * j:4 * j + 4, bass.ds(b * NU, NU)].rearrange("p e k n -> p (e k) n")
                    for w in (m_w1, m_w3) for j in range(2)]

        def dn_src_e(e, half, part):
            return [m_w2[:, bass.ds(e, 1), k0:k0 + kc, half * NB:(half + 1) * NB].rearrange("p e k n -> p (e k) n")
                    for k0, (kc, _) in zip(DN_K0[part], G_DN[part])]

        TURNS = [(0, 4, 6, 3), (4, 4, 7, 4), (8, 4, 6, 5), (12, 4, 7, 6), (16, 3, 6, 7), (19, 3, 3, None)]
        TURN_AFTER = {after: g for g, (_, _, _, after) in enumerate(TURNS) if after is not None}
        GATHER_AFTER = 2

        def q_moe(n):
            return Q_MOE + 6 * n

        def up_group(n, b):
            return q_moe(n) + b // 2, b % 2

        def up_shapes(b):
            return G_UP if b < UB else G_DN[0]

        block = ctx.enter_context(nc.Block())

        @block.sync
        def _(sp):
            sp.dma_start(x[:], a["x"][0].rearrange("(t p) d -> p t d", p=P)).then_inc(x_in, 16)
            sp.dma_start(small[:].rearrange("p a b -> p (a b)"), c["small"]).then_inc(const_in, 16)
            for par in range(2):
                load_group(sp, 0, par, G_SQ, sq_src(w_in, par), first=True)
            with sp.Fori(1, 4) as q:
                for par in range(2):
                    load_group(sp, Q_IN + q, par, G_SQ, sq_src(w_in, 2 * q + par))
            for par in range(2):
                load_group(sp, Q_OUT, par, G_SQ, sq_src(w_out, par))
            with sp.Fori(0, 4) as q:
                for par in range(2):
                    load_group(sp, Q_UP + q, par, G_UP, up_src(w_1, w_3, 2 * q + par))
            for half in range(2):
                for part in range(2):
                    load_group(sp, Q_DN + half, part, G_DN[part], dn_src(w_2, half, part))
            with sp.Fori(0, 3) as q:
                for par in range(2):
                    load_group(sp, Q_IN2 + q, par, G_SQ, sq_src(w_in2, 2 * q + par))
            for par in range(2):
                load_group(sp, Q_OUT2, par, G_SQ, sq_src(w_out2, par))

            def load_expert(n, e):
                with sp.Fori(0, 4) as q:
                    for par in range(2):
                        load_group(sp, q_moe(n) + q, par, G_UP, up_src_e(e, 2 * q + par))
                for half in range(2):
                    for part in range(2):
                        load_group(sp, q_moe(n) + 4 + half, part, G_DN[part], dn_src_e(e, half, part))

            with sp.Fori(0, NE) as n:
                load_expert(n, n)
            sp.wait_ge(more_set, 1)
            flag = sp.value_load(more[0:1, 0:1], min_val=0, max_val=1)
            with sp.If(flag):
                with sp.Fori(0, NE) as e:
                    load_expert(e + NE, e)
            for t in range(NT):
                sp.wait_ge(ln_done, NT * 3 + t + 1)
                sp.dma_start(out[0][t * P:(t + 1) * P, :], x[:, t, :]).then_inc(out_sent, 16)
            sp.wait_ge(out_sent, 16 * NT)

        @block.gpsimd
        def _(pool):
            n_link = [0]

            def link(ins):
                n_link[0] += 1
                ins.then_inc(pool_link, 1)
                pool.wait_ge(pool_link, n_link[0])

            def load_gains(i, g, b):
                if i:
                    pool.wait_ge(ln_done, NT * i)
                pool.dma_start(gains[:, 0, :], a[g].partition_broadcast(P)).then_inc(gain_in, 16)
                pool.dma_start(gains[:, 1, :], a[b].partition_broadcast(P)).then_inc(gain_in, 16)

            def rsqrt(dst, src, scale):
                link(nc.gpsimd.tensor_scalar(dst, src, scale, EPS, ALU.mult, ALU.add))
                return nc.gpsimd.tensor_tensor(dst, dst, neg_half[:, 0:dst.shape[1]], ALU.pow)

            def ln_rsqrt(i):
                for t in range(NT):
                    pool.wait_ge(ln_mv, NT * i + t + 1)
                    rsqrt(ln_rs[:, t:t + 1], mv[:, t, 1:2], 1.0).then_inc(ln_rstd, 1)

            def rotate(src, t, tmp, done):
                n = src.shape[1] // 32
                both = src.rearrange("p (n c) -> p n c", c=32)
                half = src.rearrange("p (n h c) -> p n h c", h=2, c=32)
                A = tmp[:, 0, 0:n * 32].rearrange("p (n c) -> p n c", c=32)
                B = tmp[:, 1, 0:n * 32].rearrange("p (n c) -> p n c", c=32)
                Ah = tmp[:, 0, 0:n * 32].rearrange("p (n h c) -> p n h c", h=2, c=32)
                Bh = tmp[:, 1, 0:n * 32].rearrange("p (n h c) -> p n h c", h=2, c=32)
                cos = rope[:, t, 0:1, :].broadcast_to([P, n, 32])
                sin = rope[:, t, 1:2, :].broadcast_to([P, n, 32])
                nc.gpsimd.tensor_tensor(A, both, cos, ALU.mult)
                link(nc.gpsimd.tensor_tensor(B, both, sin, ALU.mult))
                nc.gpsimd.tensor_tensor(half[:, :, 0, :], Ah[:, :, 0, :], Bh[:, :, 1, :], ALU.subtract).then_inc(done, 1)
                nc.gpsimd.tensor_tensor(half[:, :, 1, :], Ah[:, :, 1, :], Bh[:, :, 0, :], ALU.add).then_inc(done, 1)

            pool.dma_start(rope[:].rearrange("p t h c -> p (t h c)"), c["rope"]).then_inc(rope_in, 16)
            pool.dma_start(lbs[:, 0, :], a["ev_lb_logits"][0].partition_broadcast(P)).then_inc(lb_in, 16)
            pool.dma_start(levraw[:], c["levels"]).then_inc(lev_in, 16)
            pool.dma_start(band[:].rearrange("p t s -> p (t s)"), c["band"]).then_inc(band_in, 16)
            pool.dma_start(hnorm[:], a["ev_hgrn_norm"][0].partition_broadcast(P)).then_inc(vec_in, 16)
            nc.gpsimd.memset(neg_half[:], -0.5)
            pool.wait_ge(rope_in, 16)
            pool.wait_ge(g_sig, 3)
            pool.wait_ge(vec_in, 16)
            for t in range(NT):
                link(nc.gpsimd.tensor_tensor(proj[:, t, GA:GA + 512], proj[:, t, GA:GA + 512],
                                             sga[:, t, :], ALU.mult))
                v = proj[:, t, GA:GA + 512].rearrange("p (h c) -> p h c", h=AH)
                nc.gpsimd.tensor_tensor(v, v, hnorm[:, None, :].broadcast_to([P, AH, AD]), ALU.mult).then_inc(gate_c, 1)
            pool.wait_ge(in_act, 7)
            pool.wait_ge(in_dve, 7)
            for u, (t, col) in enumerate((t, col) for t in range(NT) for col in (QB, KB)):
                if u:
                    pool.wait_ge(rope_done, 2 * u)
                rotate(proj[:, t, col:col + 512], t, ropeT, rope_done)
            def rms_heads(r, on, gain, dst):
                pool.wait_ge(r_ms, r + 1)
                link(rsqrt(vec[:, 40:48], vec[:, 32:40], 1.0 / AD))
                rs = vec[:, 40:48].rearrange("p (t h) -> p t h", h=4)[:, :, :, None].broadcast_to([P, NT, 4, 128])
                link(nc.gpsimd.tensor_tensor(on, on, rs, ALU.mult))
                nc.gpsimd.tensor_tensor(dst.rearrange("p t (h c) -> p t h c", h=4), on, gain, ALU.mult).then_inc(heads_out, 1)

            rms_heads(0, on0, proj[:, :, GA:GA + 512].rearrange("p t (h c) -> p t h c", h=4), proj[:, :, 0:512])
            load_gains(0, "ev_ln1_g", "ev_ln1_b")
            ln_rsqrt(0)
            load_gains(1, "ev_ln2_g", "ev_ln2_b")
            ln_rsqrt(1)

            pool.wait_ge(ln_done, NT * 2)
            pool.dma_start(sub[:], a["od_subln"][0].partition_broadcast(P)).then_inc(sub_in, 16)
            pool.dma_start(lamv[:].rearrange("p a b -> p (a b)"),
                           a["od_lambda"][0].rearrange("a b -> (a b)").partition_broadcast(P)).then_inc(lm_in, 16)
            load_gains(2, "od_ln1_g", "od_ln1_b")
            for u, (col, t) in enumerate((col, t) for col in (0, D) for t in range(NT)):
                if t == 0:
                    pool.wait_ge(in_act, 10 + 2 * col // D)
                    pool.wait_ge(in_dve, 10 + 2 * col // D)
                if u:
                    pool.wait_ge(rope2_pool, 2 * u)
                rotate(proj2[:, t, col:col + D], t, rtP, rope2_pool)
            rms_heads(1, on2, sub[:, None, None, :].broadcast_to([P, NT, 4, 128]), proj2[:, :, 0:512])
            pool.wait_ge(r_ms, 3)
            rsqrt(vec[:, 40:48], vec[:, 32:40], 1.0 / AD).then_inc(r_rs, 1)
            ln_rsqrt(2)
            pool.wait_ge(ln_done, NT * 3)
            pool.dma_start(router[:], a["od_router"][0].rearrange("(k p) e -> p k e", p=P)).then_inc(rt_in, 16)
            pool.dma_start(before[:].rearrange("p a b -> p (a b)"), c["before"]).then_inc(bf_in, 16)
            nc.gpsimd.memset(ones[:], 1.0).then_inc(ones_set, 1)
            load_gains(3, "od_ln2_g", "od_ln2_b")
            ln_rsqrt(3)


        @block.scalar
        def _(act):
            def transposed_hi(i):
                for b in range(4):
                    act.wait_ge(t_ps, 4 * i + b + 1)
                    nc.scalar.copy(by_bank(xT_hi, b), psum[:, 4 + b, :].rearrange("p (k s) -> p k s", s=P)).then_inc(t_hi, 1)

            def keep_square(sq, on, ready, value):
                act.wait_ge(ready, value)
                nc.scalar.copy(on, psum[:, 6:8, :].rearrange("p t (h c) -> p t h c", h=4)).then_inc(on_kept, 1)
                act.wait_ge(on_kept, 1 if on is on0 else 2)
                nc.scalar.activation(sq, on, ACT.Square).then_inc(r_sq, 1)

            transposed_hi(0)
            split_hi(act, Q_IN, 0, G_SQ, first=True)
            act.wait_ge(lb_d, 1)
            nc.scalar.activation(lbs[:, 0, :], lbs[:, 0, :], ACT.Exp).then_inc(lb_e, 1)

            def in_block(q, par, dst, col, after):
                after()
                act.wait_ge(tile_used, group_used(q, par))
                nc.scalar.copy(dst[:, 0, bass.ds(col, NB)], psum[:, 2 * par, :]).then_inc(in_act, 1)

            def even_block(b):
                q, par = Q_IN + b // 2, b % 2
                nxt = (q, 1) if par == 0 else (q + 1, 0)
                in_block(q, par, proj, b * NB, lambda: split_hi(act, *nxt, G_SQ))

            for b in range(3):
                even_block(b)
            act.wait_ge(in_dve, 3)
            act.wait_ge(in_act, 3)
            act.wait_ge(g_lev, 2)
            nc.scalar.activation(sB[:], proj[:, :, ZF:ZF + 1024], ACT.Sigmoid, scale=-1.0).then_inc(g_sig, 1)
            nc.scalar.activation(sA[:], proj[:, :, ZF:ZF + 1024], ACT.Sigmoid).then_inc(g_sig, 1)
            even_block(3)
            even_block(4)
            act.wait_ge(in_dve, 5)
            act.wait_ge(in_act, 5)
            nc.scalar.activation(sga[:], proj[:, :, GA:GA + 512], ACT.Sigmoid).then_inc(g_sig, 1)
            act.wait_ge(g_f, 1)
            nc.scalar.activation(sA[:], sA[:], ACT.Ln).then_inc(g_ln, 1)
            for b in range(5, 8):
                even_block(b)
            act.wait_ge(g_ln, 1)
            nc.scalar.copy(xT_hi[:].rearrange("p k s -> p (k s)"), sA[:].rearrange("p t c -> p (t c)")).then_inc(g_hi, 1)
            for b in range(0, 6, 2):
                act.wait_ge(ht2_ps, b + 1)
                nc.scalar.copy(hT[:, b // 2, 0:2, :].rearrange("p h s -> p (h s)"), psum[:, b, :]).then_inc(ht2_act, 1)
            for n in range(2 * NL):
                act.wait_ge(e_ps, n + 1)
                if n == 0:
                    act.wait_ge(g_lo, 1)
                if n >= 2:
                    act.wait_ge(e_qk, n - 1)
                nc.scalar.activation(expE[n % 2][:].rearrange("p h d s -> p h (d s)"),
                                     psum[:, 2 * (n % 2):2 * (n % 2) + 2, :], ACT.Exp).then_inc(e_exp, 1)
            for b in (0, 2):
                act.wait_ge(bt_ps, b + 1)
                nc.scalar.copy(qkT[:, 2 * b:2 * b + 2, :].rearrange("p k s -> p (k s)"), psum[:, b, :]).then_inc(bt_act, 1)
            keep_square(sq0, on0, o_ps, 1)

            def move_probs(h):
                act.wait_ge(b_tp, h + 1)
                if h >= 2:
                    act.wait_ge(b_av, h - 1)
                nc.scalar.copy(pT[h % 2][:].rearrange("p s t -> p (s t)"), psum[:, 4 + h % 2, :]).then_inc(b_te, 1)

            for h in range(BH):
                act.wait_ge(b_nm, h + 1)
                for t in range(NT):
                    nc.scalar.activation(zP[h % 2][:, t, :], zP[h % 2][:, t, :], ACT.Exp,
                                         bias=vec[:, 16 + 2 * h + t:17 + 2 * h + t],
                                         accum_out=vec[:, 48 + 2 * h + t:49 + 2 * h + t]).then_inc(b_p, 1)
                if h:
                    move_probs(h - 1)
            move_probs(BH - 1)
            transposed_hi(1)
            split_hi(act, Q_OUT, 1, G_SQ)
            split_hi(act, Q_UP, 0, G_UP)

            transposed_hi(2)

            def up_blocks(q, first=False, last=False):
                for par in range(2):
                    if par == 0:
                        split_hi(act, Q_UP + q, 1, G_UP)
                    elif last:
                        split_hi(act, Q_DN, 0, G_DN[0])
                    else:
                        split_hi(act, Q_UP + q + 1, 0, G_UP)
                    act.wait_ge(tile_used, group_used(Q_UP + q, par))
                    if not (first and par == 0):
                        act.wait_ge(up_h, 2 * q + par)
                    nc.scalar.activation(silu[:], psum[:, 4 * par:4 * par + 2, 0:NU], ACT.Silu).then_inc(up_silu, 1)

            def hidden_hi(g):
                act.wait_ge(ht_ps, g + 1)
                nc.scalar.copy(hT_hi[:, 2 * g:2 * g + 2, :].rearrange("p k s -> p (k s)"), psum[:, g % 4, :]).then_inc(ht_hi, 1)

            up_blocks(0, first=True)
            with act.Fori(1, 3) as q:
                up_blocks(q)
            up_blocks(3, last=True)
            for g in range(6):
                hidden_hi(g)
            split_hi(act, Q_DN, 1, G_DN[1])
            for g in range(6, 11):
                hidden_hi(g)
            split_hi(act, Q_DN + 1, 0, G_DN[0])
            split_hi(act, Q_DN + 1, 1, G_DN[1])
            split_hi(act, Q_IN2, 0, G_SQ)

            transposed_hi(3)
            with act.Fori(0, 2) as q:
                in_block(Q_IN2 + q, 0, proj2, q * 2 * NB, lambda: split_hi(act, Q_IN2 + q, 1, G_SQ))
                in_block(Q_IN2 + q, 1, proj2, q * 2 * NB + NB, lambda: split_hi(act, Q_IN2 + q + 1, 0, G_SQ))
            def queries_keys(half):
                for b in (0, 2):
                    act.wait_ge(bt_ps, 4 + 4 * half + b + 1)
                    k0 = 8 * half + 2 * b
                    nc.scalar.copy(qkT2[:, k0:k0 + 2, :].rearrange("p k s -> p (k s)"), psum[:, 4 + b, :]).then_inc(bt_act, 1)

            in_block(Q_IN2 + 2, 0, proj2, 4 * NB, lambda: split_hi(act, Q_IN2 + 2, 1, G_SQ))
            queries_keys(0)
            in_block(Q_IN2 + 2, 1, proj2, 5 * NB, lambda: split_hi(act, Q_OUT2, 0, G_SQ))
            queries_keys(1)

            act.wait_ge(lam_s, 1)
            nc.scalar.activation(vec[:, 90:92], vec[:, 88:90], ACT.Exp).then_inc(lam_x, 1)

            def map_exps(h):
                p = h % 2
                act.wait_ge(c_mx, h + 1)
                if h >= 2:
                    act.wait_ge(c_a, h - 1)
                for u in range(4):
                    nc.scalar.activation(eP[p][:, u // 2, u % 2, :], psum[:, 2 * p + u // 2, (u % 2) * S:(u % 2 + 1) * S],
                                         ACT.Exp, bias=vec[:, 16 + 4 * p + u:17 + 4 * p + u], scale=CD ** -0.5,
                                         accum_out=vec[:, 48 + 4 * p + u:49 + 4 * p + u]).then_inc(c_e, 1)

            def move_maps(h):
                act.wait_ge(c_tp, h + 1)
                if h >= 2:
                    act.wait_ge(c_av, h - 1)
                nc.scalar.copy(aT[h % 2][:].rearrange("p s t -> p (s t)"), psum[:, 4 + h % 2, :]).then_inc(c_te, 1)

            map_exps(0)
            map_exps(1)
            for h in range(CH):
                move_maps(h)
                if h + 2 < CH:
                    map_exps(h + 2)
                if h == 4:
                    keep_square(sq2, on2, c_av, 4)
            act.wait_ge(c_av, 8)
            nc.scalar.activation(sq2, psum[:, 6:8, :].rearrange("p t (h c) -> p t h c", h=4), ACT.Square).then_inc(r_sq, 1)
            transposed_hi(4)
            split_hi(act, Q_OUT2, 1, G_SQ)
            split_hi(act, q_moe(0), 0, G_UP)

            for b in (0, 2):
                act.wait_ge(t_ps, 20 + b + 1)
                nc.scalar.copy(by_bank(xT_f, b), psum[:, 4 + b, :].rearrange("p (k s) -> p k s", s=P)).then_inc(rx_act, 1)
            nc.scalar.copy(xn[:], x[:]).then_inc(xn_set, 1)
            act.wait_ge(m_d, 1)
            nc.scalar.activation(route[:, 4], route[:, 3], ACT.Exp).then_inc(m_ex, 1)

            def gather_hi(n):
                for b in range(2):
                    act.wait_ge(m_ga, 2 * n + b + 1)
                    nc.scalar.copy(xe_hi[:, 4 * b:4 * b + 4, :].rearrange("p k s -> p (k s)"), psum[:, 4 + b, :]).then_inc(m_ga_hi, 1)

            def keep_map(n, first=False):
                act.wait_ge(m_gt, n + 1)
                if not first:
                    act.wait_ge(m_cur, n)
                nc.scalar.copy(put_next[:], psum[:, 6, 2 * P:4 * P]).then_inc(m_put_r, 1)
                nc.scalar.copy(slot_gate[:, 0:1], psum[:, 6, 0:1]).then_inc(m_put_r, 1)

            def turn_hi(n, g):
                k0, kc, bank, _ = TURNS[g]
                act.wait_ge(m_tp, 6 * n + g + 1)
                nc.scalar.copy(hTe_hi[:, k0:k0 + kc, :].rearrange("p k s -> p (k s)"), psum[:, bank, 0:kc * P]).then_inc(m_thi, 1)

            def block_e(n, b):
                split_hi(act, *up_group(n, b + 1), up_shapes(b + 1))
                act.wait_ge(tile_used, group_used(*up_group(n, b)))
                act.wait_ge(m_h, 8 * n + b + 1)
                nc.scalar.activation(silu_e[:, b % 2, :], psum[:, 2 * (b % 2), 0:NU], ACT.Silu).then_inc(m_silu, 1)

            def expert(n, last):
                q0 = q_moe(n)
                for b in range(1, UB):
                    block_e(n, b)
                    if b == GATHER_AFTER and not last:
                        keep_map(n + 1)
                    if b in TURN_AFTER:
                        turn_hi(n, TURN_AFTER[b])
                if not last:
                    gather_hi(n + 1)
                turn_hi(n, 5)
                split_hi(act, q0 + 4, 1, G_DN[1])
                split_hi(act, q0 + 5, 0, G_DN[0])
                for half in range(2):
                    if half:
                        split_hi(act, q0 + 5, 1, G_DN[1])
                        if not last:
                            split_hi(act, q0 + 6, 0, G_UP)
                    act.wait_ge(tile_used, group_used(q0 + 4 + half, 1))
                    act.wait_ge(m_cur, n + 1)
                    nc.scalar.activation(y_hi[:, half * NB:(half + 1) * NB], psum[:, 2 * half, :], ACT.Copy,
                                         scale=slot_gate[:, 1:2]).then_inc(m_yhi, 1)
                if not last:
                    block_e(n + 1, 0)

            gather_hi(0)
            keep_map(0, first=True)
            block_e(0, 0)
            with act.Fori(0, NE - 1) as n:
                expert(n, False)
            expert(NE - 1, True)
            act.wait_ge(more_set, 1)
            flag = act.value_load(more[0:1, 0:1], min_val=0, max_val=1)
            with act.If(flag):
                with act.Fori(NE, 2 * NE) as n:
                    split_hi(act, q_moe(n), 0, G_UP)
                    gather_hi(n)
                    keep_map(n)
                    block_e(n, 0)
                    expert(n, True)

        @block.vector
        def _(dve):
            n_link = [0]

            def link(ins):
                n_link[0] += 1
                ins.then_inc(dve_link, 1)
                dve.wait_ge(dve_link, n_link[0])

            def transposed_lo(i):
                for b in range(4):
                    dve.wait_ge(t_hi, 4 * i + b + 1)
                    nc.vector.tensor_tensor(by_bank(xT_lo, b), psum[:, 4 + b, :].rearrange("p (k s) -> p k s", s=P),
                                            by_bank(xT_hi, b).bitcast(F32), ALU.subtract).then_inc(t_lo, 1)

            def residual(bank, half, t):
                v = x[:, t, half * NB:(half + 1) * NB]
                link(nc.vector.scalar_tensor_tensor(v, v, ALPHA, psum[:, bank + t, :], ALU.mult, ALU.add))
                link(nc.vector.bn_stats(stat[:, t, half, :], v))

            def mean_var(t):
                nc.vector.bn_aggr(mv[:, t, :], stat[:, t, :, :].rearrange("p a b -> p (a b)")).then_inc(ln_mv, 1)

            def normalize(i, t):
                v = x[:, t, :]
                dve.wait_ge(gain_in, 32 * (i + 1))
                dve.wait_ge(ln_rstd, NT * i + t + 1)
                link(nc.vector.tensor_scalar(v, v, mv[:, t, 0:1], ln_rs[:, t:t + 1], ALU.subtract, ALU.mult))
                link(nc.vector.tensor_tensor(v, v, gains[:, 0, :], ALU.mult))
                nc.vector.tensor_tensor(v, v, gains[:, 1, :], ALU.add).then_inc(ln_done, 1)

            def end_of_stage(i, q, bank, nxt):
                for t in range(NT):
                    if t == 0:
                        dve.wait_ge(rows_done, i + 1)
                    else:
                        dve.wait_ge(tile_used, group_used(q, 1))
                    residual(bank, 1, t)
                    mean_var(t)
                    if t == NT - 1:
                        split_lo(dve, *nxt, js=(0,))
                    normalize(i, t)

            def sum_squares(r, sq):
                dve.wait_ge(r_sq, r + 1)
                nc.vector.tensor_reduce(vec[:, 32:40].rearrange("p (t h) -> p t h", h=4), sq, AX_X, ALU.add).then_inc(r_ms, 1)

            transposed_lo(0)
            split_lo(dve, Q_IN, 0, G_SQ)
            dve.wait_ge(lb_in, 16)
            nc.vector.tensor_tensor(lbs[:, 0, :], lbs[:, 0, :], lbs[:, 0, :], ALU.subtract).then_inc(lb_d, 1)
            dve.wait_ge(lb_e, 1)
            link(nc.vector.reciprocal(lbs[:, 1, :], lbs[:, 0, :]))
            link(nc.vector.tensor_tensor(lbs[:, 1, :], lbs[:, 1, :], lbs[:, 0, :], ALU.mult))
            link(nc.vector.tensor_tensor(lbs[:, 0, :], lbs[:, 1, :], lbs[:, 1, :], ALU.subtract))
            link(nc.vector.tensor_scalar(lbs[:, 1, :], lbs[:, 0, :], -1.0, 1.0, ALU.mult, ALU.add))

            def in_block(q, par, dst, col):
                dve.wait_ge(tile_used, group_used(q, par))
                nc.vector.tensor_copy(dst[:, 1, bass.ds(col, NB)], psum[:, 2 * par + 1, :]).then_inc(in_dve, 1)

            def even_block(b):
                q, par = Q_IN + b // 2, b % 2
                split_lo(dve, *((q, 1) if par == 0 else (q + 1, 0)), G_SQ)
                in_block(q, par, proj, b * NB)

            sBv = sB[:].rearrange("p t (d c) -> p (t d) c", d=2)
            sAv = sA[:].rearrange("p t (d c) -> p (t d) c", d=2)
            lb = lbs[:, 0:1, :].broadcast_to([P, 4, 512])
            one_lb = lbs[:, 1:2, :].broadcast_to([P, 4, 512])
            even_block(0)
            dve.wait_ge(lev_in, 16)
            nc.vector.tensor_copy(lev[:].rearrange("p a b c -> p (a b c)"), levraw[:, 0:2 * (NL + 1) * P]).then_inc(g_lev, 1)
            nc.vector.tensor_copy(masks[:].rearrange("p l t -> p (l t)"), levraw[:, 2 * (NL + 1) * P:]).then_inc(g_lev, 1)
            for b in range(1, 4):
                even_block(b)
            dve.wait_ge(g_sig, 1)
            nc.vector.tensor_tensor(sBv, sBv, one_lb, ALU.mult).then_inc(g_k, 1)
            dve.wait_ge(g_sig, 2)
            link(nc.vector.tensor_tensor(sAv, sAv, one_lb, ALU.mult))
            even_block(4)
            link(nc.vector.tensor_tensor(sAv, sAv, lb, ALU.add))
            nc.vector.tensor_scalar(sAv, sAv, MIN_FORGET, None, ALU.max).then_inc(g_f, 1)
            for b in range(5, 8):
                even_block(b)
            dve.wait_ge(g_hi, 1)
            nc.vector.tensor_tensor(xT_lo[:].rearrange("p k s -> p (k s)"), sA[:].rearrange("p t c -> p (t c)"),
                                    xT_hi[:].rearrange("p k s -> p (k s)").bitcast(F32), ALU.subtract).then_inc(g_lo, 1)
            for b in range(1, 6, 2):
                dve.wait_ge(ht2_ps, b + 1)
                nc.vector.tensor_copy(hT[:, b // 2, 2:4, :].rearrange("p h s -> p (h s)"), psum[:, b, :]).then_inc(ht2_dve, 1)

            def scale_pair(n):
                m, pair = LEVELS[n // 2], n % 2
                dve.wait_ge(e_exp, n + 1)
                if n >= 2:
                    dve.wait_ge(s_ps, n - 1)
                if n == 0:
                    dve.wait_ge(ht2_act, 3)
                    dve.wait_ge(ht2_dve, 3)
                cut = lambda v: v.rearrange("p h (b f m) -> p h b f m", f=2, m=m)
                q_, kf, kb = (cut(hT[:, i, 2 * pair:2 * pair + 2, :]) for i in range(3))
                Ef, Eb = (cut(expE[n % 2][:, :, d, :]) for d in range(2))
                Qn, Kn = (cut(qk2[n % 2][:, i, :, :]) for i in range(2))
                for out_, in_, e, f in ((Qn, q_, Ef, 1), (Qn, q_, Eb, 0), (Kn, kf, Ef, 0), (Kn, kb, Eb, 1)):
                    ins = nc.vector.tensor_tensor(out_[:, :, :, f, :], in_[:, :, :, f, :], e[:, :, :, f, :], ALU.mult)
                ins.then_inc(e_qk, 1)

            def keep_scores(n):
                li, pair = n // 2, n % 2
                dve.wait_ge(s_ps, n + 1)
                src = psum[:, 4 + n % 2, :].rearrange("p (h i c) -> p h i c", h=2, i=2)
                dst = (ATo[:, 2 * pair:2 * pair + 2, :, :] if li == 0 else
                       ATd[:, :, 2 * pair:2 * pair + 2, :].rearrange("p t h c -> p h t c"))
                if li < 2:
                    ins = nc.vector.tensor_copy(dst, src)
                else:
                    dve.wait_ge(s_ev, n - 1)
                    for h in range(2):
                        ins = nc.vector.copy_predicated(dst[:, h, :, :], masks[:, li - 2:li - 1, :].broadcast_to([P, 2, P]), src[:, h, :, :])
                ins.then_inc(s_ev, 1)

            dve.wait_ge(vec_in, 16)
            dve.wait_ge(gate_c, 2)
            for n in range(2 * NL):
                scale_pair(n)
                if n:
                    keep_scores(n - 1)
            for n in range(2 * NL - 1, 2 * NL + 2):
                keep_scores(n)
            for b in (1, 3):
                dve.wait_ge(bt_ps, b + 1)
                nc.vector.tensor_copy(qkT[:, 2 * b:2 * b + 2, :].rearrange("p k s -> p (k s)"), psum[:, b, :]).then_inc(bt_dve, 1)
            dve.wait_ge(band_in, 16)
            for h in range(BH):
                dve.wait_ge(b_s, h + 1)
                if h >= 2:
                    dve.wait_ge(b_tp, h - 1)
                link(nc.vector.scalar_tensor_tensor(zP[h % 2][:].rearrange("p t s -> p (t s)"), psum[:, h % 4, :],
                                                    BD ** -0.5, band[:].rearrange("p t s -> p (t s)"), ALU.mult, ALU.add))
                link(nc.vector.tensor_reduce(vec[:, 2 * h:2 * h + 2], zP[h % 2][:], AX_X, ALU.max))
                nc.vector.tensor_scalar(vec[:, 16 + 2 * h:18 + 2 * h], vec[:, 2 * h:2 * h + 2], -1.0, None,
                                        ALU.mult).then_inc(b_nm, 1)
                if h == 2:
                    sum_squares(0, sq0)
            dve.wait_ge(b_p, 2 * BH)
            link(nc.vector.reciprocal(vec[:, 64:80], vec[:, 48:64]))
            dve.wait_ge(b_av, BH)
            rinv = vec[:, 64:80].rearrange("p (h t) -> p t h", t=NT)
            for t in range(NT):
                ins = nc.vector.tensor_tensor(proj[:, t, 512:1024].rearrange("p (h c) -> p h c", h=BH),
                                              psum[:, 6 + t, :].rearrange("p (h c) -> p h c", h=BH),
                                              rinv[:, t, :, None].broadcast_to([P, BH, BD]), ALU.mult)
                ins.then_inc(mix_done, 1)
            transposed_lo(1)

            def out_projection(i, q, nxt):
                split_lo(dve, q, 1, G_SQ)
                dve.wait_ge(tile_used, group_used(q, 0))
                for t in range(NT):
                    residual(0, 0, t)
                end_of_stage(i, q, 2, nxt)

            out_projection(0, Q_OUT, (Q_UP, 0, G_UP))
            transposed_lo(2)
            split_lo(dve, Q_UP, 0, G_UP, js=(1, 2, 3))

            def up_blocks(q, last=False):
                for par in range(2):
                    if par == 0:
                        split_lo(dve, Q_UP + q, 1, G_UP)
                    elif last:
                        split_lo(dve, Q_DN, 0, G_DN[0])
                    else:
                        split_lo(dve, Q_UP + q + 1, 0, G_UP)
                    b = 2 * q + par
                    dve.wait_ge(up_silu, b + 1)
                    nc.vector.tensor_tensor(h_nat[:, :, bass.ds(b * NU, NU)], silu[:],
                                            psum[:, 4 * par + 2:4 * par + 4, 0:NU], ALU.mult).then_inc(up_h, 1)

            def hidden_lo(g):
                dve.wait_ge(ht_hi, g + 1)
                dst = slice(2 * g, 2 * g + 2)
                nc.vector.tensor_tensor(hT_lo[:, dst, :].rearrange("p k s -> p (k s)"), psum[:, g % 4, :],
                                        hT_hi[:, dst, :].rearrange("p k s -> p (k s)").bitcast(F32),
                                        ALU.subtract).then_inc(ht_lo, 1)

            with dve.Fori(0, 3) as q:
                up_blocks(q)
            up_blocks(3, last=True)
            for g in range(6):
                hidden_lo(g)
            split_lo(dve, Q_DN, 1, G_DN[1])
            for g in range(6, 11):
                hidden_lo(g)
            split_lo(dve, Q_DN + 1, 0, G_DN[0])
            dve.wait_ge(tile_used, group_used(Q_DN, 1))
            for t in range(NT):
                residual(4, 0, t)
            split_lo(dve, Q_DN + 1, 1, G_DN[1])
            end_of_stage(1, Q_DN + 1, 6, (Q_IN2, 0, G_SQ))
            transposed_lo(3)
            split_lo(dve, Q_IN2, 0, G_SQ, js=(1, 2, 3))
            with dve.Fori(0, 2) as q:
                split_lo(dve, Q_IN2 + q, 1, G_SQ)
                in_block(Q_IN2 + q, 0, proj2, q * 2 * NB)
                split_lo(dve, Q_IN2 + q + 1, 0, G_SQ)
                in_block(Q_IN2 + q, 1, proj2, q * 2 * NB + NB)
            dve.wait_ge(lm_in, 16)
            lam4 = lamv[:].rearrange("p (a b) c -> p a b c", b=2)
            link(nc.vector.tensor_tensor(lam4[:, :, 0, :], lam4[:, :, 0, :], lam4[:, :, 1, :], ALU.mult))
            nc.vector.tensor_reduce(vec[:, 88:90], lam4[:, :, 0, :], AX_X, ALU.add).then_inc(lam_s, 1)
            dve.wait_ge(sub_in, 16)
            link(nc.vector.tensor_scalar(sub[:], sub[:], 1.0 - LAMBDA_INIT, None, ALU.mult))
            split_lo(dve, Q_IN2 + 2, 1, G_SQ)
            def queries_keys(half):
                for b in (1, 3):
                    dve.wait_ge(bt_ps, 4 + 4 * half + b + 1)
                    k0 = 8 * half + 2 * b
                    nc.vector.tensor_copy(qkT2[:, k0:k0 + 2, :].rearrange("p k s -> p (k s)"), psum[:, 4 + b, :]).then_inc(bt_dve, 1)

            in_block(Q_IN2 + 2, 0, proj2, 4 * NB)
            queries_keys(0)
            split_lo(dve, Q_OUT2, 0, G_SQ)
            in_block(Q_IN2 + 2, 1, proj2, 5 * NB)
            queries_keys(1)
            dve.wait_ge(lam_x, 1)
            link(nc.vector.tensor_tensor(vec[:, 92:93], vec[:, 91:92], vec[:, 90:91], ALU.subtract))
            link(nc.vector.tensor_scalar(vec[:, 92:93], vec[:, 92:93], -LAMBDA_INIT, None, ALU.add))

            def map_max(h):
                p = h % 2
                dve.wait_ge(c_s, h + 1)
                link(nc.vector.tensor_reduce(vec[:, 4 * p:4 * p + 4],
                                             psum[:, 2 * p:2 * p + 2, :].rearrange("p m (t s) -> p (m t) s", t=2), AX_X, ALU.max))
                nc.vector.tensor_scalar(vec[:, 16 + 4 * p:20 + 4 * p], vec[:, 4 * p:4 * p + 4], -(CD ** -0.5), None,
                                        ALU.mult).then_inc(c_mx, 1)

            def combine(h):
                p = h % 2
                dve.wait_ge(c_e, 4 * h + 4)
                if h >= 2:
                    dve.wait_ge(c_tp, h - 1)
                link(nc.vector.reciprocal(vec[:, 64 + 4 * p:68 + 4 * p], vec[:, 48 + 4 * p:52 + 4 * p]))
                link(nc.vector.tensor_scalar(vec[:, 80 + 2 * p:82 + 2 * p], vec[:, 66 + 4 * p:68 + 4 * p], vec[:, 92:93], None, ALU.mult))
                for t in range(NT):
                    link(nc.vector.tensor_scalar(eP[p][:, 1, t, :], eP[p][:, 1, t, :], vec[:, 80 + 2 * p + t:81 + 2 * p + t], None, ALU.mult))
                    ins = nc.vector.scalar_tensor_tensor(aP[p][:, t, :], eP[p][:, 0, t, :], vec[:, 64 + 4 * p + t:65 + 4 * p + t],
                                                         eP[p][:, 1, t, :], ALU.mult, ALU.add)
                ins.then_inc(c_a, 1)

            map_max(0)
            map_max(1)
            for h in range(CH):
                combine(h)
                if h + 2 < CH:
                    map_max(h + 2)
                if h == 5:
                    sum_squares(1, sq2)
            dve.wait_ge(heads_out, 2)
            sum_squares(2, sq2)
            dve.wait_ge(r_rs, 1)
            rs = vec[:, 40:48].rearrange("p (t h) -> p t h", h=4)[:, :, :, None].broadcast_to([P, NT, 4, 128])
            link(nc.vector.tensor_tensor(on2, psum[:, 6:8, :].rearrange("p t (h c) -> p t h c", h=4), rs, ALU.mult))
            nc.vector.tensor_tensor(proj2[:, :, 512:1024].rearrange("p t (h c) -> p t h c", h=4), on2,
                                    sub[:, None, None, :].broadcast_to([P, NT, 4, 128]), ALU.mult).then_inc(mix_done, 1)
            transposed_lo(4)
            out_projection(2, Q_OUT2, (q_moe(0), 0, G_UP))

            LG, GTR, TOP, DIF, EXS, SEL, GATE, POS = range(8)
            for b in (1, 3):
                dve.wait_ge(t_ps, 20 + b + 1)
                nc.vector.tensor_copy(by_bank(xT_f, b), psum[:, 4 + b, :].rearrange("p (k s) -> p k s", s=P)).then_inc(rx_dve, 1)
            split_lo(dve, q_moe(0), 0, G_UP, js=(1, 2, 3))
            dve.wait_ge(m_lg, 1)
            link(nc.vector.tensor_copy(route[:, LG], psum[:, 0, 0:NT * NE].rearrange("p (t e) -> p t e", e=NE)))
            dve.wait_ge(bf_in, 16)
            for t in range(NT):
                other = route[:, LG, t, None, :].broadcast_to([P, NE, NE])
                mine = route[:, LG, t, :, None].broadcast_to([P, NE, NE])
                nc.vector.tensor_tensor(cmp[:, 0, t], other, mine, ALU.is_gt)
                link(nc.vector.tensor_tensor(cmp[:, 1, t], other, mine, ALU.is_equal))
                link(nc.vector.tensor_tensor(cmp[:, 1, t], cmp[:, 1, t], before[:], ALU.mult))
                link(nc.vector.tensor_tensor(cmp[:, 0, t], cmp[:, 0, t], cmp[:, 1, t], ALU.add))
            flat = lambda i: route[:, i].rearrange("p t e -> p (t e)")
            link(nc.vector.tensor_reduce(flat(GTR), cmp[:, 0].rearrange("p t a b -> p (t a) b"), AX_X, ALU.add))
            nc.vector.tensor_scalar(flat(SEL), flat(GTR), 2.0, None, ALU.is_lt).then_inc(m_sel, 1)
            link(nc.vector.tensor_reduce(route[:, TOP, :, 0], route[:, LG], AX_X, ALU.max))
            nc.vector.tensor_tensor(route[:, DIF], route[:, LG], route[:, TOP, :, 0:1].broadcast_to([P, NT, NE]),
                                    ALU.subtract).then_inc(m_d, 1)
            dve.wait_ge(m_ex, 1)
            dve.wait_ge(m_sel, 1)
            link(nc.vector.tensor_tensor(route[:, EXS], route[:, EXS], route[:, SEL], ALU.mult))
            link(nc.vector.tensor_reduce(route[:, TOP, :, 1], route[:, EXS], AX_X, ALU.add))
            link(nc.vector.reciprocal(route[:, TOP, :, 2], route[:, TOP, :, 1]))
            link(nc.vector.tensor_tensor(route[:, GATE], route[:, EXS], route[:, TOP, :, 2:3].broadcast_to([P, NT, NE]), ALU.mult))
            dve.wait_ge(m_pos, 1)
            link(nc.vector.tensor_scalar(flat(POS), psum[:, 1, 0:NT * NE], 1.0, None, ALU.add))
            link(nc.vector.tensor_tensor(flat(POS), flat(POS), flat(SEL), ALU.mult))
            for r in range(2):
                link(nc.vector.tensor_scalar(seat[:, :, r * NE:(r + 1) * NE], route[:, POS], -1.0 - r * P, None, ALU.add))

            def pick_tokens(n, e):
                for t in range(NT):
                    nc.vector.tensor_scalar(pick[:, t, :], slots, seat[:, t, bass.ds(n, 1)], None, ALU.is_equal)
                nc.vector.tensor_copy(gate_col[:], route[:, GATE, :, bass.ds(e, 1)].rearrange("p t e -> p (t e)")).then_inc(m_pick, 1)

            def gather_lo(n):
                for b in range(2):
                    dve.wait_ge(m_ga_hi, 2 * n + b + 1)
                    dst = slice(4 * b, 4 * b + 4)
                    nc.vector.tensor_tensor(xe_lo[:, dst, :].rearrange("p k s -> p (k s)"), psum[:, 4 + b, :],
                                            xe_hi[:, dst, :].rearrange("p k s -> p (k s)").bitcast(F32),
                                            ALU.subtract).then_inc(m_ga_lo, 1)

            def make_current(n):
                dve.wait_ge(m_put_r, 2 * n + 2)
                nc.vector.tensor_copy(put[:], put_next[:].bitcast(F32))
                nc.vector.tensor_copy(slot_gate[:, 1:2], slot_gate[:, 0:1]).then_inc(m_cur, 1)

            def turn_lo(n, g):
                k0, kc, bank, _ = TURNS[g]
                dve.wait_ge(m_thi, 6 * n + g + 1)
                nc.vector.tensor_tensor(hTe_lo[:, k0:k0 + kc, :].rearrange("p k s -> p (k s)"), psum[:, bank, 0:kc * P],
                                        hTe_hi[:, k0:k0 + kc, :].rearrange("p k s -> p (k s)").bitcast(F32),
                                        ALU.subtract).then_inc(m_tlo, 1)

            def block_e(n, b):
                split_lo(dve, *up_group(n, b + 1), up_shapes(b + 1))
                dve.wait_ge(m_silu, 8 * n + b + 1)
                nc.vector.tensor_tensor(h_e[:, b * NU:(b + 1) * NU], silu_e[:, b % 2, :], psum[:, 2 * (b % 2) + 1, 0:NU],
                                        ALU.mult).then_inc(m_h, 1)

            def add_half(n, half):
                cols = slice(half * NB, (half + 1) * NB)
                dve.wait_ge(m_sc, 2 * n + half + 1)
                nc.vector.tensor_tensor(x[:, :, cols], x[:, :, cols], psum[:, 4 + 2 * half:6 + 2 * half, :],
                                        ALU.add).then_inc(m_acc, 1)

            def expert(n, e, last):
                q0 = q_moe(n)
                if not last:
                    dve.wait_ge(m_gt, n + 1)
                    pick_tokens(n + 1, e + 1)
                for b in range(1, UB):
                    block_e(n, b)
                    if b in TURN_AFTER:
                        turn_lo(n, TURN_AFTER[b])
                if not last:
                    gather_lo(n + 1)
                turn_lo(n, 5)
                split_lo(dve, q0 + 4, 1, G_DN[1])
                split_lo(dve, q0 + 5, 0, G_DN[0])
                for half in range(2):
                    if half:
                        split_lo(dve, q0 + 5, 1, G_DN[1])
                        add_half(n, 0)
                        if not last:
                            split_lo(dve, q0 + 6, 0, G_UP)
                    cols = slice(half * NB, (half + 1) * NB)
                    dve.wait_ge(m_yhi, 2 * n + half + 1)
                    nc.vector.scalar_tensor_tensor(y_lo[:, cols], psum[:, 2 * half, :], slot_gate[:, 1:2],
                                                   y_hi[:, cols].bitcast(F32), ALU.mult, ALU.subtract).then_inc(m_ylo, 1)
                if not last:
                    block_e(n + 1, 0)
                add_half(n, 1)
                if not last:
                    make_current(n + 1)

            pick_tokens(0, 0)
            link(nc.vector.tensor_reduce(route[:, TOP, 0, 3:4], psum[:, 2, 0:NE], AX_X, ALU.max))
            nc.vector.tensor_scalar(more[:], route[:, TOP, 0, 3:4], float(P), None, ALU.is_gt).then_inc(more_set, 1)
            gather_lo(0)
            make_current(0)
            nc.vector.memset(mv[:, 0, :], 0.0).then_inc(m_h, 1)
            nc.vector.memset(mv[:, 1, :], 0.0).then_inc(m_h, 1)
            nc.vector.memset(stat[:], 0.0).then_inc(m_acc, 1)
            dve.wait_ge(xn_set, 1)
            link(nc.vector.tensor_scalar(x[:], x[:], ALPHA, None, ALU.mult))
            block_e(0, 0)
            with dve.Fori(0, NE - 1) as n:
                expert(n, n, False)
            expert(NE - 1, NE - 1, True)
            dve.wait_ge(m_acc, 2 * NE + 1)
            flag = dve.value_load(more[0:1, 0:1], min_val=0, max_val=1)
            with dve.If(flag):
                with dve.Fori(0, NE) as e:
                    split_lo(dve, q_moe(e + NE), 0, G_UP)
                    dve.wait_ge(m_gt, e + NE)
                    pick_tokens(e + NE, e)
                    gather_lo(e + NE)
                    make_current(e + NE)
                    block_e(e + NE, 0)
                    expert(e + NE, e, True)
                dve.wait_ge(m_acc, 4 * NE + 1)
            for t in range(NT):
                for half in range(2):
                    link(nc.vector.bn_stats(stat[:, t, half, :], x[:, t, half * NB:(half + 1) * NB]))
                mean_var(t)
            for t in range(NT):
                normalize(3, t)

        @block.tensor
        def _(pe):
            def transpose_chunks(src, ts=range(NT), norm=None):
                for t in ts:
                    if norm is not None:
                        pe.wait_ge(ln_done, NT * norm + t + 1)
                    for kb in range(2):
                        for kk in range(4):
                            ins = nc.tensor.transpose(psum[:, 4 + 2 * t + kb, kk * P:(kk + 1) * P], src(4 * kb + kk, t), ident)
                        ins.then_inc(t_ps, 1)

            def last_group(q, shapes, k0s, lhs, bank, last_k):
                hi, lo = lhs
                for t in range(NT):
                    for j, (kc, n) in enumerate(shapes):
                        if t == 0:
                            pe.wait_ge(lo_done, 2 * GT * q + GT + j + 1)
                        for kk in range(kc):
                            k = k0s[j] + kk
                            w_h = whi[j][:, kk * n:(kk + 1) * n]
                            w_l = wlo[j][:, kk * n:(kk + 1) * n]
                            ps = psum[:, bank + t, :]
                            nc.tensor.matmul(ps, hi[:, k, t * P:(t + 1) * P], w_h, start=(k == 0), stop=False)
                            nc.tensor.matmul(ps, hi[:, k, t * P:(t + 1) * P], w_l, start=False, stop=False)
                            ins = nc.tensor.matmul(ps, lo[:, k, t * P:(t + 1) * P], w_h, start=False, stop=(k == last_k))
                        if t == NT - 1:
                            ins.then_inc(tile_used, 1)
                    if t == 0:
                        ins.then_inc(rows_done, 1)

            def x_chunk(k, t):
                return x[:, t, k * P:(k + 1) * P]

            def square_block(q, par, bank):
                for j in range(GT):
                    tile_products(pe, q, par, j, 2, NB, 2 * j, (xT_hi, xT_lo),
                                  [(psum[:, bank + t, :], t * P) for t in range(NT)], 0, KD - 1)

            pe.wait_ge(x_in, 16)
            pe.wait_ge(const_in, 16)
            transpose_chunks(x_chunk)
            pe.wait_ge(t_lo, 4)
            for par in range(2):
                square_block(Q_IN, par, 2 * par)
            with pe.Fori(1, 4) as q:
                for par in range(2):
                    pe.wait_ge(in_act, 2 * q + par - 1)
                    pe.wait_ge(in_dve, 2 * q + par - 1)
                    square_block(Q_IN + q, par, 2 * par)

            pe.wait_ge(in_act, 8)
            pe.wait_ge(in_dve, 8)
            for i in range(3):
                if i == 1:
                    pe.wait_ge(g_k, 1)
                for hp in range(2):
                    for hh in range(2):
                        for t in range(NT):
                            h = 2 * hp + hh
                            src = proj[:, t, h * AD:(h + 1) * AD] if i == 0 else sB[:, t, (i - 1) * 512 + h * AD:(i - 1) * 512 + (h + 1) * AD]
                            ins = nc.tensor.transpose(psum[:, 2 * i + hp, hh * S + t * P:hh * S + t * P + P], src, ident)
                    ins.then_inc(ht2_ps, 1)

            lf_hi = xT_hi[:].rearrange("p k s -> p (k s)").rearrange("p (t d c) -> p t d c", t=2, d=2)
            lf_lo = xT_lo[:].rearrange("p k s -> p (k s)").rearrange("p (t d c) -> p t d c", t=2, d=2)

            def exponents(n):
                li, pair = n // 2, n % 2
                if n == 0:
                    pe.wait_ge(g_lo, 1)
                    pe.wait_ge(g_lev, 1)
                    pe.wait_ge(ht2_act, 3)
                    pe.wait_ge(ht2_dve, 3)
                if n >= 2:
                    pe.wait_ge(e_exp, n - 1)
                for hh in range(2):
                    h = 2 * pair + hh
                    for d in range(2):
                        for t in range(NT):
                            dst = psum[:, 2 * (n % 2) + hh, d * S + t * P:d * S + t * P + P]
                            m = lev[:, d, t if li == 0 else li + 1, :]
                            nc.tensor.matmul(dst, lf_hi[:, t, d, h * AD:(h + 1) * AD], m, start=True, stop=False)
                            ins = nc.tensor.matmul(dst, lf_lo[:, t, d, h * AD:(h + 1) * AD], m, start=False, stop=True)
                ins.then_inc(e_ps, 1)

            def scores(n):
                li, pair = n // 2, n % 2
                if n >= 2:
                    pe.wait_ge(s_ev, n - 1)
                if n < 2 * NL:
                    pe.wait_ge(e_qk, n + 1)
                for hh in range(2):
                    h = 2 * pair + hh
                    for i in range(2):
                        dst = psum[:, 4 + n % 2, hh * S + i * P:hh * S + i * P + P]
                        ts, tt = (i, 1 - i) if li == 0 else (i, i)
                        if n < 2 * NL:
                            q_, k_ = (qk2[n % 2][:, w, hh, :] for w in range(2))
                            ins = nc.tensor.matmul(dst, k_[:, ts * P:(ts + 1) * P], q_[:, tt * P:(tt + 1) * P], start=True, stop=True)
                        else:
                            q_ = hT[:, 0, h, tt * P:(tt + 1) * P]
                            nc.tensor.matmul(dst, hT[:, 1, h, ts * P:(ts + 1) * P], q_, start=True, stop=False)
                            ins = nc.tensor.matmul(dst, hT[:, 2, h, ts * P:(ts + 1) * P], q_, start=False, stop=True)
                ins.then_inc(s_ps, 1)

            exponents(0)
            for n in range(2 * NL + 2):
                if n + 1 < 2 * NL:
                    exponents(n + 1)
                scores(n)
            pe.wait_ge(s_ev, 2 * NL + 2)
            for t in range(NT):
                for h in range(AH):
                    dst = psum[:, 6 + t, h * AD:(h + 1) * AD]
                    v = [proj[:, tt, VA + h * AD:VA + (h + 1) * AD] for tt in range(NT)]
                    nc.tensor.matmul(dst, ATd[:, t, h, :], v[t], start=True, stop=False)
                    ins = nc.tensor.matmul(dst, ATo[:, h, 1 - t, :], v[1 - t], start=False, stop=True)
            ins.then_inc(o_ps, 1)

            pe.wait_ge(rope_done, 8)
            pe.wait_ge(e_exp, 2 * NL)
            for b in range(4):
                for kk in range(2):
                    for t in range(NT):
                        col = QB + (2 * b + kk) * P
                        ins = nc.tensor.transpose(psum[:, b, kk * S + t * P:kk * S + t * P + P], proj[:, t, col:col + P], ident)
                ins.then_inc(bt_ps, 1)

            def b_scores(h):
                if h == 0:
                    pe.wait_ge(bt_act, 2)
                    pe.wait_ge(bt_dve, 2)
                if h >= 4:
                    pe.wait_ge(b_nm, h - 3)
                rows = slice(BD * (h % 2), BD * (h % 2) + BD)
                for t in range(NT):
                    ins = nc.tensor.matmul(psum[:, h % 4, t * S:(t + 1) * S], qkT[rows, h // 2, t * P:(t + 1) * P],
                                           qkT[rows, 4 + h // 2, :], start=True, stop=True)
                ins.then_inc(b_s, 1)

            def turn(src, h, done):
                for sc in range(NT):
                    for t in range(NT):
                        ins = nc.tensor.transpose(psum[:, 4 + h % 2, sc * S + t * P:sc * S + t * P + P],
                                                  src[:, t, sc * P:(sc + 1) * P], ident)
                ins.then_inc(done, 1)

            def b_turn(h):
                pe.wait_ge(b_p, 2 * h + 2)
                if h >= 2:
                    pe.wait_ge(b_te, h - 1)
                turn(zP[h % 2], h, b_tp)

            def b_values(h):
                pe.wait_ge(b_te, h + 1)
                if h == 0:
                    pe.wait_ge(on_kept, 1)
                for t in range(NT):
                    for sc in range(NT):
                        ins = nc.tensor.matmul(psum[:, 6 + t, h * BD:(h + 1) * BD], pT[h % 2][:, sc, t * P:(t + 1) * P],
                                               proj[:, sc, VB + h * BD:VB + (h + 1) * BD], start=(sc == 0), stop=(sc == NT - 1))
                ins.then_inc(b_av, 1)

            for h in range(3):
                b_scores(h)
            for h in range(BH):
                if h + 3 < BH:
                    b_scores(h + 3)
                b_turn(h)
                if h:
                    b_values(h - 1)
            b_values(BH - 1)
            pe.wait_ge(heads_out, 1)
            pe.wait_ge(mix_done, 2)
            transpose_chunks(lambda k, t: proj[:, t, k * P:(k + 1) * P])
            pe.wait_ge(t_lo, 8)
            square_block(Q_OUT, 0, 0)
            last_group(Q_OUT, G_SQ, [2 * j for j in range(GT)], (xT_hi, xT_lo), 2, KD - 1)

            transpose_chunks(x_chunk, norm=0)
            pe.wait_ge(t_lo, 12)

            def up_block(q, par, wait):
                if wait:
                    pe.wait_ge(up_h, 2 * q + par - 1)
                for j in range(GT):
                    tile_products(pe, Q_UP + q, par, j, 4, NU, 4 * (j % 2), (xT_hi, xT_lo),
                                  [(psum[:, 4 * par + 2 * (j // 2) + t, 0:NU], t * P) for t in range(NT)], 0, KD - 1)

            for par in range(2):
                up_block(0, par, False)
            with pe.Fori(1, 4) as q:
                for par in range(2):
                    up_block(q, par, True)
            pe.wait_ge(up_h, 8)

            n_turned = [0]

            def turn_hidden(upto):
                while n_turned[0] < min(upto, KF // 2):
                    g = n_turned[0]
                    n_turned[0] += 1
                    if g >= 4:
                        pe.wait_ge(ht_lo, g - 3)
                    for kk in range(2):
                        for t in range(NT):
                            k = 2 * g + kk
                            ins = nc.tensor.transpose(psum[:, g % 4, kk * S + t * P:kk * S + t * P + P],
                                                      h_nat[:, t, k * P:(k + 1) * P], ident)
                    ins.then_inc(ht_ps, 1)

            for half in range(2):
                for part in range(2):
                    if half and part:
                        last_group(Q_DN + 1, G_DN[1], DN_K0[1], (hT_hi, hT_lo), 6, KF - 1)
                        continue
                    for j, (kc, n) in enumerate(G_DN[part]):
                        k0 = DN_K0[part][j]
                        if half == 0:
                            need = (k0 + kc + 1) // 2
                            turn_hidden(need + 3)
                            pe.wait_ge(ht_lo, need)
                        tile_products(pe, Q_DN + half, part, j, kc, n, k0, (hT_hi, hT_lo),
                                      [(psum[:, 4 + 2 * half + t, :], t * P) for t in range(NT)], 0, KF - 1)

            transpose_chunks(x_chunk, norm=1)
            pe.wait_ge(t_lo, 16)
            for par in range(2):
                square_block(Q_IN2, par, 2 * par)
            def queries_keys(half):
                for b in range(4):
                    if half:
                        pe.wait_ge(bt_dve if b % 2 else bt_act, 3 + b // 2)
                    for kk in range(2):
                        for t in range(NT):
                            col = half * D + (2 * b + kk) * P
                            ins = nc.tensor.transpose(psum[:, 4 + b, kk * S + t * P:kk * S + t * P + P], proj2[:, t, col:col + P], ident)
                    ins.then_inc(bt_ps, 1)

            for b in range(2, 6):
                pe.wait_ge(in_act, 8 + b - 1)
                pe.wait_ge(in_dve, 8 + b - 1)
                square_block(Q_IN2 + b // 2, b % 2, 2 * (b % 2))
                if b == 4:
                    pe.wait_ge(rope2_pool, 4)
                    queries_keys(0)
            pe.wait_ge(rope2_pool, 8)
            queries_keys(1)
            pe.wait_ge(in_act, 14)
            pe.wait_ge(in_dve, 14)

            def map_scores(h):
                if h >= 2:
                    pe.wait_ge(c_e, 4 * (h - 1))
                if h % 2 == 0:
                    pe.wait_ge(bt_dve if h % 4 else bt_act, 5 + h // 4)
                for t in range(NT):
                    for m in range(2):
                        rows = slice(CD * m, CD * m + CD)
                        ins = nc.tensor.matmul(psum[:, 2 * (h % 2) + m, t * S:(t + 1) * S], qkT2[rows, h, t * P:(t + 1) * P],
                                               qkT2[rows, 8 + h, :], start=True, stop=True)
                ins.then_inc(c_s, 1)

            def map_turn(h):
                pe.wait_ge(c_a, h + 1)
                if h >= 2:
                    pe.wait_ge(c_te, h - 1)
                turn(aP[h % 2], h, c_tp)

            def map_values(h):
                pe.wait_ge(c_te, h + 1)
                if h == 4:
                    pe.wait_ge(on_kept, 2)
                for t in range(NT):
                    for sc in range(NT):
                        ins = nc.tensor.matmul(psum[:, 6 + t, (h % 4) * 128:(h % 4 + 1) * 128], aT[h % 2][:, sc, t * P:(t + 1) * P],
                                               proj2[:, sc, 2 * D + h * 128:2 * D + (h + 1) * 128], start=(sc == 0), stop=(sc == NT - 1))
                ins.then_inc(c_av, 1)

            map_scores(0)
            map_scores(1)
            for h in range(CH):
                if h + 2 < CH:
                    map_scores(h + 2)
                map_turn(h)
                if h:
                    map_values(h - 1)
            map_values(CH - 1)
            pe.wait_ge(heads_out, 2)
            pe.wait_ge(mix_done, 3)
            transpose_chunks(lambda k, t: proj2[:, t, k * P:(k + 1) * P])
            pe.wait_ge(t_lo, 20)
            square_block(Q_OUT2, 0, 0)
            last_group(Q_OUT2, G_SQ, [2 * j for j in range(GT)], (xT_hi, xT_lo), 2, KD - 1)

            pe.wait_ge(rt_in, 16)
            for t in range(NT):
                transpose_chunks(x_chunk, ts=(t,), norm=2)
                pe.wait_ge(rx_act, t + 1)
                pe.wait_ge(rx_dve, t + 1)
                for k in range(KD):
                    ins = nc.tensor.matmul(psum[:, 0, t * NE:(t + 1) * NE], xT_f[:, k, t * P:(t + 1) * P], router[:, k, :],
                                           start=(k == 0), stop=(k == KD - 1))
            ins.then_inc(m_lg, 1)
            SEL = 5
            pe.wait_ge(m_sel, 1)
            pe.wait_ge(ones_set, 1)
            nc.tensor.matmul(psum[:, 1, 0:NE], earlier, route[:, SEL, 0, :], start=True, stop=True)
            nc.tensor.matmul(psum[:, 1, NE:2 * NE], ones[:], route[:, SEL, 0, :], start=True, stop=False)
            nc.tensor.matmul(psum[:, 1, NE:2 * NE], earlier, route[:, SEL, 1, :], start=False, stop=True)
            for t in range(NT):
                ins = nc.tensor.matmul(psum[:, 2, 0:NE], ones[:], route[:, SEL, t, :], start=(t == 0), stop=(t == NT - 1))
            ins.then_inc(m_pos, 1)

            def gather(n):
                pe.wait_ge(m_pick, n + 1)
                for k in range(KD):
                    for t in range(NT):
                        ins = nc.tensor.matmul(psum[:, 4 + k // 4, (k % 4) * P:(k % 4 + 1) * P],
                                               xn[:, t, k * P:(k + 1) * P], pick[:, t, :], start=(t == 0), stop=(t == NT - 1))
                    if k % 4 == 3:
                        ins.then_inc(m_ga, 1)
                for t in range(NT):
                    ins = nc.tensor.transpose(psum[:, 6, 2 * P + t * P:3 * P + t * P], pick[:, t, :], ident)
                for t in range(NT):
                    ins = nc.tensor.matmul(psum[:, 6, 0:1], pick[:, t, :], gate_col[:, t:t + 1],
                                           start=(t == 0), stop=(t == NT - 1))
                ins.then_inc(m_gt, 1)

            def turn_hidden_e(n, g):
                k0, kc, bank, _ = TURNS[g]
                for k in range(kc):
                    ins = nc.tensor.transpose(psum[:, bank, k * P:(k + 1) * P], h_e[:, (k0 + k) * P:(k0 + k + 1) * P], ident)
                ins.then_inc(m_tp, 1)

            def scatter(n, half):
                pe.wait_ge(m_ylo, 2 * n + half + 1)
                pe.wait_ge(m_cur, n + 1)
                for t in range(NT):
                    dst = psum[:, 4 + 2 * half + t, :]
                    cols = slice(half * NB, (half + 1) * NB)
                    nc.tensor.matmul(dst, put[:, t * P:(t + 1) * P], y_hi[:, cols], start=True, stop=False)
                    ins = nc.tensor.matmul(dst, put[:, t * P:(t + 1) * P], y_lo[:, cols], start=False, stop=True)
                ins.then_inc(m_sc, 1)

            def block_e(n, b):
                pe.wait_ge(m_h, 8 * n + b + 1)
                for j in range(GT):
                    tile_products(pe, *up_group(n, b), j, 4, NU, 4 * (j % 2), (xe_hi, xe_lo),
                                  [(psum[:, 2 * (b % 2) + j // 2, 0:NU], 0)], 0, KD - 1)

            def first_block(n):
                pe.wait_ge(m_ga_hi, 2 * n + 2)
                pe.wait_ge(m_ga_lo, 2 * n + 2)
                block_e(n, 0)

            def expert(n, last):
                q0 = q_moe(n)
                for b in range(1, UB):
                    block_e(n, b)
                    if b == GATHER_AFTER:
                        pe.wait_ge(m_acc, 2 * n + 1)
                        if not last:
                            gather(n + 1)
                    if b in TURN_AFTER:
                        g = TURN_AFTER[b]
                        pe.wait_ge(m_h, 8 * n + b + 2)
                        if g == 0 and not last:
                            pe.wait_ge(m_put_r, 2 * n + 4)
                        if g >= 2:
                            pe.wait_ge(m_tlo, 6 * n + g - 1)
                        turn_hidden_e(n, g)
                for half in range(2):
                    for part in range(2):
                        if half and part:
                            if not last:
                                pe.wait_ge(m_ga_lo, 2 * n + 4)
                            scatter(n, 0)
                        for j, (kc, w) in enumerate(G_DN[part]):
                            k0 = DN_K0[part][j]
                            if not half:
                                done = [g for g, (c0, _, _, _) in enumerate(TURNS) if c0 < k0 + kc]
                                pe.wait_ge(m_tlo, 6 * n + len(done))
                            tile_products(pe, q0 + 4 + half, part, j, kc, w, k0, (hTe_hi, hTe_lo),
                                          [(psum[:, 2 * half, :], 0)], 0, KF - 1)
                            if not half and not part and j == 0:
                                pe.wait_ge(m_h, 8 * n + 10)
                                turn_hidden_e(n, 5)
                if not last:
                    first_block(n + 1)
                scatter(n, 1)

            pe.wait_ge(xn_set, 1)
            gather(0)
            pe.wait_ge(more_set, 1)
            first_block(0)
            with pe.Fori(0, NE - 1) as n:
                expert(n, False)
            expert(NE - 1, True)
            flag = pe.value_load(more[0:1, 0:1], min_val=0, max_val=1)
            with pe.If(flag):
                with pe.Fori(NE, 2 * NE) as n:
                    pe.wait_ge(m_acc, 2 * n + 1)
                    gather(n)
                    first_block(n)
                    expert(n, True)


_INPUTS = ["x", "ev_w_in", "ev_lb_logits", "ev_hgrn_norm", "ev_w_out", "ev_ln1_g", "ev_ln1_b", "ev_w1", "ev_w3", "ev_w2",
           "ev_ln2_g", "ev_ln2_b", "od_w_in", "od_lambda", "od_subln", "od_w_out", "od_ln1_g", "od_ln1_b", "od_router",
           "od_w1", "od_w3", "od_w2", "od_ln2_g", "od_ln2_b"]


def kernel(**inputs):
    import concourse.bacc as bacc
    from concourse.bass_utils import run_bass_kernel_spmd as run

    nc = bacc.Bacc("TRN2", target_bir_lowering=False, num_devices=1)
    arrays, ins, consts = {}, {}, {}
    for name in _INPUTS:
        v = np.ascontiguousarray(inputs[name])
        arrays[f"in_{name}"] = v
        ins[name] = nc.dram_tensor(f"in_{name}", v.shape, mybir.dt.from_np(v.dtype), kind="ExternalInput").ap()
    for name, v in constants().items():
        arrays[f"const_{name}"] = v
        consts[name] = nc.dram_tensor(f"const_{name}", v.shape, mybir.dt.from_np(v.dtype), kind="ExternalInput").ap()
    out = nc.dram_tensor("out", (1, S, D), F32, kind="ExternalOutput").ap()
    trunk(nc, ins, consts, out)
    return run(nc, [arrays], core_ids=[0]).results[0]["out"]
```

```python
import math
from contextlib import ExitStack

import numpy as np
import concourse.bass as bass
from concourse import mybir

ALU = mybir.AluOpType
ACT = mybir.ActivationFunctionType
AX_X = mybir.AxisListType.X
F32 = mybir.dt.float32
F32R = mybir.dt.float32r
U8 = mybir.dt.uint8
I32 = mybir.dt.int32

P = 128
S, D = 256, 1024
NT = S // P
KD = D // P
AH, AD = 4, 128
BH, BD = 8, 64
CH, CD = 8, 64
FF = 2816
KF = FF // P
NE = 8
EVEN_IN, ODD_IN = 4096, 3072
QA, ZF, ZB, VA, GA, QB, KB, VB = (512 * i for i in range(8))
DEPTH = 2
ALPHA = (2 * DEPTH) ** 0.25
LAMBDA_INIT = 0.8 - 0.6 * math.exp(-0.3 * 1)
EPS = 1e-5
MIN_FORGET = 1e-30
LEVELS = (128, 64, 32, 16, 8, 4, 2, 1)
NL = len(LEVELS)
LEV_SLOTS = NL + 2

NB = 512
NU = 352
UB = FF // NU
TILE = 1536
GT = 4
RAW = 2 * GT
G_SQ = [(2, NB)] * GT
G_UP = [(4, NU)] * GT
G_DN = [[(3, NB)] * 4, [(3, NB), (3, NB), (2, NB), (2, NB)]]
DN_K0 = [[0, 3, 6, 9], [12, 15, 18, 20]]


def level_matrices():
    u, t = np.arange(P)[:, None], np.arange(P)[None, :]
    out = np.zeros((P, 2, LEV_SLOTS, P), np.float32)
    out[:, 0, 0], out[:, 1, 0] = u > t, u >= t
    out[:, 0, 2], out[:, 1, 2] = u <= t, u < t
    for m in LEVELS[1:]:
        mid = t // (2 * m) * 2 * m + m
        right = t >= mid
        fw = np.where(right, (u >= mid) & (u <= t), (u > t) & (u < mid))
        bw = np.where(right, (u >= mid) & (u < t), (u >= t) & (u < mid))
        for slot in ((1, 3) if m == 64 else (2 + LEVELS.index(m),)):
            out[:, 0, slot], out[:, 1, slot] = fw, bw
    return out.reshape(P, -1)


def level_masks():
    s, t = np.arange(P)[:, None], np.arange(P)[None, :]
    ms = [(s // (2 * m) == t // (2 * m)) & (s // m != t // m) for m in LEVELS[2:]] + [s == t]
    return np.stack(ms, 1).astype(np.float32).reshape(P, -1)


def constants():
    pos = np.arange(S)
    diff = pos[:, None] - pos[None, :]
    times = (np.abs(diff) <= 64).astype(np.int32) + (diff % 4 == 0) + (diff % 16 == 0)
    bias = np.where(times > 0, np.log(np.maximum(times, 1).astype(np.float32)), -1e30).astype(np.float32)
    inv = np.float32(10000.0) ** (-np.arange(0, BD, 2, dtype=np.float32) / np.float32(BD))
    ang = pos.astype(np.float32)[:, None] * inv.astype(np.float32)[None, :]
    rope = np.concatenate([np.cos(ang), np.sin(ang)], 1).astype(np.float32)
    a = np.arange(P)
    e = np.arange(NE)
    small = np.zeros((P, 3, P), np.float32)
    small[:, 0] = np.eye(P)
    small[:, 1] = a[:, None] < a[None, :]
    small[:, 2] = a[None, :]
    before = np.broadcast_to((e[None, :] < e[:, None]).astype(np.float32).reshape(1, -1), (P, NE * NE))
    return {
        "levels": np.concatenate([level_matrices(), level_masks()], 1),
        "band": np.ascontiguousarray(bias.reshape(NT, P, S).transpose(1, 0, 2)).reshape(P, -1),
        "rope": np.ascontiguousarray(rope.reshape(NT, P, BD).transpose(1, 0, 2)).reshape(P, -1),
        "small": small.reshape(P, -1),
        "before": np.ascontiguousarray(before),
    }


def trunk(nc, a, c, out):
    with ExitStack() as ctx:
        sem = lambda name: ctx.enter_context(nc.semaphore(name))

        base = (nc.sbuf_base + 63) // 64 * 64
        top = nc.sbuf_usable_end
        cur = [base]

        def at(name, shape, dt=F32, offset=None):
            size = int(np.prod(shape[1:])) * (1 if dt == U8 else 4)
            here = cur[0] if offset is None else offset
            if offset is None:
                cur[0] = here + (size + 31) // 32 * 32
            assert here + size <= top, (name, here + size, top)
            return nc.alloc_sbuf_tensor_at(name, shape, dt, offset=here), here + (size + 31) // 32 * 32

        def own(name, shape, dt=F32):
            return at(name, shape, dt)[0]

        raw = [own(f"raw{i}", [P, TILE]) for i in range(RAW)]
        whi = [own(f"whi{i}", [P, TILE], F32R) for i in range(GT)]
        wlo = [own(f"wlo{i}", [P, TILE], F32R) for i in range(GT)]
        x = own("x", [P, NT, D])
        xT_at = cur[0]
        xT_hi = own("xT_hi", [P, KD, S], F32R)
        xT_lo = own("xT_lo", [P, KD, S], F32R)
        small = own("small", [P, 3, P])
        ident, earlier, slots = small[:, 0, :], small[:, 1, :], small[:, 2, :]
        rope = own("rope", [P, NT, 2, BD // 2])
        stat = own("stat", [P, NT, 2, 6])
        mv = own("mv", [P, NT, 2])
        ln_rs = own("ln_rs", [P, NT])
        neg_half = own("neg_half", [P, 8])
        router = own("router", [P, KD, NE])
        before = own("before", [P, NE, NE])
        vec = own("vec", [P, 96])
        phase = cur[0]

        gains, after_gains = at("gains", [P, 2, D], F32, phase)
        lev, after_lev = at("lev", [P, 2, LEV_SLOTS, P], F32R, phase)
        o = max(after_gains, after_lev)
        masks, o = at("masks", [P, NL - 1, P], U8, o)
        band, o = at("band", [P, NT, S], F32, o)
        ropeT, _ = at("ropeT", [P, 2, 512], F32, o)
        lbs, o = at("lbs", [P, 2, 512], F32, o)
        proj, o = at("proj", [P, NT, EVEN_IN], F32, o)
        levraw = nc.alloc_sbuf_tensor_at("levraw", [P, (2 * LEV_SLOTS + NL - 1) * P], F32, offset=o)
        sA, oA = at("sA", [P, NT, 1024], F32, o)
        expE = [at(f"expE{i}", [P, 4, 2, P], F32, o + i * 4096)[0] for i in range(2)]
        sB, oB = at("sB", [P, NT, 1024], F32, oA)
        qk2 = [at(f"qk2_{i}", [P, 2, 2, S], F32, oA + i * 4096)[0] for i in range(2)]
        hT, oC = at("hgT", [P, 3, AH, S], F32, oB)
        ATo, oD = at("ATo", [P, AH, 2, P], F32, oC)
        ATd = proj[:, :, ZB:ZB + 512].rearrange("p t (h c) -> p t h c", h=AH)
        qkT, q1 = at("qkT", [P, 8, S], F32, oB)
        zP = [at(f"zP{i}", [P, NT, S], F32, q1 + 2048 * i)[0] for i in range(2)]
        pT = [at(f"pT{i}", [P, NT, S], F32, q1 + 4096 + 2048 * i)[0] for i in range(2)]
        hnorm, oF = at("hnorm", [P, AD], F32, max(oD, q1 + 8192))
        sga = at("sga", [P, NT, 512], F32, oC)[0]
        h_nat, f1 = at("h_nat", [P, NT, FF], F32, after_gains)
        hT_hi, f2 = at("hT_hi", [P, KF, S], F32R, f1)
        hT_lo, f3 = at("hT_lo", [P, KF, S], F32R, f2)
        silu, f4 = at("silu", [P, NT, NU], F32, f3)
        proj2, d1 = at("proj2", [P, NT, ODD_IN], F32, after_gains)
        qkT2, d2 = at("qkT2", [P, 16, S], F32, d1)
        eP = [at(f"eP{i}", [P, 2, NT, S], F32, d2 + 4096 * i)[0] for i in range(2)]
        aP = [at(f"aP{i}", [P, NT, S], F32, d2 + 8192 + 2048 * i)[0] for i in range(2)]
        aT = [at(f"aT{i}", [P, NT, S], F32, d2 + 12288 + 2048 * i)[0] for i in range(2)]
        rtP, d4 = at("rtP", [P, 2, 1024], F32, d2 + 16384)
        sub, d5 = at("sub", [P, 2 * CD], F32, d4)
        lamv, d6 = at("lamv", [P, 4, CD], F32, d5)
        sq2 = proj2[:, :, D:D + 512].rearrange("p t (h c) -> p t h c", h=4)
        on2 = proj2[:, :, D + 512:2 * D].rearrange("p t (h c) -> p t h c", h=4)

        four_heads = lambda v: v[:].rearrange("p a b c -> p (a b c)").rearrange("p (t h c) -> p t h c", t=NT, h=4)
        sq0, on0 = four_heads(expE[0]), four_heads(qk2[0])

        xn, m2 = at("xn", [P, NT, D], F32, after_gains)
        xe_hi, m3 = at("xe_hi", [P, KD, P], F32R, m2)
        xe_lo, m4 = at("xe_lo", [P, KD, P], F32R, m3)
        h_e, m5 = at("h_e", [P, FF], F32, m4)
        hTe_hi, m6 = at("hTe_hi", [P, KF, P], F32R, m5)
        hTe_lo, m7 = at("hTe_lo", [P, KF, P], F32R, m6)
        silu_e, m8 = at("silu_e", [P, 2, NU], F32, m7)
        pick, m9 = at("pick", [P, NT, P], F32, m8)
        put_next, m10 = at("put_next", [P, S], F32R, m9)
        put, m11 = at("put", [P, S], F32R, m10)
        y_hi, m12 = at("y_hi", [P, D], F32R, m11)
        y_lo, m13 = at("y_lo", [P, D], F32R, m12)
        xT_f, m14 = at("xT_f", [P, KD, S], F32, m5)
        route, m16 = at("route", [P, 12, NT, NE], F32, m13)
        cmp, m17 = at("cmp", [P, 2, NT, NE, NE], F32, m16)
        ones, m19 = at("ones", [P, P], F32, m17)
        seat, m20 = at("seat", [P, NT, 2 * NE], F32, m19)
        gate_col, m21 = at("gate_col", [P, NT], F32, m20)
        slot_gate, m22 = at("slot_gate", [P, 2], F32, m21)
        more, m23 = at("more", [P, 1], I32, m22)

        late = [at(f"late{j}", [P, kc * n], F32, where)[0] for j, ((kc, n), where) in
                enumerate(zip(G_DN[1], (xT_at, xT_at + 6144, xT_at + 12288, m23)))]

        psum = ctx.enter_context(nc.psum_tensor("psum", [P, 8, 512], F32))

        raw_full = [sem(f"raw_full{i}") for i in range(RAW)]
        late_full, hi_done, lo_done, tile_used = (
            sem(name) for name in ("late_full", "hi_done", "lo_done", "tile_used"))
        const_in, x_in, band_in, lb_in, lev_in = (
            sem(name) for name in ("const_in", "x_in", "band_in", "lb_in", "lev_in"))
        vec_in, gain_in, rope_in, router_in, before_in = (
            sem(name) for name in ("vec_in", "gain_in", "rope_in", "router_in", "before_in"))
        sub_in, lambda_in = (
            sem(name) for name in ("sub_in", "lambda_in"))
        dve_link, pool_link = (
            sem(name) for name in ("dve_link", "pool_link"))
        tokens_turned, tokens_hi, tokens_lo = (
            sem(name) for name in ("tokens_turned", "tokens_hi", "tokens_lo"))
        block_out_act, block_out_dve = (
            sem(name) for name in ("block_out_act", "block_out_dve"))
        rows_done, ln_stats, ln_root, ln_scaled0, ln_done0 = (
            sem(name) for name in ("rows_done", "ln_stats", "ln_root", "ln_scaled0", "ln_done0"))
        ln_done1 = sem("ln_done1")
        mix_done, heads_out = (
            sem(name) for name in ("mix_done", "heads_out"))
        on_kept, squares_ready, square_sums, rms_ready = (
            sem(name) for name in ("on_kept", "squares_ready", "square_sums", "rms_ready"))
        up_silu, up_hidden, hidden_turned, hidden_hi_ready, hidden_lo_ready = (
            sem(name) for name in ("up_silu", "up_hidden", "hidden_turned", "hidden_hi_ready", "hidden_lo_ready"))
        bounds_shifted, bounds_exp, sigmoids_ready, keys_ready, forgets_ready = (
            sem(name) for name in ("bounds_shifted", "bounds_exp", "sigmoids_ready", "keys_ready", "forgets_ready"))
        logs_ready, logs_hi, logs_lo, levels_ready, out_gate_ready = (
            sem(name) for name in ("logs_ready", "logs_hi", "logs_lo", "levels_ready", "out_gate_ready"))
        hgrn_qk_turned, hgrn_qk_act, hgrn_qk_dve = (
            sem(name) for name in ("hgrn_qk_turned", "hgrn_qk_act", "hgrn_qk_dve"))
        exponents_ready, decays_ready, qk_scaled, unit_scores, scores_kept = (
            sem(name) for name in ("exponents_ready", "decays_ready", "qk_scaled", "unit_scores", "scores_kept"))
        hgrn_summed = sem("hgrn_summed")
        rope_done, rope2_pool, qk_turned, qk_out_act, qk_out_dve = (
            sem(name) for name in ("rope_done", "rope2_pool", "qk_turned", "qk_out_act", "qk_out_dve"))
        dil_scores, dil_negmax, dil_probs, dil_turned, dil_moved = (
            sem(name) for name in ("dil_scores", "dil_negmax", "dil_probs", "dil_turned", "dil_moved"))
        dil_values = sem("dil_values")
        map_scored, map_negmax, map_probs, maps_combined, maps_turned = (
            sem(name) for name in ("map_scored", "map_negmax", "map_probs", "maps_combined", "maps_turned"))
        maps_moved, maps_summed = (
            sem(name) for name in ("maps_moved", "maps_summed"))
        lambda_sums, lambda_exps = (
            sem(name) for name in ("lambda_sums", "lambda_exps"))
        router_x_act, router_x_dve, logits_ready, experts_chosen, logits_shifted = (
            sem(name) for name in ("router_x_act", "router_x_dve", "logits_ready", "experts_chosen", "logits_shifted"))
        gate_exps, ones_set, positions_ready, more_set, xn_set = (
            sem(name) for name in ("gate_exps", "ones_set", "positions_ready", "more_set", "xn_set"))
        pick_ready, pick_used, gathered, gathered_hi, gathered_lo = (
            sem(name) for name in ("pick_ready", "pick_used", "gathered", "gathered_hi", "gathered_lo"))
        map_kept, map_current = (
            sem(name) for name in ("map_kept", "map_current"))
        silu_ready, hidden_ready, chunks_turned, chunks_hi, chunks_lo = (
            sem(name) for name in ("silu_ready", "hidden_ready", "chunks_turned", "chunks_hi", "chunks_lo"))
        y_hi_ready, y_lo_ready, rows_scattered, rows_added = (
            sem(name) for name in ("y_hi_ready", "y_lo_ready", "rows_scattered", "rows_added"))
        out_sent = sem("out_sent")

        def by_bank(xT, b):
            return xT[:, 4 * (b % 2):4 * (b % 2) + 4, (b // 2) * P:(b // 2 + 1) * P]

        def rawv(par, j, kc, n):
            return raw[GT * par + j][:, 0:kc * n].rearrange("p (k n) -> p k n", n=n)

        def load_group(sp, q, par, shapes, srcs, first=False):
            for j, ((kc, n), src) in enumerate(zip(shapes, srcs)):
                if not first:
                    sp.wait_ge(lo_done, 2 * GT * q + GT * (par - 2) + j + 1)
                sp.dma_start(rawv(par, j, kc, n), src).then_inc(raw_full[GT * par + j], 16)

        def split_hi(act, q, par, shapes, js=range(GT), first=False, in_late=False, after_late=False):
            for j in js:
                kc, n = shapes[j]
                if in_late:
                    act.wait_ge(late_full, 16 * GT)
                else:
                    act.wait_ge(raw_full[GT * par + j], 16 * (q if after_late and par else q + 1))
                if not first:
                    act.wait_ge(tile_used, 2 * GT * q + GT * (par - 1) + j + 1)
                src = late[j] if in_late else raw[GT * par + j]
                nc.scalar.copy(whi[j][:, 0:kc * n], src[:, 0:kc * n]).then_inc(hi_done, 1)

        def split_lo(dve, q, par, shapes, js=range(GT), in_late=False):
            for j in js:
                kc, n = shapes[j]
                dve.wait_ge(hi_done, 2 * GT * q + GT * par + j + 1)
                src = late[j] if in_late else raw[GT * par + j]
                nc.vector.tensor_tensor(wlo[j][:, 0:kc * n], src[:, 0:kc * n],
                                        whi[j][:, 0:kc * n].bitcast(F32), ALU.subtract).then_inc(lo_done, 1)

        EARLY, LATE = (0, 1, 2), (3,)

        def group_used(q, par):
            return 2 * GT * q + GT * (par + 1)

        def tile_products(pe, q, par, j, kc, n, k0, lhs, outs, first_k, last_k):
            pe.wait_ge(lo_done, 2 * GT * q + GT * par + j + 1)
            hi, lo = lhs
            for kk in range(kc):
                k = k0 + kk
                w_h = whi[j][:, kk * n:(kk + 1) * n]
                w_l = wlo[j][:, kk * n:(kk + 1) * n]
                for ps, t0 in outs:
                    nc.tensor.matmul(ps, hi[:, k, t0:t0 + P], w_h, start=(k == first_k), stop=False)
                    nc.tensor.matmul(ps, hi[:, k, t0:t0 + P], w_l, start=False, stop=False)
                    last = nc.tensor.matmul(ps, lo[:, k, t0:t0 + P], w_h, start=False, stop=(k == last_k))
            last.then_inc(tile_used, 1)

        Q_IN, Q_OUT, Q_UP, Q_DN, Q_IN2, Q_OUT2, Q_MOE = 0, 4, 5, 9, 11, 14, 15
        w_in = a["ev_w_in"][0].rearrange("(k p) n -> p k n", p=P)
        w_out = a["ev_w_out"][0].rearrange("(k p) n -> p k n", p=P)
        w_1 = a["ev_w1"][0].rearrange("(k p) n -> p k n", p=P)
        w_3 = a["ev_w3"][0].rearrange("(k p) n -> p k n", p=P)
        w_2 = a["ev_w2"][0].rearrange("(k p) n -> p k n", p=P)
        w_in2 = a["od_w_in"][0].rearrange("(k p) n -> p k n", p=P)
        w_out2 = a["od_w_out"][0].rearrange("(k p) n -> p k n", p=P)

        def sq_src(w, b):
            return [w[:, 2 * j:2 * j + 2, bass.ds(b * NB, NB)] for j in range(GT)]

        def up_src(w1, w3, b):
            return [w[:, 4 * j:4 * j + 4, bass.ds(b * NU, NU)] for w in (w1, w3) for j in range(2)]

        def dn_src(w2, half, part):
            return [w2[:, k0:k0 + kc, half * NB:(half + 1) * NB] for k0, (kc, _) in zip(DN_K0[part], G_DN[part])]

        m_w1 = a["od_w1"][0].rearrange("e (k p) n -> p e k n", p=P)
        m_w3 = a["od_w3"][0].rearrange("e (k p) n -> p e k n", p=P)
        m_w2 = a["od_w2"][0].rearrange("e (k p) n -> p e k n", p=P)

        def up_src_e(e, b):
            return [w[:, bass.ds(e, 1), 4 * j:4 * j + 4, bass.ds(b * NU, NU)].rearrange("p e k n -> p (e k) n")
                    for w in (m_w1, m_w3) for j in range(2)]

        def dn_src_e(e, half, part):
            return [m_w2[:, bass.ds(e, 1), k0:k0 + kc, half * NB:(half + 1) * NB].rearrange("p e k n -> p (e k) n")
                    for k0, (kc, _) in zip(DN_K0[part], G_DN[part])]

        TURNS = [(0, 4, 6, 3), (4, 4, 7, 4), (8, 4, 6, 5), (12, 4, 7, 6), (16, 3, 6, 7), (19, 3, 3, None)]
        TURN_AFTER = {after: g for g, (_, _, _, after) in enumerate(TURNS) if after is not None}
        GATHER_AFTER = 2

        def unit(n):
            return (2 * (n // 4) + n % 2, n // 2 % 2) if n < 2 * NL else (NL, n % 2)

        def kept(n):
            li, pair = unit(n)
            return (ATo[:, 2 * pair:2 * pair + 2, :, :] if li == 0 else
                    ATd[:, :, 2 * pair:2 * pair + 2, :].rearrange("p t h c -> p h t c"))

        def stands_before(n):
            same_pair = [m for m in range(n) if unit(m)[1] == unit(n)[1]]
            return max(same_pair[-1] + 1, 4)

        def q_moe(n):
            return Q_MOE + 6 * n

        def up_group(n, b):
            return q_moe(n) + b // 2, b % 2

        def up_shapes(b):
            return G_UP if b < UB else G_DN[0]

        block = ctx.enter_context(nc.Block())

        @block.sync
        def _(sp):
            sp.dma_start(x[:], a["x"][0].rearrange("(t p) d -> p t d", p=P)).then_inc(x_in, 16)
            sp.dma_start(small[:].rearrange("p a b -> p (a b)"), c["small"]).then_inc(const_in, 16)
            for par in range(2):
                load_group(sp, 0, par, G_SQ, sq_src(w_in, par), first=True)
            with sp.Fori(1, 4) as q:
                for par in range(2):
                    load_group(sp, Q_IN + q, par, G_SQ, sq_src(w_in, 2 * q + par))
            for par in range(2):
                load_group(sp, Q_OUT, par, G_SQ, sq_src(w_out, par))
            with sp.Fori(0, 4) as q:
                for par in range(2):
                    load_group(sp, Q_UP + q, par, G_UP, up_src(w_1, w_3, 2 * q + par))
            for half in range(2):
                for part in range(2):
                    load_group(sp, Q_DN + half, part, G_DN[part], dn_src(w_2, half, part))
            with sp.Fori(0, 3) as q:
                for par in range(2):
                    load_group(sp, Q_IN2 + q, par, G_SQ, sq_src(w_in2, 2 * q + par))
            for par in range(2):
                load_group(sp, Q_OUT2, par, G_SQ, sq_src(w_out2, par))

            def load_up(n, e, first):
                with sp.Fori(first, 4) as q:
                    for par in range(2):
                        load_group(sp, q_moe(n) + q, par, G_UP, up_src_e(e, 2 * q + par))

            def load_down(n, e, groups=4):
                for half, part in ((0, 0), (0, 1), (1, 0), (1, 1))[:groups]:
                    load_group(sp, q_moe(n) + 4 + half, part, G_DN[part], dn_src_e(e, half, part))

            for par in range(2):
                load_group(sp, Q_MOE, par, G_UP, up_src_e(0, par))
            sp.wait_ge(tile_used, group_used(Q_OUT2, 1))
            for j, src in enumerate(dn_src_e(NE - 1, 1, 1)):
                kc, n = G_DN[1][j]
                sp.dma_start(late[j][:].rearrange("p (k n) -> p k n", n=n), src).then_inc(late_full, 16)
            load_up(0, 0, 1)
            load_down(0, 0)
            with sp.Fori(1, NE - 1) as n:
                load_up(n, n, 0)
                load_down(n, n)
            load_up(NE - 1, NE - 1, 0)
            load_down(NE - 1, NE - 1, groups=3)
            sp.wait_ge(more_set, 1)
            flag = sp.value_load(more[0:1, 0:1], min_val=0, max_val=1)
            with sp.If(flag):
                with sp.Fori(0, NE) as e:
                    load_up(e + NE, e, 0)
                    load_down(e + NE, e)
            for t in range(NT):
                sp.wait_ge(ln_done1 if t else ln_done0, 4)
                sp.dma_start(out[0][t * P:(t + 1) * P, :], x[:, t, :]).then_inc(out_sent, 16)
            sp.wait_ge(out_sent, 16 * NT)

        @block.gpsimd
        def _(pool):
            n_link = [0]

            def link(ins):
                n_link[0] += 1
                ins.then_inc(pool_link, 1)
                pool.wait_ge(pool_link, n_link[0])

            def load_gains(i, g, b):
                if i:
                    pool.wait_ge(ln_done0, i)
                    pool.wait_ge(ln_done1, i)
                pool.dma_start(gains[:, 0, :], a[g].partition_broadcast(P)).then_inc(gain_in, 16)
                pool.dma_start(gains[:, 1, :], a[b].partition_broadcast(P)).then_inc(gain_in, 16)

            def rsqrt(dst, src, scale):
                link(nc.gpsimd.tensor_scalar(dst, src, scale, EPS, ALU.mult, ALU.add))
                return nc.gpsimd.tensor_tensor(dst, dst, neg_half[:, 0:dst.shape[1]], ALU.pow)

            def add_bias(i):
                pool.wait_ge(ln_scaled0, i + 1)
                nc.gpsimd.tensor_tensor(x[:, 0, :], x[:, 0, :], gains[:, 1, :], ALU.add).then_inc(ln_done0, 1)

            def ln_rsqrt(i):
                for t in range(NT):
                    pool.wait_ge(ln_stats, NT * i + t + 1)
                    rsqrt(ln_rs[:, t:t + 1], mv[:, t, 1:2], 1.0).then_inc(ln_root, 1)
                    if t == 0 and i < 3:
                        add_bias(i)
                if i == 3:
                    add_bias(i)

            def rotate(src, t, tmp, done):
                n = src.shape[1] // 32
                both = src.rearrange("p (n c) -> p n c", c=32)
                half = src.rearrange("p (n h c) -> p n h c", h=2, c=32)
                A = tmp[:, 0, 0:n * 32].rearrange("p (n c) -> p n c", c=32)
                B = tmp[:, 1, 0:n * 32].rearrange("p (n c) -> p n c", c=32)
                Ah = tmp[:, 0, 0:n * 32].rearrange("p (n h c) -> p n h c", h=2, c=32)
                Bh = tmp[:, 1, 0:n * 32].rearrange("p (n h c) -> p n h c", h=2, c=32)
                cos = rope[:, t, 0:1, :].broadcast_to([P, n, 32])
                sin = rope[:, t, 1:2, :].broadcast_to([P, n, 32])
                nc.gpsimd.tensor_tensor(A, both, cos, ALU.mult)
                link(nc.gpsimd.tensor_tensor(B, both, sin, ALU.mult))
                nc.gpsimd.tensor_tensor(half[:, :, 0, :], Ah[:, :, 0, :], Bh[:, :, 1, :], ALU.subtract).then_inc(done, 1)
                nc.gpsimd.tensor_tensor(half[:, :, 1, :], Ah[:, :, 1, :], Bh[:, :, 0, :], ALU.add).then_inc(done, 1)

            pool.dma_start(rope[:].rearrange("p t h c -> p (t h c)"), c["rope"]).then_inc(rope_in, 16)
            pool.dma_start(lbs[:, 0, :], a["ev_lb_logits"][0].partition_broadcast(P)).then_inc(lb_in, 16)
            pool.dma_start(levraw[:], c["levels"]).then_inc(lev_in, 16)
            pool.dma_start(band[:].rearrange("p t s -> p (t s)"), c["band"]).then_inc(band_in, 16)
            pool.dma_start(hnorm[:], a["ev_hgrn_norm"][0].partition_broadcast(P)).then_inc(vec_in, 16)
            pool.dma_start(router[:], a["od_router"][0].rearrange("(k p) e -> p k e", p=P)).then_inc(router_in, 16)
            pool.dma_start(before[:].rearrange("p a b -> p (a b)"), c["before"]).then_inc(before_in, 16)
            nc.gpsimd.memset(neg_half[:], -0.5)
            pool.wait_ge(rope_in, 16)
            pool.wait_ge(sigmoids_ready, 3)
            pool.wait_ge(vec_in, 16)
            for t in range(NT):
                link(nc.gpsimd.tensor_tensor(proj[:, t, GA:GA + 512], proj[:, t, GA:GA + 512],
                                             sga[:, t, :], ALU.mult))
                v = proj[:, t, GA:GA + 512].rearrange("p (h c) -> p h c", h=AH)
                nc.gpsimd.tensor_tensor(v, v, hnorm[:, None, :].broadcast_to([P, AH, AD]), ALU.mult).then_inc(out_gate_ready, 1)
            pool.wait_ge(keys_ready, 1)
            pool.wait_ge(forgets_ready, 1)
            pool.wait_ge(block_out_act, 7)
            pool.wait_ge(block_out_dve, 7)
            for u, (t, col) in enumerate((t, col) for t in range(NT) for col in (QB, KB)):
                if u:
                    pool.wait_ge(rope_done, 2 * u)
                rotate(proj[:, t, col:col + 512], t, ropeT, rope_done)
            def rms_heads(r, on, gain, dst):
                pool.wait_ge(square_sums, r + 1)
                link(rsqrt(vec[:, 40:48], vec[:, 32:40], 1.0 / AD))
                rs = vec[:, 40:48].rearrange("p (t h) -> p t h", h=4)[:, :, :, None].broadcast_to([P, NT, 4, 128])
                link(nc.gpsimd.tensor_tensor(on, on, rs, ALU.mult))
                nc.gpsimd.tensor_tensor(dst.rearrange("p t (h c) -> p t h c", h=4), on, gain, ALU.mult).then_inc(heads_out, 1)

            rms_heads(0, on0, proj[:, :, GA:GA + 512].rearrange("p t (h c) -> p t h c", h=4), proj[:, :, 0:512])
            load_gains(0, "ev_ln1_g", "ev_ln1_b")
            ln_rsqrt(0)
            load_gains(1, "ev_ln2_g", "ev_ln2_b")
            ln_rsqrt(1)

            pool.wait_ge(ln_done1, 2)
            pool.dma_start(sub[:], a["od_subln"][0].partition_broadcast(P)).then_inc(sub_in, 16)
            pool.dma_start(lamv[:].rearrange("p a b -> p (a b)"),
                           a["od_lambda"][0].rearrange("a b -> (a b)").partition_broadcast(P)).then_inc(lambda_in, 16)
            load_gains(2, "od_ln1_g", "od_ln1_b")
            for u, (col, t) in enumerate((col, t) for col in (0, D) for t in range(NT)):
                if t == 0:
                    pool.wait_ge(block_out_act, 10 + 2 * col // D)
                    pool.wait_ge(block_out_dve, 10 + 2 * col // D)
                if u:
                    pool.wait_ge(rope2_pool, 2 * u)
                rotate(proj2[:, t, col:col + D], t, rtP, rope2_pool)
            rms_heads(1, on2, sub[:, None, None, :].broadcast_to([P, NT, 4, 128]), proj2[:, :, 0:512])
            for t in range(NT):
                pool.wait_ge(square_sums, 3 + t)
                rsqrt(vec[:, 40 + 4 * t:44 + 4 * t], vec[:, 32 + 4 * t:36 + 4 * t], 1.0 / AD).then_inc(rms_ready, 1)
            ln_rsqrt(2)
            pool.wait_ge(ln_done1, 3)
            nc.gpsimd.memset(ones[:], 1.0).then_inc(ones_set, 1)
            load_gains(3, "od_ln2_g", "od_ln2_b")
            ln_rsqrt(3)


        @block.scalar
        def _(act):
            def transposed_hi(i):
                for b in range(4):
                    act.wait_ge(tokens_turned, 4 * i + b + 1)
                    nc.scalar.copy(by_bank(xT_hi, b), psum[:, 4 + b, :].rearrange("p (k s) -> p k s", s=P)).then_inc(tokens_hi, 1)

            def keep_square(sq, on, ready, value):
                act.wait_ge(ready, value)
                nc.scalar.copy(on, psum[:, 6:8, :].rearrange("p t (h c) -> p t h c", h=4)).then_inc(on_kept, 1)
                act.wait_ge(on_kept, 1 if on is on0 else 2)
                nc.scalar.activation(sq, on, ACT.Square).then_inc(squares_ready, 1)

            transposed_hi(0)
            split_hi(act, Q_IN, 0, G_SQ, first=True)

            def in_block(q, par, dst, col, nxt, to_end=True):
                split_hi(act, *nxt, G_SQ, js=EARLY)
                act.wait_ge(tile_used, group_used(q, par))
                nc.scalar.copy(dst[:, 0, bass.ds(col, NB)], psum[:, 2 * par, :]).then_inc(block_out_act, 1)
                if to_end:
                    split_hi(act, *nxt, G_SQ, js=LATE)

            def even_block(b):
                q, par = Q_IN + b // 2, b % 2
                nxt = (q, 1) if par == 0 else (q + 1, 0)
                in_block(q, par, proj, b * NB, nxt, to_end=b < 7)

            even_block(0)
            even_block(1)
            act.wait_ge(bounds_shifted, 1)
            nc.scalar.activation(lbs[:, 0, :], lbs[:, 0, :], ACT.Exp).then_inc(bounds_exp, 1)
            even_block(2)
            act.wait_ge(block_out_dve, 3)
            act.wait_ge(block_out_act, 3)
            act.wait_ge(levels_ready, 2)
            nc.scalar.activation(sB[:], proj[:, :, ZF:ZF + 1024], ACT.Sigmoid, scale=-1.0).then_inc(sigmoids_ready, 1)
            nc.scalar.activation(sA[:], proj[:, :, ZF:ZF + 1024], ACT.Sigmoid).then_inc(sigmoids_ready, 1)
            even_block(3)
            even_block(4)
            act.wait_ge(block_out_dve, 5)
            act.wait_ge(block_out_act, 5)
            nc.scalar.activation(sga[:], proj[:, :, GA:GA + 512], ACT.Sigmoid).then_inc(sigmoids_ready, 1)
            act.wait_ge(forgets_ready, 1)
            nc.scalar.activation(sA[:], sA[:], ACT.Ln).then_inc(logs_ready, 1)
            for b in range(5, 8):
                even_block(b)
                if b < 7:
                    for i in ((0, 1) if b == 5 else (2,)):
                        act.wait_ge(hgrn_qk_turned, 2 * i + 1)
                        nc.scalar.copy(hT[:, i, 0:2, :].rearrange("p h s -> p (h s)"), psum[:, 4 + 2 * i % 4, :]).then_inc(hgrn_qk_act, 1)
            act.wait_ge(logs_ready, 1)
            for t in range(NT):
                nc.scalar.copy(xT_hi[:, 4 * t:4 * t + 4, :].rearrange("p k s -> p (k s)"), sA[:, t, :]).then_inc(logs_hi, 1)
            split_hi(act, Q_OUT, 0, G_SQ, js=LATE)
            for n in range(2 * NL):
                act.wait_ge(exponents_ready, n // 2 + 1)
                if n == 0:
                    act.wait_ge(logs_lo, 2)
                if n >= 2:
                    act.wait_ge(qk_scaled, n - 1)
                nc.scalar.activation(expE[n % 2][:],
                                     psum[:, 0:4, :].rearrange("p b (d l c) -> p b d l c", d=2, l=2)[:, :, :, n % 2, :],
                                     ACT.Exp).then_inc(decays_ready, 1)
                if n == 3:
                    act.wait_ge(out_gate_ready, 2)
                if n in (3, 5):
                    for u in (n - 3, n - 2):
                        act.wait_ge(unit_scores, u + 1)
                        nc.scalar.copy(kept(u), psum[:, 4 + u % 2, :].rearrange("p (h i c) -> p h i c", h=2, i=2)).then_inc(scores_kept, 1)
            for b in (0, 2):
                act.wait_ge(qk_turned, b + 1)
                nc.scalar.copy(qkT[:, 2 * b:2 * b + 2, :].rearrange("p k s -> p (k s)"), psum[:, b, :]).then_inc(qk_out_act, 1)
            keep_square(sq0, on0, hgrn_summed, 1)

            def move_probs(h):
                act.wait_ge(dil_turned, h + 1)
                if h >= 2:
                    act.wait_ge(dil_values, h - 1)
                nc.scalar.copy(pT[h % 2][:].rearrange("p s t -> p (s t)"), psum[:, 4 + h % 2, :]).then_inc(dil_moved, 1)

            for h in range(BH):
                act.wait_ge(dil_negmax, h + 1)
                for t in range(NT):
                    nc.scalar.activation(zP[h % 2][:, t, :], zP[h % 2][:, t, :], ACT.Exp,
                                         bias=vec[:, 16 + 2 * h + t:17 + 2 * h + t],
                                         accum_out=vec[:, 48 + 2 * h + t:49 + 2 * h + t]).then_inc(dil_probs, 1)
                if h:
                    move_probs(h - 1)
            move_probs(BH - 1)
            transposed_hi(1)
            split_hi(act, Q_OUT, 1, G_SQ)
            split_hi(act, Q_UP, 0, G_UP)

            transposed_hi(2)

            def up_blocks(q, first=False, last=False):
                for par in range(2):
                    nxt = (Q_UP + q, 1, G_UP) if par == 0 else (Q_DN, 0, G_DN[0]) if last else (Q_UP + q + 1, 0, G_UP)
                    split_hi(act, *nxt, js=EARLY)
                    act.wait_ge(tile_used, group_used(Q_UP + q, par))
                    if not (first and par == 0):
                        act.wait_ge(up_hidden, 2 * q + par)
                    nc.scalar.activation(silu[:], psum[:, 4 * par:4 * par + 2, 0:NU], ACT.Silu).then_inc(up_silu, 1)
                    split_hi(act, *nxt, js=LATE)

            def hidden_hi(g):
                act.wait_ge(hidden_turned, g + 1)
                nc.scalar.copy(hT_hi[:, 2 * g:2 * g + 2, :].rearrange("p k s -> p (k s)"), psum[:, g % 4, :]).then_inc(hidden_hi_ready, 1)

            up_blocks(0, first=True)
            with act.Fori(1, 3) as q:
                up_blocks(q)
            up_blocks(3, last=True)
            for g in range(6):
                hidden_hi(g)
            split_hi(act, Q_DN, 1, G_DN[1])
            for g in range(6, 11):
                hidden_hi(g)
            split_hi(act, Q_DN + 1, 0, G_DN[0])
            split_hi(act, Q_DN + 1, 1, G_DN[1])
            split_hi(act, Q_IN2, 0, G_SQ)

            transposed_hi(3)
            with act.Fori(0, 2) as q:
                in_block(Q_IN2 + q, 0, proj2, q * 2 * NB, (Q_IN2 + q, 1))
                in_block(Q_IN2 + q, 1, proj2, q * 2 * NB + NB, (Q_IN2 + q + 1, 0))
            def queries_keys(half):
                for b in (0, 2):
                    act.wait_ge(qk_turned, 4 + 4 * half + b + 1)
                    k0 = 8 * half + 2 * b
                    nc.scalar.copy(qkT2[:, k0:k0 + 2, :].rearrange("p k s -> p (k s)"), psum[:, 4 + b, :]).then_inc(qk_out_act, 1)

            in_block(Q_IN2 + 2, 0, proj2, 4 * NB, (Q_IN2 + 2, 1))
            queries_keys(0)
            in_block(Q_IN2 + 2, 1, proj2, 5 * NB, (Q_OUT2, 0))
            queries_keys(1)

            act.wait_ge(lambda_sums, 1)
            nc.scalar.activation(vec[:, 90:92], vec[:, 88:90], ACT.Exp).then_inc(lambda_exps, 1)

            def map_exps(h):
                p = h % 2
                act.wait_ge(map_negmax, h + 1)
                if h >= 2:
                    act.wait_ge(maps_combined, h - 1)
                for u in range(4):
                    nc.scalar.activation(eP[p][:, u // 2, u % 2, :], psum[:, 2 * p + u // 2, (u % 2) * S:(u % 2 + 1) * S],
                                         ACT.Exp, bias=vec[:, 16 + 4 * p + u:17 + 4 * p + u], scale=CD ** -0.5,
                                         accum_out=vec[:, 48 + 4 * p + u:49 + 4 * p + u]).then_inc(map_probs, 1)

            def move_maps(h):
                act.wait_ge(maps_turned, h + 1)
                if h >= 2:
                    act.wait_ge(maps_summed, h - 1)
                nc.scalar.copy(aT[h % 2][:].rearrange("p s t -> p (s t)"), psum[:, 4 + h % 2, :]).then_inc(maps_moved, 1)

            map_exps(0)
            map_exps(1)
            for h in range(CH):
                move_maps(h)
                if h + 2 < CH:
                    map_exps(h + 2)
                if h == 4:
                    keep_square(sq2, on2, maps_summed, 4)
            act.wait_ge(maps_summed, 8)
            act.wait_ge(heads_out, 2)
            for t in range(NT):
                nc.scalar.activation(sq2[:, t], psum[:, 6 + t, :].rearrange("p (h c) -> p h c", h=4), ACT.Square).then_inc(squares_ready, 1)
            transposed_hi(4)
            split_hi(act, Q_OUT2, 1, G_SQ)
            split_hi(act, q_moe(0), 0, G_UP)

            for b in range(3):
                act.wait_ge(tokens_turned, 20 + b + 1)
                nc.scalar.copy(by_bank(xT_f, b), psum[:, 4 + b, :].rearrange("p (k s) -> p k s", s=P)).then_inc(router_x_act, 1)
            nc.scalar.copy(xn[:], x[:]).then_inc(xn_set, 1)
            act.wait_ge(logits_shifted, 1)
            nc.scalar.activation(route[:, 4], route[:, 3], ACT.Exp).then_inc(gate_exps, 1)

            def gather_hi(n):
                for b in range(2):
                    act.wait_ge(gathered, 2 * n + b + 1)
                    nc.scalar.copy(xe_hi[:, 4 * b:4 * b + 4, :].rearrange("p k s -> p (k s)"), psum[:, 4 + b, :]).then_inc(gathered_hi, 1)

            def keep_map(n, first=False):
                act.wait_ge(pick_used, n + 1)
                if not first:
                    act.wait_ge(map_current, n)
                nc.scalar.copy(put_next[:], psum[:, 6, 2 * P:4 * P]).then_inc(map_kept, 1)
                nc.scalar.copy(slot_gate[:, 0:1], psum[:, 6, 0:1]).then_inc(map_kept, 1)

            def turn_hi(n, g):
                k0, kc, bank, _ = TURNS[g]
                act.wait_ge(chunks_turned, 6 * n + g + 1)
                nc.scalar.copy(hTe_hi[:, k0:k0 + kc, :].rearrange("p k s -> p (k s)"), psum[:, bank, 0:kc * P]).then_inc(chunks_hi, 1)

            def block_e(n, b, again=False):
                split_hi(act, *up_group(n, b + 1), up_shapes(b + 1), js=EARLY, after_late=again)
                act.wait_ge(tile_used, group_used(*up_group(n, b)))
                act.wait_ge(hidden_ready, 8 * n + b + 1)
                nc.scalar.activation(silu_e[:, b % 2, :], psum[:, 2 * (b % 2), 0:NU], ACT.Silu).then_inc(silu_ready, 1)
                split_hi(act, *up_group(n, b + 1), up_shapes(b + 1), js=LATE, after_late=again)

            def expert(n, last, again=False):
                q0 = q_moe(n)
                for b in range(1, UB):
                    block_e(n, b, again)
                    if b == GATHER_AFTER and not last:
                        keep_map(n + 1)
                    if b in TURN_AFTER:
                        turn_hi(n, TURN_AFTER[b])
                if not last:
                    gather_hi(n + 1)
                turn_hi(n, 5)
                split_hi(act, q0 + 4, 1, G_DN[1], after_late=again)
                split_hi(act, q0 + 5, 0, G_DN[0])
                for half in range(2):
                    if half:
                        split_hi(act, q0 + 5, 1, G_DN[1], in_late=last and not again, after_late=again)
                        if not last:
                            split_hi(act, q0 + 6, 0, G_UP)
                    act.wait_ge(tile_used, group_used(q0 + 4 + half, 1))
                    act.wait_ge(map_current, n + 1)
                    nc.scalar.activation(y_hi[:, half * NB:(half + 1) * NB], psum[:, 2 * half, :], ACT.Copy,
                                         scale=slot_gate[:, 1:2]).then_inc(y_hi_ready, 1)
                if not last:
                    block_e(n + 1, 0)

            gather_hi(0)
            keep_map(0, first=True)
            block_e(0, 0)
            with act.Fori(0, NE - 1) as n:
                expert(n, False)
            expert(NE - 1, True)
            act.wait_ge(more_set, 1)
            flag = act.value_load(more[0:1, 0:1], min_val=0, max_val=1)
            with act.If(flag):
                with act.Fori(NE, 2 * NE) as n:
                    split_hi(act, q_moe(n), 0, G_UP)
                    gather_hi(n)
                    keep_map(n)
                    block_e(n, 0, again=True)
                    expert(n, True, again=True)

        @block.vector
        def _(dve):
            n_link = [0]

            def link(ins):
                n_link[0] += 1
                ins.then_inc(dve_link, 1)
                dve.wait_ge(dve_link, n_link[0])

            def transposed_lo(i):
                for b in range(4):
                    dve.wait_ge(tokens_hi, 4 * i + b + 1)
                    nc.vector.tensor_tensor(by_bank(xT_lo, b), psum[:, 4 + b, :].rearrange("p (k s) -> p k s", s=P),
                                            by_bank(xT_hi, b).bitcast(F32), ALU.subtract).then_inc(tokens_lo, 1)

            def residual(bank, half, t):
                v = x[:, t, half * NB:(half + 1) * NB]
                link(nc.vector.scalar_tensor_tensor(v, v, ALPHA, psum[:, bank + t, :], ALU.mult, ALU.add))
                link(nc.vector.bn_stats(stat[:, t, half, :], v))

            def mean_var(t):
                nc.vector.bn_aggr(mv[:, t, :], stat[:, t, :, :].rearrange("p a b -> p (a b)")).then_inc(ln_stats, 1)

            def normalize(i, t):
                v = x[:, t, :]
                dve.wait_ge(gain_in, 32 * (i + 1))
                dve.wait_ge(ln_root, NT * i + t + 1)
                link(nc.vector.tensor_scalar(v, v, mv[:, t, 0:1], ln_rs[:, t:t + 1], ALU.subtract, ALU.mult))
                ins = nc.vector.tensor_tensor(v, v, gains[:, 0, :], ALU.mult)
                if t == 0:
                    ins.then_inc(ln_scaled0, 1)
                else:
                    link(ins)
                    nc.vector.tensor_tensor(v, v, gains[:, 1, :], ALU.add).then_inc(ln_done1, 1)

            def end_of_stage(i, q, bank, nxt):
                for t in range(NT):
                    if t == 0:
                        dve.wait_ge(rows_done, i + 1)
                    else:
                        dve.wait_ge(tile_used, group_used(q, 1))
                    residual(bank, 1, t)
                    mean_var(t)
                    if t == NT - 1:
                        split_lo(dve, *nxt, js=(0,))
                    normalize(i, t)

            def sum_squares(r, sq):
                dve.wait_ge(squares_ready, r + 1)
                nc.vector.tensor_reduce(vec[:, 32:40].rearrange("p (t h) -> p t h", h=4), sq, AX_X, ALU.add).then_inc(square_sums, 1)

            transposed_lo(0)
            split_lo(dve, Q_IN, 0, G_SQ)

            def in_block(q, par, dst, col, nxt, to_end=True):
                split_lo(dve, *nxt, G_SQ, js=EARLY)
                dve.wait_ge(tile_used, group_used(q, par))
                nc.vector.tensor_copy(dst[:, 1, bass.ds(col, NB)], psum[:, 2 * par + 1, :]).then_inc(block_out_dve, 1)
                if to_end:
                    split_lo(dve, *nxt, G_SQ, js=LATE)

            def even_block(b):
                q, par = Q_IN + b // 2, b % 2
                in_block(q, par, proj, b * NB, (q, 1) if par == 0 else (q + 1, 0), to_end=b < 7)

            sBv = sB[:].rearrange("p t (d c) -> p (t d) c", d=2)
            sAv = sA[:].rearrange("p t (d c) -> p (t d) c", d=2)
            lb = lbs[:, 0:1, :].broadcast_to([P, 4, 512])
            one_lb = lbs[:, 1:2, :].broadcast_to([P, 4, 512])
            even_block(0)
            dve.wait_ge(lev_in, 16)
            nc.vector.tensor_copy(lev[:].rearrange("p a b c -> p (a b c)"), levraw[:, 0:2 * LEV_SLOTS * P]).then_inc(levels_ready, 1)
            nc.vector.tensor_copy(masks[:].rearrange("p l t -> p (l t)"), levraw[:, 2 * LEV_SLOTS * P:]).then_inc(levels_ready, 1)
            even_block(1)
            dve.wait_ge(lb_in, 16)
            nc.vector.tensor_tensor(lbs[:, 0, :], lbs[:, 0, :], lbs[:, 0, :], ALU.subtract).then_inc(bounds_shifted, 1)
            even_block(2)
            dve.wait_ge(bounds_exp, 1)
            link(nc.vector.reciprocal(lbs[:, 1, :], lbs[:, 0, :]))
            link(nc.vector.tensor_tensor(lbs[:, 1, :], lbs[:, 1, :], lbs[:, 0, :], ALU.mult))
            link(nc.vector.tensor_tensor(lbs[:, 0, :], lbs[:, 1, :], lbs[:, 1, :], ALU.subtract))
            link(nc.vector.tensor_scalar(lbs[:, 1, :], lbs[:, 0, :], -1.0, 1.0, ALU.mult, ALU.add))
            even_block(3)
            dve.wait_ge(sigmoids_ready, 1)
            nc.vector.tensor_tensor(sBv, sBv, one_lb, ALU.mult).then_inc(keys_ready, 1)
            dve.wait_ge(sigmoids_ready, 2)
            link(nc.vector.tensor_tensor(sAv, sAv, one_lb, ALU.mult))
            even_block(4)
            link(nc.vector.tensor_tensor(sAv, sAv, lb, ALU.add))
            nc.vector.tensor_scalar(sAv, sAv, MIN_FORGET, None, ALU.max).then_inc(forgets_ready, 1)
            for b in range(5, 8):
                even_block(b)
                if b < 7:
                    for i in ((0, 1) if b == 5 else (2,)):
                        dve.wait_ge(hgrn_qk_turned, 2 * i + 2)
                        nc.vector.tensor_copy(hT[:, i, 2:4, :].rearrange("p h s -> p (h s)"), psum[:, 5 + 2 * i % 4, :]).then_inc(hgrn_qk_dve, 1)
            for t in range(NT):
                dve.wait_ge(logs_hi, t + 1)
                nc.vector.tensor_tensor(xT_lo[:, 4 * t:4 * t + 4, :].rearrange("p k s -> p (k s)"), sA[:, t, :],
                                        xT_hi[:, 4 * t:4 * t + 4, :].rearrange("p k s -> p (k s)").bitcast(F32),
                                        ALU.subtract).then_inc(logs_lo, 1)
            split_lo(dve, Q_OUT, 0, G_SQ, js=LATE)

            def scale_pair(n):
                li, pair = unit(n)
                m = LEVELS[li]
                dve.wait_ge(decays_ready, n + 1)
                if n >= 2:
                    dve.wait_ge(unit_scores, n - 1)
                if n == 0:
                    dve.wait_ge(hgrn_qk_act, 3)
                    dve.wait_ge(hgrn_qk_dve, 3)
                if li:
                    cut = lambda v: v.rearrange("p a (b f m) -> p a b f m", f=2, m=m)
                    tiles = lambda v: cut(v.rearrange("p h (t c) -> p (h t) c", t=NT))
                    q_, kf, kb = (tiles(hT[:, i, 2 * pair:2 * pair + 2, :]) for i in range(3))
                    Ef, Eb = (cut(expE[n % 2][:, :, d, :]) for d in range(2))
                    Qn, Kn = (tiles(qk2[n % 2][:, i, :, :]) for i in range(2))
                else:
                    cut = lambda v: v.rearrange("p h (b f m) -> p h b f m", f=2, m=m)
                    q_, kf, kb = (cut(hT[:, i, 2 * pair:2 * pair + 2, :]) for i in range(3))
                    Ef, Eb = (expE[n % 2][:, :, d, :].rearrange("p (h b f) m -> p h b f m", b=1, f=2) for d in range(2))
                    Qn, Kn = (cut(qk2[n % 2][:, i, :, :]) for i in range(2))
                for out_, in_, e, f in ((Qn, q_, Ef, 1), (Qn, q_, Eb, 0), (Kn, kf, Ef, 0), (Kn, kb, Eb, 1)):
                    ins = nc.vector.tensor_tensor(out_[:, :, :, f, :], in_[:, :, :, f, :], e[:, :, :, f, :], ALU.mult)
                ins.then_inc(qk_scaled, 1)

            def keep_scores(n):
                dve.wait_ge(unit_scores, n + 1)
                dve.wait_ge(scores_kept, stands_before(n))
                src = psum[:, 4 + n % 2, :].rearrange("p (h i c) -> p h i c", h=2, i=2)
                level = unit(n)[0]
                for h in range(2):
                    ins = nc.vector.copy_predicated(kept(n)[:, h, :, :], masks[:, level - 2:level - 1, :].broadcast_to([P, 2, P]), src[:, h, :, :])
                ins.then_inc(scores_kept, 1)

            dve.wait_ge(vec_in, 16)
            for n in range(2 * NL):
                scale_pair(n)
                if n > 4:
                    keep_scores(n - 1)
            for n in range(2 * NL - 1, 2 * NL + 2):
                keep_scores(n)
            for b in (1, 3):
                dve.wait_ge(qk_turned, b + 1)
                nc.vector.tensor_copy(qkT[:, 2 * b:2 * b + 2, :].rearrange("p k s -> p (k s)"), psum[:, b, :]).then_inc(qk_out_dve, 1)
            dve.wait_ge(band_in, 16)
            for h in range(BH):
                dve.wait_ge(dil_scores, h + 1)
                if h >= 2:
                    dve.wait_ge(dil_turned, h - 1)
                link(nc.vector.scalar_tensor_tensor(zP[h % 2][:].rearrange("p t s -> p (t s)"), psum[:, h % 4, :],
                                                    BD ** -0.5, band[:].rearrange("p t s -> p (t s)"), ALU.mult, ALU.add))
                link(nc.vector.tensor_reduce(vec[:, 2 * h:2 * h + 2], zP[h % 2][:], AX_X, ALU.max))
                nc.vector.tensor_scalar(vec[:, 16 + 2 * h:18 + 2 * h], vec[:, 2 * h:2 * h + 2], -1.0, None,
                                        ALU.mult).then_inc(dil_negmax, 1)
                if h == 2:
                    sum_squares(0, sq0)
            dve.wait_ge(dil_probs, 2 * BH)
            link(nc.vector.reciprocal(vec[:, 64:80], vec[:, 48:64]))
            dve.wait_ge(dil_values, BH)
            rinv = vec[:, 64:80].rearrange("p (h t) -> p t h", t=NT)
            for t in range(NT):
                ins = nc.vector.tensor_tensor(proj[:, t, 512:1024].rearrange("p (h c) -> p h c", h=BH),
                                              psum[:, 6 + t, :].rearrange("p (h c) -> p h c", h=BH),
                                              rinv[:, t, :, None].broadcast_to([P, BH, BD]), ALU.mult)
                ins.then_inc(mix_done, 1)
            transposed_lo(1)

            def out_projection(i, q, nxt):
                split_lo(dve, q, 1, G_SQ)
                dve.wait_ge(tile_used, group_used(q, 0))
                for t in range(NT):
                    residual(0, 0, t)
                end_of_stage(i, q, 2, nxt)

            out_projection(0, Q_OUT, (Q_UP, 0, G_UP))
            transposed_lo(2)
            split_lo(dve, Q_UP, 0, G_UP, js=(1, 2, 3))

            def up_blocks(q, last=False):
                for par in range(2):
                    nxt = (Q_UP + q, 1, G_UP) if par == 0 else (Q_DN, 0, G_DN[0]) if last else (Q_UP + q + 1, 0, G_UP)
                    split_lo(dve, *nxt, js=EARLY)
                    b = 2 * q + par
                    dve.wait_ge(up_silu, b + 1)
                    nc.vector.tensor_tensor(h_nat[:, :, bass.ds(b * NU, NU)], silu[:],
                                            psum[:, 4 * par + 2:4 * par + 4, 0:NU], ALU.mult).then_inc(up_hidden, 1)
                    split_lo(dve, *nxt, js=LATE)

            def hidden_lo(g):
                dve.wait_ge(hidden_hi_ready, g + 1)
                dst = slice(2 * g, 2 * g + 2)
                nc.vector.tensor_tensor(hT_lo[:, dst, :].rearrange("p k s -> p (k s)"), psum[:, g % 4, :],
                                        hT_hi[:, dst, :].rearrange("p k s -> p (k s)").bitcast(F32),
                                        ALU.subtract).then_inc(hidden_lo_ready, 1)

            with dve.Fori(0, 3) as q:
                up_blocks(q)
            up_blocks(3, last=True)
            for g in range(6):
                hidden_lo(g)
            split_lo(dve, Q_DN, 1, G_DN[1])
            for g in range(6, 11):
                hidden_lo(g)
            split_lo(dve, Q_DN + 1, 0, G_DN[0])
            dve.wait_ge(tile_used, group_used(Q_DN, 1))
            for t in range(NT):
                residual(4, 0, t)
            split_lo(dve, Q_DN + 1, 1, G_DN[1])
            end_of_stage(1, Q_DN + 1, 6, (Q_IN2, 0, G_SQ))
            transposed_lo(3)
            split_lo(dve, Q_IN2, 0, G_SQ, js=(1, 2, 3))
            with dve.Fori(0, 2) as q:
                in_block(Q_IN2 + q, 0, proj2, q * 2 * NB, (Q_IN2 + q, 1))
                in_block(Q_IN2 + q, 1, proj2, q * 2 * NB + NB, (Q_IN2 + q + 1, 0))
            dve.wait_ge(lambda_in, 16)
            lam4 = lamv[:].rearrange("p (a b) c -> p a b c", b=2)
            link(nc.vector.tensor_tensor(lam4[:, :, 0, :], lam4[:, :, 0, :], lam4[:, :, 1, :], ALU.mult))
            nc.vector.tensor_reduce(vec[:, 88:90], lam4[:, :, 0, :], AX_X, ALU.add).then_inc(lambda_sums, 1)
            dve.wait_ge(sub_in, 16)
            link(nc.vector.tensor_scalar(sub[:], sub[:], 1.0 - LAMBDA_INIT, None, ALU.mult))
            def queries_keys(half):
                for b in (1, 3):
                    dve.wait_ge(qk_turned, 4 + 4 * half + b + 1)
                    k0 = 8 * half + 2 * b
                    nc.vector.tensor_copy(qkT2[:, k0:k0 + 2, :].rearrange("p k s -> p (k s)"), psum[:, 4 + b, :]).then_inc(qk_out_dve, 1)

            in_block(Q_IN2 + 2, 0, proj2, 4 * NB, (Q_IN2 + 2, 1))
            queries_keys(0)
            in_block(Q_IN2 + 2, 1, proj2, 5 * NB, (Q_OUT2, 0))
            queries_keys(1)
            dve.wait_ge(lambda_exps, 1)
            link(nc.vector.tensor_tensor(vec[:, 92:93], vec[:, 91:92], vec[:, 90:91], ALU.subtract))
            link(nc.vector.tensor_scalar(vec[:, 92:93], vec[:, 92:93], -LAMBDA_INIT, None, ALU.add))

            def map_max(h):
                p = h % 2
                dve.wait_ge(map_scored, h + 1)
                link(nc.vector.tensor_reduce(vec[:, 4 * p:4 * p + 4],
                                             psum[:, 2 * p:2 * p + 2, :].rearrange("p m (t s) -> p (m t) s", t=2), AX_X, ALU.max))
                nc.vector.tensor_scalar(vec[:, 16 + 4 * p:20 + 4 * p], vec[:, 4 * p:4 * p + 4], -(CD ** -0.5), None,
                                        ALU.mult).then_inc(map_negmax, 1)

            def combine(h):
                p = h % 2
                dve.wait_ge(map_probs, 4 * h + 4)
                if h >= 2:
                    dve.wait_ge(maps_turned, h - 1)
                link(nc.vector.reciprocal(vec[:, 64 + 4 * p:68 + 4 * p], vec[:, 48 + 4 * p:52 + 4 * p]))
                link(nc.vector.tensor_scalar(vec[:, 80 + 2 * p:82 + 2 * p], vec[:, 66 + 4 * p:68 + 4 * p], vec[:, 92:93], None, ALU.mult))
                for t in range(NT):
                    link(nc.vector.tensor_scalar(eP[p][:, 1, t, :], eP[p][:, 1, t, :], vec[:, 80 + 2 * p + t:81 + 2 * p + t], None, ALU.mult))
                    ins = nc.vector.scalar_tensor_tensor(aP[p][:, t, :], eP[p][:, 0, t, :], vec[:, 64 + 4 * p + t:65 + 4 * p + t],
                                                         eP[p][:, 1, t, :], ALU.mult, ALU.add)
                ins.then_inc(maps_combined, 1)

            map_max(0)
            map_max(1)
            for h in range(CH):
                combine(h)
                if h + 2 < CH:
                    map_max(h + 2)
                if h == 5:
                    sum_squares(1, sq2)
            dve.wait_ge(heads_out, 2)
            for t in range(NT):
                dve.wait_ge(squares_ready, 3 + t)
                nc.vector.tensor_reduce(vec[:, 32 + 4 * t:36 + 4 * t], sq2[:, t], AX_X, ALU.add).then_inc(square_sums, 1)
            for t in range(NT):
                dve.wait_ge(rms_ready, t + 1)
                link(nc.vector.tensor_tensor(on2[:, t], psum[:, 6 + t, :].rearrange("p (h c) -> p h c", h=4),
                                             vec[:, 40 + 4 * t:44 + 4 * t, None].broadcast_to([P, 4, 128]), ALU.mult))
                nc.vector.tensor_tensor(proj2[:, t, 512:1024].rearrange("p (h c) -> p h c", h=4), on2[:, t],
                                        sub[:, None, :].broadcast_to([P, 4, 128]), ALU.mult).then_inc(mix_done, 1)
            transposed_lo(4)
            out_projection(2, Q_OUT2, (q_moe(0), 0, G_UP))

            LG, GTR, TOP, DIF, EXS, SEL, GATE, POS = range(8)
            dve.wait_ge(tokens_turned, 24)
            nc.vector.tensor_copy(by_bank(xT_f, 3), psum[:, 7, :].rearrange("p (k s) -> p k s", s=P)).then_inc(router_x_dve, 1)
            split_lo(dve, q_moe(0), 0, G_UP, js=(1, 2, 3))
            dve.wait_ge(logits_ready, 1)
            link(nc.vector.tensor_copy(route[:, LG], psum[:, 0, 0:NT * NE].rearrange("p (t e) -> p t e", e=NE)))
            dve.wait_ge(before_in, 16)
            both = lambda i: cmp[:, i].rearrange("p t a b -> p (t a b)")
            other = route[:, LG, :, None, :].broadcast_to([P, NT, NE, NE])
            mine = route[:, LG, :, :, None].broadcast_to([P, NT, NE, NE])
            nc.vector.tensor_tensor(cmp[:, 0], other, mine, ALU.is_gt)
            link(nc.vector.tensor_tensor(cmp[:, 1], other, mine, ALU.is_equal))
            link(nc.vector.tensor_tensor(cmp[:, 1], cmp[:, 1], before[:, None, :, :].broadcast_to([P, NT, NE, NE]), ALU.mult))
            link(nc.vector.tensor_tensor(both(0), both(0), both(1), ALU.add))
            flat = lambda i: route[:, i].rearrange("p t e -> p (t e)")
            link(nc.vector.tensor_reduce(flat(GTR), cmp[:, 0].rearrange("p t a b -> p (t a) b"), AX_X, ALU.add))
            nc.vector.tensor_scalar(flat(SEL), flat(GTR), 2.0, None, ALU.is_lt).then_inc(experts_chosen, 1)
            link(nc.vector.tensor_reduce(route[:, TOP, :, 0], route[:, LG], AX_X, ALU.max))
            nc.vector.tensor_tensor(route[:, DIF], route[:, LG], route[:, TOP, :, 0:1].broadcast_to([P, NT, NE]),
                                    ALU.subtract).then_inc(logits_shifted, 1)
            dve.wait_ge(gate_exps, 1)
            dve.wait_ge(experts_chosen, 1)
            link(nc.vector.tensor_tensor(route[:, EXS], route[:, EXS], route[:, SEL], ALU.mult))
            link(nc.vector.tensor_reduce(route[:, TOP, :, 1], route[:, EXS], AX_X, ALU.add))
            link(nc.vector.reciprocal(route[:, TOP, :, 2], route[:, TOP, :, 1]))
            link(nc.vector.tensor_tensor(route[:, GATE], route[:, EXS], route[:, TOP, :, 2:3].broadcast_to([P, NT, NE]), ALU.mult))
            dve.wait_ge(positions_ready, 1)
            link(nc.vector.tensor_scalar(flat(POS), psum[:, 1, 0:NT * NE], 1.0, None, ALU.add))
            link(nc.vector.tensor_tensor(flat(POS), flat(POS), flat(SEL), ALU.mult))
            for r in range(2):
                link(nc.vector.tensor_scalar(seat[:, :, r * NE:(r + 1) * NE], route[:, POS], -1.0 - r * P, None, ALU.add))

            def pick_tokens(n, e):
                for t in range(NT):
                    nc.vector.tensor_scalar(pick[:, t, :], slots, seat[:, t, bass.ds(n, 1)], None, ALU.is_equal)
                nc.vector.tensor_copy(gate_col[:], route[:, GATE, :, bass.ds(e, 1)].rearrange("p t e -> p (t e)")).then_inc(pick_ready, 1)

            def gather_lo(n):
                for b in range(2):
                    dve.wait_ge(gathered_hi, 2 * n + b + 1)
                    dst = slice(4 * b, 4 * b + 4)
                    nc.vector.tensor_tensor(xe_lo[:, dst, :].rearrange("p k s -> p (k s)"), psum[:, 4 + b, :],
                                            xe_hi[:, dst, :].rearrange("p k s -> p (k s)").bitcast(F32),
                                            ALU.subtract).then_inc(gathered_lo, 1)

            def make_current(n):
                dve.wait_ge(map_kept, 2 * n + 2)
                nc.vector.tensor_copy(put[:], put_next[:].bitcast(F32))
                nc.vector.tensor_copy(slot_gate[:, 1:2], slot_gate[:, 0:1]).then_inc(map_current, 1)

            def turn_lo(n, g):
                k0, kc, bank, _ = TURNS[g]
                dve.wait_ge(chunks_hi, 6 * n + g + 1)
                nc.vector.tensor_tensor(hTe_lo[:, k0:k0 + kc, :].rearrange("p k s -> p (k s)"), psum[:, bank, 0:kc * P],
                                        hTe_hi[:, k0:k0 + kc, :].rearrange("p k s -> p (k s)").bitcast(F32),
                                        ALU.subtract).then_inc(chunks_lo, 1)

            def block_e(n, b):
                split_lo(dve, *up_group(n, b + 1), up_shapes(b + 1), js=EARLY)
                dve.wait_ge(silu_ready, 8 * n + b + 1)
                nc.vector.tensor_tensor(h_e[:, b * NU:(b + 1) * NU], silu_e[:, b % 2, :], psum[:, 2 * (b % 2) + 1, 0:NU],
                                        ALU.mult).then_inc(hidden_ready, 1)
                split_lo(dve, *up_group(n, b + 1), up_shapes(b + 1), js=LATE)

            def add_half(n, half):
                cols = slice(half * NB, (half + 1) * NB)
                dve.wait_ge(rows_scattered, 2 * n + half + 1)
                nc.vector.tensor_tensor(x[:, :, cols], x[:, :, cols], psum[:, 4 + 2 * half:6 + 2 * half, :],
                                        ALU.add).then_inc(rows_added, 1)

            def statistics(half):
                dve.wait_ge(rows_added, 2 * NE + half)
                for t in range(NT):
                    nc.vector.bn_stats(stat[:, t, half, :], x[:, t, half * NB:(half + 1) * NB])

            def expert(n, e, last, end=False):
                q0 = q_moe(n)
                if not last:
                    dve.wait_ge(pick_used, n + 1)
                    pick_tokens(n + 1, e + 1)
                for b in range(1, UB):
                    block_e(n, b)
                    if b in TURN_AFTER:
                        turn_lo(n, TURN_AFTER[b])
                if not last:
                    gather_lo(n + 1)
                turn_lo(n, 5)
                split_lo(dve, q0 + 4, 1, G_DN[1])
                split_lo(dve, q0 + 5, 0, G_DN[0])
                for half in range(2):
                    if half:
                        split_lo(dve, q0 + 5, 1, G_DN[1], in_late=end)
                        add_half(n, 0)
                        if end:
                            statistics(0)
                        if not last:
                            split_lo(dve, q0 + 6, 0, G_UP)
                    cols = slice(half * NB, (half + 1) * NB)
                    dve.wait_ge(y_hi_ready, 2 * n + half + 1)
                    nc.vector.scalar_tensor_tensor(y_lo[:, cols], psum[:, 2 * half, :], slot_gate[:, 1:2],
                                                   y_hi[:, cols].bitcast(F32), ALU.mult, ALU.subtract).then_inc(y_lo_ready, 1)
                if not last:
                    block_e(n + 1, 0)
                add_half(n, 1)
                if not last:
                    make_current(n + 1)

            pick_tokens(0, 0)
            link(nc.vector.tensor_reduce(route[:, TOP, 0, 3:4], psum[:, 2, 0:NE], AX_X, ALU.max))
            nc.vector.tensor_scalar(more[:], route[:, TOP, 0, 3:4], float(P), None, ALU.is_gt).then_inc(more_set, 1)
            gather_lo(0)
            make_current(0)
            nc.vector.memset(mv[:, 0, :], 0.0).then_inc(hidden_ready, 1)
            nc.vector.memset(mv[:, 1, :], 0.0).then_inc(hidden_ready, 1)
            nc.vector.memset(stat[:], 0.0).then_inc(rows_added, 1)
            dve.wait_ge(xn_set, 1)
            link(nc.vector.tensor_scalar(x[:], x[:], ALPHA, None, ALU.mult))
            block_e(0, 0)
            with dve.Fori(0, NE - 1) as n:
                expert(n, n, False)
            expert(NE - 1, NE - 1, True, end=True)
            statistics(1)
            flag = dve.value_load(more[0:1, 0:1], min_val=0, max_val=1)
            with dve.If(flag):
                with dve.Fori(0, NE) as e:
                    split_lo(dve, q_moe(e + NE), 0, G_UP)
                    dve.wait_ge(pick_used, e + NE)
                    pick_tokens(e + NE, e)
                    gather_lo(e + NE)
                    make_current(e + NE)
                    block_e(e + NE, 0)
                    expert(e + NE, e, True)
                dve.wait_ge(rows_added, 4 * NE + 1)
                for t in range(NT):
                    for half in range(2):
                        nc.vector.bn_stats(stat[:, t, half, :], x[:, t, half * NB:(half + 1) * NB])
            link(nc.vector.memset(vec[:, 0:1], 0.0))
            for t in range(NT):
                mean_var(t)
            for t in range(NT):
                normalize(3, t)

        @block.tensor
        def _(pe):
            def transpose_chunks(src, ts=range(NT), norm=None, mixed=None):
                for t in ts:
                    if mixed is not None:
                        pe.wait_ge(mix_done, mixed + t + 1)
                    if norm is not None:
                        pe.wait_ge(ln_done1 if t else ln_done0, norm + 1)
                    for kb in range(2):
                        for kk in range(4):
                            ins = nc.tensor.transpose(psum[:, 4 + 2 * t + kb, kk * P:(kk + 1) * P], src(4 * kb + kk, t), ident)
                        ins.then_inc(tokens_turned, 1)

            def last_group(q, shapes, k0s, lhs, bank, last_k):
                hi, lo = lhs
                for t in range(NT):
                    for j, (kc, n) in enumerate(shapes):
                        if t == 0:
                            pe.wait_ge(lo_done, 2 * GT * q + GT + j + 1)
                        for kk in range(kc):
                            k = k0s[j] + kk
                            w_h = whi[j][:, kk * n:(kk + 1) * n]
                            w_l = wlo[j][:, kk * n:(kk + 1) * n]
                            ps = psum[:, bank + t, :]
                            nc.tensor.matmul(ps, hi[:, k, t * P:(t + 1) * P], w_h, start=(k == 0), stop=False)
                            nc.tensor.matmul(ps, hi[:, k, t * P:(t + 1) * P], w_l, start=False, stop=False)
                            ins = nc.tensor.matmul(ps, lo[:, k, t * P:(t + 1) * P], w_h, start=False, stop=(k == last_k))
                        if t == NT - 1:
                            ins.then_inc(tile_used, 1)
                    if t == 0:
                        ins.then_inc(rows_done, 1)

            def x_chunk(k, t):
                return x[:, t, k * P:(k + 1) * P]

            def square_block(q, par, bank, turned=None):
                for j in range(GT):
                    if turned is not None and 2 * j in (0, 4):
                        pe.wait_ge(tokens_lo, turned - 1 + j // 2)
                    tile_products(pe, q, par, j, 2, NB, 2 * j, (xT_hi, xT_lo),
                                  [(psum[:, bank + t, :], t * P) for t in range(NT)], 0, KD - 1)

            pe.wait_ge(x_in, 16)
            pe.wait_ge(const_in, 16)
            transpose_chunks(x_chunk)
            square_block(Q_IN, 0, 0, turned=4)
            square_block(Q_IN, 1, 2)
            def queries_keys_hgrn(i):
                for hp in range(2):
                    if i == 2:
                        pe.wait_ge(hgrn_qk_dve if hp else hgrn_qk_act, 1)
                    for hh in range(2):
                        for t in range(NT):
                            h = 2 * hp + hh
                            src = proj[:, t, h * AD:(h + 1) * AD] if i == 0 else sB[:, t, (i - 1) * 512 + h * AD:(i - 1) * 512 + (h + 1) * AD]
                            ins = nc.tensor.transpose(psum[:, 4 + 2 * i % 4 + hp, hh * S + t * P:hh * S + t * P + P], src, ident)
                    ins.then_inc(hgrn_qk_turned, 1)

            for b in range(2, 8):
                pe.wait_ge(block_out_act, b - 1)
                pe.wait_ge(block_out_dve, b - 1)
                square_block(Q_IN + b // 2, b % 2, 2 * (b % 2))
                if b == 5:
                    pe.wait_ge(keys_ready, 1)
                    queries_keys_hgrn(0)
                    queries_keys_hgrn(1)
                if b == 6:
                    queries_keys_hgrn(2)

            pe.wait_ge(block_out_act, 8)
            pe.wait_ge(block_out_dve, 8)
            lf_hi = xT_hi[:].rearrange("p k s -> p (k s)").rearrange("p (t d c) -> p t d c", t=2, d=2)
            lf_lo = xT_lo[:].rearrange("p k s -> p (k s)").rearrange("p (t d c) -> p t d c", t=2, d=2)

            def exponents(u):
                lp, pair = u // 2, u % 2
                if u == 0:
                    pe.wait_ge(levels_ready, 1)
                else:
                    pe.wait_ge(decays_ready, 2 * u)
                for t in range(NT):
                    if u == 0:
                        pe.wait_ge(logs_lo, t + 1)
                    for hh in range(2):
                        h = 2 * pair + hh
                        for d in range(2):
                            dst = psum[:, 2 * hh + t, d * S:(d + 1) * S]
                            slot = 2 * t if lp == 0 else 2 + 2 * lp
                            m = lev[:, d, slot:slot + 2, :].rearrange("p l c -> p (l c)")
                            nc.tensor.matmul(dst, lf_hi[:, t, d, h * AD:(h + 1) * AD], m, start=True, stop=False)
                            ins = nc.tensor.matmul(dst, lf_lo[:, t, d, h * AD:(h + 1) * AD], m, start=False, stop=True)
                ins.then_inc(exponents_ready, 1)

            def scores(n):
                li, pair = unit(n)
                if n == 0:
                    pe.wait_ge(hgrn_qk_act, 3)
                    pe.wait_ge(hgrn_qk_dve, 3)
                if n >= 2:
                    pe.wait_ge(scores_kept, n - 1)
                if n < 2 * NL:
                    pe.wait_ge(qk_scaled, n + 1)
                for hh in range(2):
                    h = 2 * pair + hh
                    for i in range(2):
                        dst = psum[:, 4 + n % 2, hh * S + i * P:hh * S + i * P + P]
                        ts, tt = (i, 1 - i) if li == 0 else (i, i)
                        if n < 2 * NL:
                            q_, k_ = (qk2[n % 2][:, w, hh, :] for w in range(2))
                            ins = nc.tensor.matmul(dst, k_[:, ts * P:(ts + 1) * P], q_[:, tt * P:(tt + 1) * P], start=True, stop=True)
                        else:
                            q_ = hT[:, 0, h, tt * P:(tt + 1) * P]
                            nc.tensor.matmul(dst, hT[:, 1, h, ts * P:(ts + 1) * P], q_, start=True, stop=False)
                            ins = nc.tensor.matmul(dst, hT[:, 2, h, ts * P:(ts + 1) * P], q_, start=False, stop=True)
                ins.then_inc(unit_scores, 1)

            exponents(0)
            for n in range(2 * NL + 2):
                if n % 2 == 0 and n + 2 < 2 * NL:
                    exponents(n // 2 + 1)
                scores(n)
            pe.wait_ge(rope_done, 8)
            pe.wait_ge(decays_ready, 2 * NL)
            for b in range(4):
                for kk in range(2):
                    for t in range(NT):
                        col = QB + (2 * b + kk) * P
                        ins = nc.tensor.transpose(psum[:, b, kk * S + t * P:kk * S + t * P + P], proj[:, t, col:col + P], ident)
                ins.then_inc(qk_turned, 1)

            pe.wait_ge(scores_kept, 2 * NL + 2)
            for t in range(NT):
                for h in range(AH):
                    dst = psum[:, 6 + t, h * AD:(h + 1) * AD]
                    v = [proj[:, tt, VA + h * AD:VA + (h + 1) * AD] for tt in range(NT)]
                    nc.tensor.matmul(dst, ATd[:, t, h, :], v[t], start=True, stop=False)
                    ins = nc.tensor.matmul(dst, ATo[:, h, 1 - t, :], v[1 - t], start=False, stop=True)
            ins.then_inc(hgrn_summed, 1)

            def b_scores(h):
                if h == 0:
                    pe.wait_ge(qk_out_act, 2)
                    pe.wait_ge(qk_out_dve, 2)
                if h >= 4:
                    pe.wait_ge(dil_negmax, h - 3)
                rows = slice(BD * (h % 2), BD * (h % 2) + BD)
                for t in range(NT):
                    ins = nc.tensor.matmul(psum[:, h % 4, t * S:(t + 1) * S], qkT[rows, h // 2, t * P:(t + 1) * P],
                                           qkT[rows, 4 + h // 2, :], start=True, stop=True)
                ins.then_inc(dil_scores, 1)

            def turn(src, h, done):
                for sc in range(NT):
                    for t in range(NT):
                        ins = nc.tensor.transpose(psum[:, 4 + h % 2, sc * S + t * P:sc * S + t * P + P],
                                                  src[:, t, sc * P:(sc + 1) * P], ident)
                ins.then_inc(done, 1)

            def b_turn(h):
                pe.wait_ge(dil_probs, 2 * h + 2)
                if h >= 2:
                    pe.wait_ge(dil_moved, h - 1)
                turn(zP[h % 2], h, dil_turned)

            def b_values(h):
                pe.wait_ge(dil_moved, h + 1)
                if h == 0:
                    pe.wait_ge(on_kept, 1)
                for t in range(NT):
                    for sc in range(NT):
                        ins = nc.tensor.matmul(psum[:, 6 + t, h * BD:(h + 1) * BD], pT[h % 2][:, sc, t * P:(t + 1) * P],
                                               proj[:, sc, VB + h * BD:VB + (h + 1) * BD], start=(sc == 0), stop=(sc == NT - 1))
                ins.then_inc(dil_values, 1)

            for h in range(3):
                b_scores(h)
            for h in range(BH):
                if h + 3 < BH:
                    b_scores(h + 3)
                b_turn(h)
                if h:
                    b_values(h - 1)
            b_values(BH - 1)
            pe.wait_ge(heads_out, 1)
            transpose_chunks(lambda k, t: proj[:, t, k * P:(k + 1) * P], mixed=0)
            square_block(Q_OUT, 0, 0, turned=8)
            last_group(Q_OUT, G_SQ, [2 * j for j in range(GT)], (xT_hi, xT_lo), 2, KD - 1)

            transpose_chunks(x_chunk, norm=0)
            def up_block(q, par, wait):
                if wait:
                    pe.wait_ge(up_hidden, 2 * q + par - 1)
                for j in range(GT):
                    if not wait and par == 0 and j < 2:
                        pe.wait_ge(tokens_lo, 11 + j)
                    tile_products(pe, Q_UP + q, par, j, 4, NU, 4 * (j % 2), (xT_hi, xT_lo),
                                  [(psum[:, 4 * par + 2 * (j // 2) + t, 0:NU], t * P) for t in range(NT)], 0, KD - 1)

            for par in range(2):
                up_block(0, par, False)
            with pe.Fori(1, 4) as q:
                for par in range(2):
                    up_block(q, par, True)
            pe.wait_ge(up_hidden, 8)

            n_turned = [0]

            def turn_hidden(upto):
                while n_turned[0] < min(upto, KF // 2):
                    g = n_turned[0]
                    n_turned[0] += 1
                    if g >= 4:
                        pe.wait_ge(hidden_lo_ready, g - 3)
                    for kk in range(2):
                        for t in range(NT):
                            k = 2 * g + kk
                            ins = nc.tensor.transpose(psum[:, g % 4, kk * S + t * P:kk * S + t * P + P],
                                                      h_nat[:, t, k * P:(k + 1) * P], ident)
                    ins.then_inc(hidden_turned, 1)

            for half in range(2):
                for part in range(2):
                    if half and part:
                        last_group(Q_DN + 1, G_DN[1], DN_K0[1], (hT_hi, hT_lo), 6, KF - 1)
                        continue
                    for j, (kc, n) in enumerate(G_DN[part]):
                        k0 = DN_K0[part][j]
                        if half == 0:
                            need = (k0 + kc + 1) // 2
                            turn_hidden(need + 3)
                            pe.wait_ge(hidden_lo_ready, need)
                        tile_products(pe, Q_DN + half, part, j, kc, n, k0, (hT_hi, hT_lo),
                                      [(psum[:, 4 + 2 * half + t, :], t * P) for t in range(NT)], 0, KF - 1)

            transpose_chunks(x_chunk, norm=1)
            square_block(Q_IN2, 0, 0, turned=16)
            square_block(Q_IN2, 1, 2)
            def queries_keys(half):
                for b in range(4):
                    if half:
                        pe.wait_ge(qk_out_dve if b % 2 else qk_out_act, 3 + b // 2)
                    for kk in range(2):
                        for t in range(NT):
                            col = half * D + (2 * b + kk) * P
                            ins = nc.tensor.transpose(psum[:, 4 + b, kk * S + t * P:kk * S + t * P + P], proj2[:, t, col:col + P], ident)
                    ins.then_inc(qk_turned, 1)

            for b in range(2, 6):
                pe.wait_ge(block_out_act, 8 + b - 1)
                pe.wait_ge(block_out_dve, 8 + b - 1)
                square_block(Q_IN2 + b // 2, b % 2, 2 * (b % 2))
                if b == 4:
                    pe.wait_ge(rope2_pool, 4)
                    queries_keys(0)
            pe.wait_ge(rope2_pool, 8)
            queries_keys(1)
            pe.wait_ge(block_out_act, 14)
            pe.wait_ge(block_out_dve, 14)

            def map_scores(h):
                if h >= 2:
                    pe.wait_ge(map_probs, 4 * (h - 1))
                if h % 2 == 0:
                    pe.wait_ge(qk_out_dve if h % 4 else qk_out_act, 5 + h // 4)
                for t in range(NT):
                    for m in range(2):
                        rows = slice(CD * m, CD * m + CD)
                        ins = nc.tensor.matmul(psum[:, 2 * (h % 2) + m, t * S:(t + 1) * S], qkT2[rows, h, t * P:(t + 1) * P],
                                               qkT2[rows, 8 + h, :], start=True, stop=True)
                ins.then_inc(map_scored, 1)

            def map_turn(h):
                pe.wait_ge(maps_combined, h + 1)
                if h >= 2:
                    pe.wait_ge(maps_moved, h - 1)
                turn(aP[h % 2], h, maps_turned)

            def map_values(h):
                pe.wait_ge(maps_moved, h + 1)
                if h == 4:
                    pe.wait_ge(on_kept, 2)
                for t in range(NT):
                    for sc in range(NT):
                        ins = nc.tensor.matmul(psum[:, 6 + t, (h % 4) * 128:(h % 4 + 1) * 128], aT[h % 2][:, sc, t * P:(t + 1) * P],
                                               proj2[:, sc, 2 * D + h * 128:2 * D + (h + 1) * 128], start=(sc == 0), stop=(sc == NT - 1))
                ins.then_inc(maps_summed, 1)

            map_scores(0)
            map_scores(1)
            for h in range(CH):
                if h + 2 < CH:
                    map_scores(h + 2)
                map_turn(h)
                if h:
                    map_values(h - 1)
            map_values(CH - 1)
            pe.wait_ge(heads_out, 2)
            transpose_chunks(lambda k, t: proj2[:, t, k * P:(k + 1) * P], mixed=2)
            square_block(Q_OUT2, 0, 0, turned=20)
            last_group(Q_OUT2, G_SQ, [2 * j for j in range(GT)], (xT_hi, xT_lo), 2, KD - 1)

            pe.wait_ge(router_in, 16)
            for t in range(NT):
                transpose_chunks(x_chunk, ts=(t,), norm=2)
                pe.wait_ge(router_x_act, 2 + t)
                if t:
                    pe.wait_ge(router_x_dve, 1)
                for k in range(KD):
                    ins = nc.tensor.matmul(psum[:, 0, t * NE:(t + 1) * NE], xT_f[:, k, t * P:(t + 1) * P], router[:, k, :],
                                           start=(k == 0), stop=(k == KD - 1))
            ins.then_inc(logits_ready, 1)
            SEL = 5
            pe.wait_ge(experts_chosen, 1)
            pe.wait_ge(ones_set, 1)
            nc.tensor.matmul(psum[:, 1, 0:NE], earlier, route[:, SEL, 0, :], start=True, stop=True)
            nc.tensor.matmul(psum[:, 1, NE:2 * NE], ones[:], route[:, SEL, 0, :], start=True, stop=False)
            nc.tensor.matmul(psum[:, 1, NE:2 * NE], earlier, route[:, SEL, 1, :], start=False, stop=True)
            for t in range(NT):
                ins = nc.tensor.matmul(psum[:, 2, 0:NE], ones[:], route[:, SEL, t, :], start=(t == 0), stop=(t == NT - 1))
            ins.then_inc(positions_ready, 1)

            def gather(n):
                pe.wait_ge(pick_ready, n + 1)
                for k in range(KD):
                    for t in range(NT):
                        ins = nc.tensor.matmul(psum[:, 4 + k // 4, (k % 4) * P:(k % 4 + 1) * P],
                                               xn[:, t, k * P:(k + 1) * P], pick[:, t, :], start=(t == 0), stop=(t == NT - 1))
                    if k % 4 == 3:
                        ins.then_inc(gathered, 1)
                for t in range(NT):
                    ins = nc.tensor.transpose(psum[:, 6, 2 * P + t * P:3 * P + t * P], pick[:, t, :], ident)
                for t in range(NT):
                    ins = nc.tensor.matmul(psum[:, 6, 0:1], pick[:, t, :], gate_col[:, t:t + 1],
                                           start=(t == 0), stop=(t == NT - 1))
                ins.then_inc(pick_used, 1)

            def turn_hidden_e(n, g):
                k0, kc, bank, _ = TURNS[g]
                for k in range(kc):
                    ins = nc.tensor.transpose(psum[:, bank, k * P:(k + 1) * P], h_e[:, (k0 + k) * P:(k0 + k + 1) * P], ident)
                ins.then_inc(chunks_turned, 1)

            def scatter(n, half):
                pe.wait_ge(y_lo_ready, 2 * n + half + 1)
                pe.wait_ge(map_current, n + 1)
                for t in range(NT):
                    dst = psum[:, 4 + 2 * half + t, :]
                    cols = slice(half * NB, (half + 1) * NB)
                    nc.tensor.matmul(dst, put[:, t * P:(t + 1) * P], y_hi[:, cols], start=True, stop=False)
                    ins = nc.tensor.matmul(dst, put[:, t * P:(t + 1) * P], y_lo[:, cols], start=False, stop=True)
                ins.then_inc(rows_scattered, 1)

            def block_e(n, b):
                pe.wait_ge(hidden_ready, 8 * n + b + 1)
                for j in range(GT):
                    tile_products(pe, *up_group(n, b), j, 4, NU, 4 * (j % 2), (xe_hi, xe_lo),
                                  [(psum[:, 2 * (b % 2) + j // 2, 0:NU], 0)], 0, KD - 1)

            def first_block(n):
                pe.wait_ge(gathered_hi, 2 * n + 2)
                pe.wait_ge(gathered_lo, 2 * n + 2)
                block_e(n, 0)

            def expert(n, last):
                q0 = q_moe(n)
                for b in range(1, UB):
                    block_e(n, b)
                    if b == GATHER_AFTER:
                        pe.wait_ge(rows_added, 2 * n + 1)
                        if not last:
                            gather(n + 1)
                    if b in TURN_AFTER:
                        g = TURN_AFTER[b]
                        pe.wait_ge(hidden_ready, 8 * n + b + 2)
                        if g == 0 and not last:
                            pe.wait_ge(map_kept, 2 * n + 4)
                        if g >= 2:
                            pe.wait_ge(chunks_lo, 6 * n + g - 1)
                        turn_hidden_e(n, g)
                for half in range(2):
                    for part in range(2):
                        if half and part:
                            if not last:
                                pe.wait_ge(gathered_lo, 2 * n + 4)
                            scatter(n, 0)
                        for j, (kc, w) in enumerate(G_DN[part]):
                            k0 = DN_K0[part][j]
                            if not half:
                                done = [g for g, (c0, _, _, _) in enumerate(TURNS) if c0 < k0 + kc]
                                pe.wait_ge(chunks_lo, 6 * n + len(done))
                            tile_products(pe, q0 + 4 + half, part, j, kc, w, k0, (hTe_hi, hTe_lo),
                                          [(psum[:, 2 * half, :], 0)], 0, KF - 1)
                            if not half and not part and j == 0:
                                pe.wait_ge(hidden_ready, 8 * n + 10)
                                turn_hidden_e(n, 5)
                if not last:
                    first_block(n + 1)
                scatter(n, 1)

            pe.wait_ge(xn_set, 1)
            gather(0)
            pe.wait_ge(more_set, 1)
            first_block(0)
            with pe.Fori(0, NE - 1) as n:
                expert(n, False)
            expert(NE - 1, True)
            flag = pe.value_load(more[0:1, 0:1], min_val=0, max_val=1)
            with pe.If(flag):
                with pe.Fori(NE, 2 * NE) as n:
                    pe.wait_ge(rows_added, 2 * n + 1)
                    gather(n)
                    first_block(n)
                    expert(n, True)


_INPUTS = ["x", "ev_w_in", "ev_lb_logits", "ev_hgrn_norm", "ev_w_out", "ev_ln1_g", "ev_ln1_b", "ev_w1", "ev_w3", "ev_w2",
           "ev_ln2_g", "ev_ln2_b", "od_w_in", "od_lambda", "od_subln", "od_w_out", "od_ln1_g", "od_ln1_b", "od_router",
           "od_w1", "od_w3", "od_w2", "od_ln2_g", "od_ln2_b"]


def kernel(**inputs):
    import concourse.bacc as bacc
    from concourse.bass_utils import run_bass_kernel_spmd as run

    nc = bacc.Bacc("TRN2", target_bir_lowering=False, num_devices=1)
    arrays, ins, consts = {}, {}, {}
    for name in _INPUTS:
        v = np.ascontiguousarray(inputs[name])
        arrays[f"in_{name}"] = v
        ins[name] = nc.dram_tensor(f"in_{name}", v.shape, mybir.dt.from_np(v.dtype), kind="ExternalInput").ap()
    for name, v in constants().items():
        arrays[f"const_{name}"] = v
        consts[name] = nc.dram_tensor(f"const_{name}", v.shape, mybir.dt.from_np(v.dtype), kind="ExternalInput").ap()
    out = nc.dram_tensor("out", (1, S, D), F32, kind="ExternalOutput").ap()
    trunk(nc, ins, consts, out)
    return run(nc, [arrays], core_ids=[0]).results[0]["out"]
```
